# Optimizing a Trainium2 kernel written in Bass

```python
import math
import jax, jax.numpy as jnp
from jax import lax
import numpy as np
import jax
import jax.numpy as jnp

D_MODEL = 1024
BATCH = 1
SEQ = 256
DEPTH = 1

HEAD_DIM_A = 64
N_HEADS_A = 8
WIDTH_A = N_HEADS_A * HEAD_DIM_A
DILATED_BRANCHES = ((128, 1), (512, 4), (2048, 16))

N_HEADS_B = 8
QK_NOPE_DIM = 64
QK_ROPE_DIM = 32
V_HEAD_DIM = 64
QK_HEAD_DIM_B = QK_NOPE_DIM + QK_ROPE_DIM
Q_LORA_RANK = 768
KV_LORA_RANK = 256
WIDTH_B = N_HEADS_B * V_HEAD_DIM
ROPE_THETA = 10000.0

MIX_WIDTH = WIDTH_A + WIDTH_B
D_FF = 4 * D_MODEL

REL_BUCKETS = 32
REL_MAX_DIST = 2048
Q_BLOCK = 128
EPS = 1e-6

IN_SPLITS = (WIDTH_A, WIDTH_A, WIDTH_A, Q_LORA_RANK, KV_LORA_RANK, QK_ROPE_DIM)
IN_WIDTH = sum(IN_SPLITS)


def rms_norm(x, g):
    xf = x.astype(jnp.float32)
    y = xf * lax.rsqrt(jnp.mean(xf * xf, axis=-1, keepdims=True) + EPS)
    return (y * g.astype(jnp.float32)).astype(x.dtype)

def t5_causal_bucket(dist):
    dist = np.asarray(dist, dtype=np.int64)
    max_exact = REL_BUCKETS // 2
    safe = np.maximum(dist, 1).astype(np.float32)
    large = max_exact + (np.log(safe / max_exact) / math.log(REL_MAX_DIST / max_exact)
                         * (REL_BUCKETS - max_exact)).astype(np.int64)
    large = np.minimum(large, REL_BUCKETS - 1)
    return np.where(dist < max_exact, dist, large).astype(np.int32)

def apply_rope(x, positions):
    r = x.shape[-1]
    inv_freq = 1.0 / (ROPE_THETA ** (jnp.arange(0, r, 2, dtype=jnp.float32) / r))
    ang = positions.astype(jnp.float32)[..., None] * inv_freq
    cos = jnp.cos(ang)[:, :, None, :]
    sin = jnp.sin(ang)[:, :, None, :]
    xf = x.astype(jnp.float32)
    x1, x2 = xf[..., : r // 2], xf[..., r // 2:]
    out = jnp.concatenate([x1 * cos - x2 * sin, x2 * cos + x1 * sin], axis=-1)
    return out.astype(x.dtype)

def to_query_blocks(t):
    b, s = t.shape[:2]
    nblk = s // Q_BLOCK
    return jnp.moveaxis(t.reshape((b, nblk, Q_BLOCK) + t.shape[2:]), 1, 0)

def from_query_blocks(t):
    t = jnp.moveaxis(t, 0, 1)
    return t.reshape((t.shape[0], t.shape[1] * t.shape[2]) + t.shape[3:])

def dilated_attention(q, k, v, rel_bias):
    b, s, h, dh = q.shape
    scale = 1.0 / math.sqrt(dh)
    branches = []
    for window, dil in DILATED_BRANCHES:
        offs_np = dil * np.arange(window // dil + 1, dtype=np.int32)
        bias = rel_bias[jnp.asarray(t5_causal_bucket(offs_np))].T.astype(jnp.float32)
        branches.append((jnp.asarray(offs_np), bias))
    nblk = s // Q_BLOCK

    def block_fn(args):
        i, qi = args
        tq = i * Q_BLOCK + jnp.arange(Q_BLOCK, dtype=jnp.int32)
        ms, ss, os_ = [], [], []
        for offs, bias in branches:
            idx = tq[:, None] - offs[None, :]
            valid = idx >= 0
            idxc = jnp.maximum(idx, 0)
            kg = k[:, idxc]
            vg = v[:, idxc]
            logits = jnp.einsum('bqhd,bqkhd->bhqk', qi, kg).astype(jnp.float32) * scale
            logits = logits + bias[None, :, None, :]
            logits = jnp.where(valid[None, None], logits, -jnp.inf)
            m = jnp.max(logits, axis=-1, keepdims=True)
            p = jnp.exp(logits - m)
            den = jnp.sum(p, axis=-1, keepdims=True)
            o = jnp.einsum('bhqk,bqkhd->bhqd', p, vg.astype(jnp.float32)) / den
            ms.append(m); ss.append(den); os_.append(o)
        m_all = jnp.stack(ms)
        w = jnp.stack(ss) * jnp.exp(m_all - jnp.max(m_all, axis=0, keepdims=True))
        out = jnp.sum(w * jnp.stack(os_), axis=0) / jnp.sum(w, axis=0)
        return jnp.transpose(out, (0, 2, 1, 3)).astype(q.dtype)

    out = lax.map(block_fn, (jnp.arange(nblk, dtype=jnp.int32), to_query_blocks(q)))
    return from_query_blocks(out)

def causal_block_attention(q, k, v):
    b, s, h, dqk = q.shape
    scale = 1.0 / math.sqrt(dqk)
    kpos = jnp.arange(s, dtype=jnp.int32)
    nblk = s // Q_BLOCK

    def block_fn(args):
        i, qi = args
        tq = i * Q_BLOCK + jnp.arange(Q_BLOCK, dtype=jnp.int32)
        logits = jnp.einsum('bqhd,bkhd->bhqk', qi, k).astype(jnp.float32) * scale
        logits = jnp.where((kpos[None, :] <= tq[:, None])[None, None], logits, -jnp.inf)
        p = jax.nn.softmax(logits, axis=-1)
        out = jnp.einsum('bhqk,bkhd->bqhd', p, v.astype(jnp.float32))
        return out.astype(q.dtype)

    out = lax.map(block_fn, (jnp.arange(nblk, dtype=jnp.int32), to_query_blocks(q)))
    return from_query_blocks(out)

def first_inputs(seed: int = 0) -> dict:
    key = jax.random.key(seed)
    ks = jax.random.split(key, 20)
    f32 = jnp.float32

    def nrm(k, shape, fan_in):
        return jax.random.normal(k, shape, f32) * (fan_in ** -0.5)

    def gain(k, n):
        return 1.0 + 0.05 * jax.random.normal(k, (n,), f32)

    x = jax.random.normal(ks[0], (BATCH, SEQ, D_MODEL), f32)
    offset = jax.random.randint(ks[1], (BATCH, 1), 0, 1024, dtype=jnp.int32)
    positions = jnp.arange(SEQ, dtype=jnp.int32)[None, :] + offset
    return {
        "x": x,
        "positions": positions,
        "norm_mix_g": gain(ks[2], D_MODEL),
        "w_in": nrm(ks[3], (D_MODEL, IN_WIDTH), D_MODEL),
        "qnorm_a_g": gain(ks[4], HEAD_DIM_A),
        "knorm_a_g": gain(ks[5], HEAD_DIM_A),
        "rel_bias": 0.5 * jax.random.normal(ks[6], (REL_BUCKETS, N_HEADS_A), f32),
        "cq_norm_g": gain(ks[7], Q_LORA_RANK),
        "ckv_norm_g": gain(ks[8], KV_LORA_RANK),
        "w_uq": nrm(ks[9], (Q_LORA_RANK, N_HEADS_B * QK_HEAD_DIM_B), Q_LORA_RANK),
        "w_ukv": nrm(ks[10], (KV_LORA_RANK, N_HEADS_B * (QK_NOPE_DIM + V_HEAD_DIM)), KV_LORA_RANK),
        "qnorm_b_g": gain(ks[11], QK_HEAD_DIM_B),
        "knorm_b_g": gain(ks[12], QK_HEAD_DIM_B),
        "w_o": nrm(ks[13], (MIX_WIDTH, D_MODEL), MIX_WIDTH),
        "norm_ffn_g": gain(ks[14], D_MODEL),
        "w_ff1": nrm(ks[15], (D_MODEL, D_FF), D_MODEL),
        "w_ff2": nrm(ks[16], (D_FF, D_MODEL), D_FF),
    }

def first_block(x, positions, norm_mix_g, w_in, qnorm_a_g, knorm_a_g, rel_bias,
              cq_norm_g, ckv_norm_g, w_uq, w_ukv, qnorm_b_g, knorm_b_g, w_o,
              norm_ffn_g, w_ff1, w_ff2):
    b, s, _ = x.shape
    h = x
    for _layer in range(DEPTH):
        xn = rms_norm(h, norm_mix_g)
        proj = jnp.einsum('bsd,de->bse', xn, w_in)
        cuts = list(np.cumsum(IN_SPLITS)[:-1])
        qa, ka, va, c_q, c_kv, k_rope = jnp.split(proj, cuts, axis=-1)

        qa = rms_norm(qa.reshape(b, s, N_HEADS_A, HEAD_DIM_A), qnorm_a_g)
        ka = rms_norm(ka.reshape(b, s, N_HEADS_A, HEAD_DIM_A), knorm_a_g)
        va = va.reshape(b, s, N_HEADS_A, HEAD_DIM_A)
        out_a = dilated_attention(qa, ka, va, rel_bias).reshape(b, s, WIDTH_A)

        qb = jnp.einsum('bsr,re->bse', rms_norm(c_q, cq_norm_g), w_uq)
        qb = qb.reshape(b, s, N_HEADS_B, QK_HEAD_DIM_B)
        kv = jnp.einsum('bsr,re->bse', rms_norm(c_kv, ckv_norm_g), w_ukv)
        kv = kv.reshape(b, s, N_HEADS_B, QK_NOPE_DIM + V_HEAD_DIM)
        k_nope, vb = kv[..., :QK_NOPE_DIM], kv[..., QK_NOPE_DIM:]
        k_rope_h = jnp.broadcast_to(k_rope[:, :, None, :], (b, s, N_HEADS_B, QK_ROPE_DIM))
        kb = jnp.concatenate([k_nope, k_rope_h], axis=-1)
        qb = rms_norm(qb, qnorm_b_g)
        kb = rms_norm(kb, knorm_b_g)
        qb = jnp.concatenate([qb[..., :QK_NOPE_DIM],
                              apply_rope(qb[..., QK_NOPE_DIM:], positions)], axis=-1)
        kb = jnp.concatenate([kb[..., :QK_NOPE_DIM],
                              apply_rope(kb[..., QK_NOPE_DIM:], positions)], axis=-1)
        out_b = causal_block_attention(qb, kb, vb).reshape(b, s, WIDTH_B)

        mixed = jnp.concatenate([out_a, out_b], axis=-1)
        h = h + jnp.einsum('bse,ed->bsd', mixed, w_o)

        hn = rms_norm(h, norm_ffn_g)
        hid = jnp.square(jax.nn.relu(jnp.einsum('bsd,df->bsf', hn, w_ff1)))
        h = h + jnp.einsum('bsf,fd->bsd', hid, w_ff2)
    return h


DEPTH_2 = 2

PLE_DIM = 256
N_HEADS = 16
HEAD_DIM = 64
ATT_DIM = N_HEADS * HEAD_DIM
NSA_KV_HEADS = 4
NSA_KV_DIM = NSA_KV_HEADS * HEAD_DIM
CMP_BLOCK = 32
CMP_STRIDE = 16
CMP_HIDDEN = 256
SEL_BLOCK = 64
SEL_TOPN = 16
WINDOW = 512
NSA_Q_BLOCK = 64
NSA_PROJ = ATT_DIM + 6 * NSA_KV_DIM + 3 * N_HEADS
MOBA_KV_HEADS = 4
MOBA_KV_DIM = MOBA_KV_HEADS * HEAD_DIM
MOBA_BLOCK = 256
MOBA_TOPK = 3
MOBA_Q_BLOCK = 16
N_GROUPS = 4
EXPERTS_PER_GROUP = 8
N_EXPERTS = N_GROUPS * EXPERTS_PER_GROUP
TOPK_IN_GROUP = 2
D_EXPERT = 128
NORM_EPS = 1e-6
FORCED_SCORE = 1e9


def rms_norm_2(x, g):
    xf = x.astype(jnp.float32)
    y = xf * lax.rsqrt(jnp.mean(xf * xf, axis=-1, keepdims=True) + NORM_EPS)
    return (y * g.astype(jnp.float32)).astype(x.dtype)

def to_heads(t, n_heads):
    b, s = t.shape[0], t.shape[1]
    return t.reshape(b, s, n_heads, HEAD_DIM).transpose(0, 2, 1, 3)

def alibi_slopes(n_heads):
    return jnp.asarray(2.0 ** (-8.0 * np.arange(1, n_heads + 1) / n_heads), dtype=jnp.float32)

def masked_softmax(s, mask, axis=-1):
    s = jnp.where(mask, s, -jnp.inf)
    m = jnp.max(s, axis=axis, keepdims=True)
    m = jnp.where(jnp.isfinite(m), m, 0.0)
    e = jnp.exp(s - m)
    return e / jnp.maximum(jnp.sum(e, axis=axis, keepdims=True), 1e-30)

def compress_blocks(k, pos, w1, w2):
    b, g, s, d = k.shape
    n_cmp = (s - CMP_BLOCK) // CMP_STRIDE + 1
    idx = np.arange(n_cmp)[:, None] * CMP_STRIDE + np.arange(CMP_BLOCK)[None, :]
    blk = (k[:, :, idx] + pos).reshape(b, g, n_cmp, CMP_BLOCK * d)
    return jax.nn.gelu(blk @ w1) @ w2

def cmp_sel_overlap(n_cmp, n_sel):
    c0 = np.arange(n_cmp)[:, None] * CMP_STRIDE
    s0 = np.arange(n_sel)[None, :] * SEL_BLOCK
    ov = np.clip(np.minimum(c0 + CMP_BLOCK, s0 + SEL_BLOCK) - np.maximum(c0, s0), 0, None)
    return jnp.asarray(ov / CMP_BLOCK, dtype=jnp.float32)

def nsa_attention(xn, w_in, q_gain, k_gain, ck_pos, ck_w1, ck_w2, cv_pos, cv_w1, cv_w2, w_out):
    b, s, _ = xn.shape
    g, r = NSA_KV_HEADS, N_HEADS // NSA_KV_HEADS
    splits = np.cumsum([ATT_DIM] + [NSA_KV_DIM] * 6).tolist()
    q, kc, vc, ks, vs, kw, vw, gl = jnp.split(xn @ w_in, splits, axis=-1)
    q = (rms_norm_2(to_heads(q, N_HEADS), q_gain) * HEAD_DIM ** -0.5).reshape(b, g, r, s, HEAD_DIM)
    kc = rms_norm_2(compress_blocks(to_heads(kc, g), ck_pos, ck_w1, ck_w2), k_gain[0])
    vc = compress_blocks(to_heads(vc, g), cv_pos, cv_w1, cv_w2)
    n_cmp = kc.shape[2]
    n_sel = s // SEL_BLOCK
    n_top = min(SEL_TOPN, n_sel)
    ks = rms_norm_2(to_heads(ks, g), k_gain[1]).reshape(b, g, n_sel, SEL_BLOCK, HEAD_DIM)
    vs = to_heads(vs, g).reshape(b, g, n_sel, SEL_BLOCK, HEAD_DIM)
    pad = ((0, 0), (0, 0), (WINDOW, 0), (0, 0))
    kw = jnp.pad(rms_norm_2(to_heads(kw, g), k_gain[2]), pad)
    vw = jnp.pad(to_heads(vw, g), pad)
    gates = jax.nn.sigmoid(gl).reshape(b, s, N_HEADS, 3).transpose(0, 2, 1, 3).reshape(b, g, r, s, 3)
    slopes = alibi_slopes(N_HEADS).reshape(1, g, r, 1, 1)
    cmp_end = jnp.arange(n_cmp) * CMP_STRIDE + (CMP_BLOCK - 1)
    overlap = cmp_sel_overlap(n_cmp, n_sel)
    blk_ids = jnp.arange(n_sel)
    bi = jnp.arange(b)[:, None, None, None]
    gi = jnp.arange(g)[None, :, None, None]

    def query_block(c):
        start = c * NSA_Q_BLOCK
        t = start + jnp.arange(NSA_Q_BLOCK)
        qc = lax.dynamic_slice_in_dim(q, start, NSA_Q_BLOCK, axis=3)
        gc = lax.dynamic_slice_in_dim(gates, start, NSA_Q_BLOCK, axis=3)
        dist_c = (t[:, None] - cmp_end[None, :]).astype(jnp.float32)
        s_c = jnp.einsum('bgrqd,bgnd->bgrqn', qc, kc).astype(jnp.float32) - slopes * dist_c
        p_c = masked_softmax(s_c, dist_c >= 0)
        o_c = jnp.einsum('bgrqn,bgnd->bgrqd', p_c.astype(vc.dtype), vc)
        imp = jnp.einsum('bgrqn,nj->bgqj', p_c, overlap)
        cur = (t // SEL_BLOCK)[:, None]
        forced = (blk_ids == 0) | (blk_ids == cur) | (blk_ids == cur - 1)
        imp = jnp.where(blk_ids <= cur, jnp.where(forced, FORCED_SCORE, imp), -jnp.inf)
        _, sel = lax.top_k(imp, n_top)
        k_g = ks[bi, gi, sel]
        v_g = vs[bi, gi, sel]
        pos = sel[..., None] * SEL_BLOCK + jnp.arange(SEL_BLOCK)
        dist_s = (t[:, None, None] - pos)[:, :, None].astype(jnp.float32)
        s_s = jnp.einsum('bgrqd,bgqnld->bgrqnl', qc, k_g).astype(jnp.float32) - slopes[..., None] * dist_s
        p_s = masked_softmax(s_s, dist_s >= 0, axis=(-2, -1))
        o_s = jnp.einsum('bgrqnl,bgqnld->bgrqd', p_s.astype(v_g.dtype), v_g)
        kwc = lax.dynamic_slice_in_dim(kw, start, NSA_Q_BLOCK + WINDOW, axis=2)
        vwc = lax.dynamic_slice_in_dim(vw, start, NSA_Q_BLOCK + WINDOW, axis=2)
        kp = start - WINDOW + jnp.arange(NSA_Q_BLOCK + WINDOW)
        dist_w = t[:, None] - kp[None, :]
        s_w = jnp.einsum('bgrqd,bgkd->bgrqk', qc, kwc).astype(jnp.float32) - slopes * dist_w.astype(jnp.float32)
        p_w = masked_softmax(s_w, (dist_w >= 0) & (dist_w < WINDOW) & (kp[None, :] >= 0))
        o_w = jnp.einsum('bgrqk,bgkd->bgrqd', p_w.astype(vwc.dtype), vwc)
        o = gc[..., 0:1] * o_c + gc[..., 1:2] * o_s + gc[..., 2:3] * o_w
        return o.transpose(0, 3, 1, 2, 4).reshape(b, NSA_Q_BLOCK, ATT_DIM)

    o = lax.map(query_block, jnp.arange(s // NSA_Q_BLOCK))
    o = o.transpose(1, 0, 2, 3).reshape(b, s, ATT_DIM)
    return o @ w_out

def shared_kv(h, kv_norm, w_kv, k_gain):
    b, s, _ = h.shape
    k, v = jnp.split(rms_norm_2(h, kv_norm) @ w_kv, 2, axis=-1)
    k = rms_norm_2(to_heads(k, MOBA_KV_HEADS), k_gain)
    v = to_heads(v, MOBA_KV_HEADS)
    nb = -(-s // MOBA_BLOCK)
    pad = ((0, 0), (0, 0), (0, nb * MOBA_BLOCK - s), (0, 0))
    kb = jnp.pad(k, pad).reshape(b, MOBA_KV_HEADS, nb, MOBA_BLOCK, HEAD_DIM)
    vb = jnp.pad(v, pad).reshape(b, MOBA_KV_HEADS, nb, MOBA_BLOCK, HEAD_DIM)
    km = jnp.mean(kb.astype(jnp.float32), axis=3).astype(kb.dtype)
    return kb, vb, km

def moba_attention(xn, kb, vb, km, w_q, q_gain, w_out):
    b, s, _ = xn.shape
    g, r = MOBA_KV_HEADS, N_HEADS // MOBA_KV_HEADS
    q = (rms_norm_2(to_heads(xn @ w_q, N_HEADS), q_gain) * HEAD_DIM ** -0.5).reshape(b, g, r, s, HEAD_DIM)
    nb = kb.shape[2]
    ktop = min(MOBA_TOPK, nb)
    slopes = alibi_slopes(N_HEADS).reshape(1, g, r, 1, 1)
    bi = jnp.arange(b)[:, None, None, None, None]
    gi = jnp.arange(g)[None, :, None, None, None]
    blk_ids = jnp.arange(nb)
    offs = jnp.arange(MOBA_BLOCK)

    def query_block(c):
        start = c * MOBA_Q_BLOCK
        t = start + jnp.arange(MOBA_Q_BLOCK)
        cb = start // MOBA_BLOCK
        qc = lax.dynamic_slice_in_dim(q, start, MOBA_Q_BLOCK, axis=3)
        sg = jnp.einsum('bgrqd,bgnd->bgrqn', qc, km).astype(jnp.float32)
        sg = jnp.where(blk_ids < cb, sg, -jnp.inf)
        _, idx = lax.top_k(sg, ktop)
        k_g = kb[bi, gi, idx]
        v_g = vb[bi, gi, idx]
        pos = idx[..., None] * MOBA_BLOCK + offs
        dist = (t[:, None, None] - pos).astype(jnp.float32)
        s_sel = jnp.einsum('bgrqd,bgrqkld->bgrqkl', qc, k_g).astype(jnp.float32)
        s_sel = jnp.where((idx < cb)[..., None], s_sel - slopes[..., None] * dist, -jnp.inf)
        ko = lax.dynamic_index_in_dim(kb, cb, axis=2, keepdims=False)
        vo = lax.dynamic_index_in_dim(vb, cb, axis=2, keepdims=False)
        dist_o = t[:, None] - (cb * MOBA_BLOCK + offs)[None, :]
        s_own = jnp.einsum('bgrqd,bgld->bgrql', qc, ko).astype(jnp.float32)
        s_own = jnp.where(dist_o >= 0, s_own - slopes * dist_o.astype(jnp.float32), -jnp.inf)
        n_sel_keys = ktop * MOBA_BLOCK
        sc = jnp.concatenate([s_sel.reshape(b, g, r, MOBA_Q_BLOCK, n_sel_keys), s_own], axis=-1)
        pr = jax.nn.softmax(sc, axis=-1)
        p_sel = pr[..., :n_sel_keys].reshape(s_sel.shape).astype(vb.dtype)
        p_own = pr[..., n_sel_keys:].astype(vb.dtype)
        o = (jnp.einsum('bgrqkl,bgrqkld->bgrqd', p_sel, v_g)
             + jnp.einsum('bgrql,bgld->bgrqd', p_own, vo))
        return o.transpose(0, 3, 1, 2, 4).reshape(b, MOBA_Q_BLOCK, ATT_DIM)

    o = lax.map(query_block, jnp.arange(s // MOBA_Q_BLOCK))
    o = o.transpose(1, 0, 2, 3).reshape(b, s, ATT_DIM)
    return o @ w_out

def hier_moe(xn, w_group, b_group, w_expert, b_expert, w_gate, w_up, w_down):
    b, s, d = xn.shape
    xt = xn.reshape(b * s, d)
    g_prob = jax.nn.softmax((xt @ w_group + b_group).astype(jnp.float32), axis=-1)
    g_w, g_idx = lax.top_k(g_prob, 1)
    e_logits = (xt @ w_expert + b_expert).astype(jnp.float32).reshape(-1, N_GROUPS, EXPERTS_PER_GROUP)
    e_logits = jnp.einsum('tge,tg->te', e_logits, jax.nn.one_hot(g_idx[:, 0], N_GROUPS, dtype=jnp.float32))
    e_prob = jax.nn.softmax(e_logits, axis=-1)
    e_w, e_idx = lax.top_k(e_prob, TOPK_IN_GROUP)
    e_w = e_w / jnp.sum(e_w, axis=-1, keepdims=True)
    comb = g_w * e_w
    expert_id = g_idx * EXPERTS_PER_GROUP + e_idx
    cw = jnp.einsum('tk,tke->te', comb, jax.nn.one_hot(expert_id, N_EXPERTS, dtype=jnp.float32)).astype(xt.dtype)
    hid = jax.nn.silu(jnp.einsum('td,edf->tef', xt, w_gate)) * jnp.einsum('td,edf->tef', xt, w_up)
    y = jnp.einsum('tef,efd->td', hid * cw[:, :, None], w_down)
    return y.reshape(b, s, d)

def second_inputs(seed: int = 0) -> dict:
    key = jax.random.key(seed)
    keys = iter(jax.random.split(key, 40))

    def nrm(shape, scale):
        return jax.random.normal(next(keys), shape, jnp.float32) * scale

    def gain(shape):
        return 1.0 + 0.05 * jax.random.normal(next(keys), shape, jnp.float32)

    n_a = (DEPTH_2 + 1) // 2
    n_b = DEPTH_2 - n_a
    cmp_in = CMP_BLOCK * HEAD_DIM
    return {
        'x': nrm((BATCH, SEQ, D_MODEL), 1.0),
        'p': nrm((DEPTH_2, BATCH, SEQ, PLE_DIM), 1.0),
        'ln_mix': gain((DEPTH_2, D_MODEL)),
        'ln_ffn': gain((DEPTH_2, D_MODEL)),
        'ln_ple': gain((DEPTH_2, D_MODEL)),
        'a_w_in': nrm((n_a, D_MODEL, NSA_PROJ), D_MODEL ** -0.5),
        'a_q_norm': gain((n_a, HEAD_DIM)),
        'a_k_norm': gain((n_a, 3, HEAD_DIM)),
        'a_ck_pos': nrm((n_a, CMP_BLOCK, HEAD_DIM), 0.1),
        'a_ck_w1': nrm((n_a, cmp_in, CMP_HIDDEN), cmp_in ** -0.5),
        'a_ck_w2': nrm((n_a, CMP_HIDDEN, HEAD_DIM), CMP_HIDDEN ** -0.5),
        'a_cv_pos': nrm((n_a, CMP_BLOCK, HEAD_DIM), 0.1),
        'a_cv_w1': nrm((n_a, cmp_in, CMP_HIDDEN), cmp_in ** -0.5),
        'a_cv_w2': nrm((n_a, CMP_HIDDEN, HEAD_DIM), CMP_HIDDEN ** -0.5),
        'a_w_out': nrm((n_a, ATT_DIM, D_MODEL), ATT_DIM ** -0.5),
        'kv_norm': gain((D_MODEL,)),
        'w_kv_shared': nrm((D_MODEL, 2 * MOBA_KV_DIM), D_MODEL ** -0.5),
        'k_norm_shared': gain((HEAD_DIM,)),
        'b_w_q': nrm((n_b, D_MODEL, ATT_DIM), D_MODEL ** -0.5),
        'b_q_norm': gain((n_b, HEAD_DIM)),
        'b_w_out': nrm((n_b, ATT_DIM, D_MODEL), ATT_DIM ** -0.5),
        'moe_w_group': nrm((DEPTH_2, D_MODEL, N_GROUPS), D_MODEL ** -0.5),
        'moe_b_group': nrm((DEPTH_2, N_GROUPS), 0.01),
        'moe_w_expert': nrm((DEPTH_2, D_MODEL, N_EXPERTS), D_MODEL ** -0.5),
        'moe_b_expert': nrm((DEPTH_2, N_EXPERTS), 0.01),
        'moe_w_gate': nrm((DEPTH_2, N_EXPERTS, D_MODEL, D_EXPERT), D_MODEL ** -0.5),
        'moe_w_up': nrm((DEPTH_2, N_EXPERTS, D_MODEL, D_EXPERT), D_MODEL ** -0.5),
        'moe_w_down': nrm((DEPTH_2, N_EXPERTS, D_EXPERT, D_MODEL), D_EXPERT ** -0.5),
        'ple_w_proj': nrm((DEPTH_2, PLE_DIM, D_MODEL), PLE_DIM ** -0.5),
        'ple_w_gate': nrm((DEPTH_2, D_MODEL, D_MODEL), D_MODEL ** -0.5),
    }

def second_block(x, p, ln_mix, ln_ffn, ln_ple, a_w_in, a_q_norm, a_k_norm, a_ck_pos, a_ck_w1, a_ck_w2,
              a_cv_pos, a_cv_w1, a_cv_w2, a_w_out, kv_norm, w_kv_shared, k_norm_shared, b_w_q, b_q_norm,
              b_w_out, moe_w_group, moe_b_group, moe_w_expert, moe_b_expert, moe_w_gate, moe_w_up,
              moe_w_down, ple_w_proj, ple_w_gate):
    n_a = (DEPTH_2 + 1) // 2
    h = x
    kb = vb = km = None
    for i in range(DEPTH_2):
        xn = rms_norm_2(h, ln_mix[i])
        if i < n_a:
            mix = nsa_attention(xn, a_w_in[i], a_q_norm[i], a_k_norm[i], a_ck_pos[i], a_ck_w1[i], a_ck_w2[i],
                                a_cv_pos[i], a_cv_w1[i], a_cv_w2[i], a_w_out[i])
        else:
            if i == n_a:
                kb, vb, km = shared_kv(h, kv_norm, w_kv_shared, k_norm_shared)
            j = i - n_a
            mix = moba_attention(xn, kb, vb, km, b_w_q[j], b_q_norm[j], b_w_out[j])
        h = h + mix.astype(h.dtype)
        h = h + hier_moe(rms_norm_2(h, ln_ffn[i]), moe_w_group[i], moe_b_group[i], moe_w_expert[i],
                         moe_b_expert[i], moe_w_gate[i], moe_w_up[i], moe_w_down[i]).astype(h.dtype)
        gate = jax.nn.sigmoid(rms_norm_2(h, ln_ple[i]) @ ple_w_gate[i])
        h = h + (gate * (p[i] @ ple_w_proj[i])).astype(h.dtype)
    return h


def setup_inputs(seed=0):
    out = dict(first_inputs(seed))
    for name, value in second_inputs(seed + 1).items():
        if name != "x":
            out[name + "_2"] = value
    return out


def reference(
    x, positions, norm_mix_g, w_in, qnorm_a_g, knorm_a_g, rel_bias, cq_norm_g, ckv_norm_g, w_uq,
    w_ukv, qnorm_b_g, knorm_b_g, w_o, norm_ffn_g, w_ff1, w_ff2, p_2, ln_mix_2, ln_ffn_2,
    ln_ple_2, a_w_in_2, a_q_norm_2, a_k_norm_2, a_ck_pos_2, a_ck_w1_2, a_ck_w2_2, a_cv_pos_2,
    a_cv_w1_2, a_cv_w2_2, a_w_out_2, kv_norm_2, w_kv_shared_2, k_norm_shared_2, b_w_q_2,
    b_q_norm_2, b_w_out_2, moe_w_group_2, moe_b_group_2, moe_w_expert_2, moe_b_expert_2,
    moe_w_gate_2, moe_w_up_2, moe_w_down_2, ple_w_proj_2, ple_w_gate_2,
):
    x = first_block(
        x, positions, norm_mix_g, w_in, qnorm_a_g, knorm_a_g, rel_bias, cq_norm_g, ckv_norm_g,
        w_uq, w_ukv, qnorm_b_g, knorm_b_g, w_o, norm_ffn_g, w_ff1, w_ff2,
    )
    return second_block(
        x, p_2, ln_mix_2, ln_ffn_2, ln_ple_2, a_w_in_2, a_q_norm_2, a_k_norm_2, a_ck_pos_2,
        a_ck_w1_2, a_ck_w2_2, a_cv_pos_2, a_cv_w1_2, a_cv_w2_2, a_w_out_2, kv_norm_2,
        w_kv_shared_2, k_norm_shared_2, b_w_q_2, b_q_norm_2, b_w_out_2, moe_w_group_2,
        moe_b_group_2, moe_w_expert_2, moe_b_expert_2, moe_w_gate_2, moe_w_up_2, moe_w_down_2,
        ple_w_proj_2, ple_w_gate_2,
    )


_drawn_inputs = setup_inputs


def setup_inputs(seed=0):
    import zlib

    import numpy as np

    out = dict(_drawn_inputs(seed))
    spreads = {}
    factors = {'qnorm_a_g': 4.199,
     'knorm_a_g': 4.011,
     'cq_norm_g': 5.852,
     'ckv_norm_g': 3.437,
     'qnorm_b_g': 3.586,
     'knorm_b_g': 3.232,
     'ln_ple_2': 5.016,
     'a_q_norm_2': 6.274,
     'a_k_norm_2': 4.851,
     'a_ck_pos_2': 7.173,
     'kv_norm_2': 3.31,
     'k_norm_shared_2': 5.31,
     'b_q_norm_2': 5.324,
     'moe_b_group_2': 6.15,
     'moe_b_expert_2': 3.996}
    for name, (base, spread) in spreads.items():
        noise = np.random.default_rng([zlib.crc32(name.encode()), seed]).standard_normal(out[name].shape)
        drawn = base * np.exp(spread * noise) if base else spread * noise
        out[name] = jnp.asarray(drawn.astype(out[name].dtype))
    for name, factor in factors.items():
        out[name] = (out[name] * factor).astype(out[name].dtype)
    return out
```

```python
import math

import numpy as np

TOKENS, TILES, P = 256, 2, 128
D_MODEL, KB = 1024, 8
HEADS_A, DIM_A = 8, 64
Q_RANK, KV_RANK, NOPE, ROPE = 768, 256, 64, 32
DIM_B = NOPE + ROPE
IN_WIDTH = 3 * HEADS_A * DIM_A + Q_RANK + KV_RANK + ROPE
NSA_WIDTH = 1024 + 6 * 256 + 48
HEADS, KV_HEADS, DIM = 16, 4, 64
N_CMP, CMP_PAD = 15, 16
EXPERTS, GROUPS, PER_GROUP = 32, 4, 8
SPAN = 384
MASKED = -1e30
EPS = 1e-6
SLOTS, SLOT = 4, 4096

TABLE = {}
_at = 0
for _name, _width in (("ident", 128), ("dist", SPAN), ("causal", SPAN), ("cmp_bias", 512), ("cmp_valid", 128),
                      ("onehot", SPAN), ("log_count", SPAN), ("inv_freq", 16), ("neg_slope", 16),
                      ("rank4", 4), ("rank8", 8)):
    TABLE[_name] = (_at, _width)
    _at += _width
TABLE_WIDTH = _at


def t5_bucket(dist):
    exact = 16
    safe = np.maximum(dist, 1).astype(np.float32)
    large = exact + (np.log(safe / exact) / math.log(2048 / exact) * 16).astype(np.int64)
    return np.where(dist < exact, dist, np.minimum(large, 31))


def constant_table():
    t = np.zeros((P, TABLE_WIDTH), np.float32)

    def put(name, value, rows=P):
        at, width = TABLE[name]
        t[:rows, at:at + width] = value.reshape(rows, width)

    q = np.arange(P)[:, None]
    dist = np.concatenate([q - np.arange(128)[None], 128 + q - np.arange(256)[None]], 1)
    put("ident", np.eye(P, dtype=np.float32))
    put("dist", np.where(dist >= 0, dist, -MASKED).astype(np.float32))
    put("causal", np.where(dist >= 0, 0, MASKED).astype(np.float32))
    slopes = (2.0 ** (-8.0 * np.arange(1, HEADS + 1) / HEADS)).astype(np.float32)
    put("neg_slope", np.broadcast_to(-slopes, (P, HEADS)))
    end = np.arange(CMP_PAD) * 16 + 31
    token = np.arange(TILES)[None, :] * P + np.arange(P)[:, None]
    cd = (token[:, :, None] - end).astype(np.float32)
    ok = (cd >= 0) & (np.arange(CMP_PAD) < N_CMP)
    bias = np.where(ok[:, None, :, None], -slopes.reshape(1, 4, 1, 4, 1) * cd[:, None, :, None], np.float32(MASKED))
    put("cmp_bias", bias.astype(np.float32))
    put("cmp_valid", np.broadcast_to(ok[:, :, None], (P, 2, 4, CMP_PAD)).astype(np.float32))
    d = 255 - np.arange(SPAN)
    real = (d >= 0)
    onehot = (t5_bucket(np.maximum(d, 0))[None] == np.arange(32)[:, None]) & real
    count = ((d <= 128).astype(int) + (d % 4 == 0) + (d % 16 == 0)) * real
    put("onehot", (onehot & (count > 0)).astype(np.float32), 32)
    logs = np.where(count > 0, np.log(np.maximum(count, 1)), MASKED).astype(np.float32)
    put("log_count", np.broadcast_to(logs, (HEADS_A, SPAN)), HEADS_A)
    inv = 1.0 / (10000.0 ** (np.arange(0, ROPE, 2) / ROPE))
    put("inv_freq", np.broadcast_to(inv.astype(np.float32), (P, 16)))
    put("rank4", np.broadcast_to(4.0 - np.arange(4), (P, 4)))
    put("rank8", np.broadcast_to(8.0 - np.arange(8), (P, 8)))
    return t


def build_program(nc, a, out):
    import concourse.bass as bass
    from concourse import mybir
    from contextlib import ExitStack

    F32 = mybir.dt.float32
    ALU, ACT, AX = mybir.AluOpType, mybir.ActivationFunctionType, mybir.AxisListType
    ds = bass.ds
    ctx = ExitStack()

    def sb(name, shape, dt=F32):
        return ctx.enter_context(nc.sbuf_tensor(name, shape, dt))

    def sem(name):
        return ctx.enter_context(nc.semaphore(name))

    bank = ctx.enter_context(nc.psum_tensor("bank", [P, 8, 512], F32))
    ring = sb("ring", [P, SLOTS, SLOT])
    h = sb("h", [P, TILES, D_MODEL])
    rows = sb("rows", [P, TILES, D_MODEL])
    second = sb("second", [P, 2048])
    turned_x = sb("turned_x", [P, KB, TOKENS])
    arena = sb("arena", [P, 8320])
    mix = sb("mix", [P, TILES, D_MODEL])
    toep = sb("toep", [P, HEADS_A, SPAN])
    work = sb("work", [P, 3072])
    table = sb("table", [P, TABLE_WIDTH])
    stat = sb("stat", [P, 1400])
    zeros = sb("zeros", [P, 512])
    junk = sb("junk", [P, 768])
    eps = sb("eps", [P, 1])

    def const(name, n=P):
        at, width = TABLE[name]
        return table[0:n, at:at + width]

    ident = const("ident")
    proj = arena[:, 0:2 * 2624].rearrange("p (t n) -> p t n", t=TILES)
    qb = arena[:, 5248:6784].rearrange("p (t n) -> p t n", t=TILES)
    kb = arena[:, 6784:8320].rearrange("p (t n) -> p t n", t=TILES)
    kvb = second[:, :].rearrange("p (t n) -> p t n", t=TILES)
    second_x = second[:, :].rearrange("p (k n) -> p k n", k=KB)
    moba_q = arena[:, 0:2048].rearrange("p (t n) -> p t n", t=TILES)
    moba_kv = arena[:, 2048:3072].rearrange("p (t n) -> p t n", t=TILES)
    ple_y = arena[:, 0:2048].rearrange("p (t n) -> p t n", t=TILES)
    ple_gate = arena[:, 2048:4096].rearrange("p (t n) -> p t n", t=TILES)
    ple_tmp = arena[:, 4096:6144].rearrange("p (t n) -> p t n", t=TILES)
    token_weight = arena[:, 0:EXPERTS * TOKENS].rearrange("p (e n) -> p e n", e=EXPERTS)

    gains = {}
    for name in ("norm_mix_g", "norm_ffn_g", "ln_mix0", "ln_ffn0", "ln_ple0", "kv_norm", "ln_mix1", "ln_ffn1",
                 "ln_ple1"):
        gains[name] = sb(f"gain_{name}", [P, KB])
    gain_cq, gain_ckv = sb("gain_cq", [P, 6]), sb("gain_ckv", [P, 2])
    head_gain = sb("head_gain", [64, 8])
    gain_bq, gain_bk = sb("gain_bq", [P, DIM_B]), sb("gain_bk", [P, DIM_B])
    pos_rows = sb("pos_rows", [16, 2, P])
    cmp_pos = sb("cmp_pos", [P, 2, 16])
    cmp_w2 = sb("cmp_w2", [P, 2, 2, 64])
    route_w = sb("route_w", [P, 2, KB, 36])
    route_b = sb("route_b", [P, 2, 36])
    rel = sb("rel", [32, HEADS_A])
    pos_i = sb("pos_i", [P, TILES], mybir.dt.int32)
    embed = sb("embed", [P, 2, TILES, 256])

    staged_q = junk[:, 0:768].rearrange("p (t h d) -> p t h d", t=TILES, h=4)
    staged_k = sb("staged_k", [P, TILES, 4, DIM_B])
    staged_k2 = sb("staged_k2", [P, TILES, 1, 64])
    qT = rows[0:DIM_B, 0, :].rearrange("p (h n) -> p h n", h=4)
    kT = rows[0:DIM_B, 1, :].rearrange("p (h n) -> p h n", h=4)
    kT2 = sb("kT2", [64, 1, TOKENS])
    logit = work[:, 0:1536].rearrange("p (h n) -> p h n", h=4)
    prob = work[:, 1536:3072].rearrange("p (h n) -> p h n", h=4)
    probT = sb("probT", [P, 2, SPAN])
    neg_max = sb("neg_max", [P, 4, 2])
    total = sb("total", [P, 8])
    share = sb("share", [P, 8])
    part = sb("part", [P, 8, 64])
    rope = sb("rope", [P, 8, TILES, 16])
    posf = sb("posf", [P, TILES])
    rope_tmp = mix[:, 1, 0:512].rearrange("p (x h d) -> p x h d", x=4, h=8)
    rope_k = sb("rope_k", [P, TILES, ROPE])
    bias_row = mix[0:HEADS_A, 0, 0:SPAN]
    spare = toep[:, :, :].rearrange("p h n -> p (h n)")
    blocks = spare[:, 0:1024].rearrange("p (j g n) -> p j g n", j=16, g=KV_HEADS)
    cmp_hid = spare[:, 1024:1280].rearrange("p (i c n) -> p i c n", i=2, c=2)
    cmp_kv = spare[0:CMP_PAD, 1280:1792].rearrange("p (i g d) -> p i g d", i=2, g=KV_HEADS)
    cmp_sq = spare[0:CMP_PAD, 1792:2048].rearrange("p (g d) -> p g d", g=KV_HEADS)
    kcT = sb("kcT", [64, 64])
    gates = sb("gates", [P, TILES, HEADS, 3])
    cl = sb("cl", [P, 8, CMP_PAD])
    cT = spare[0:CMP_PAD, 2048:3072].rearrange("p (j n) -> p j n", j=8)
    rt = sb("rt", [P, TILES, 256])
    cwT = junk[0:32, 0:TOKENS]
    cw = sb("cw", [P, TILES, EXPERTS])

    toep_dram = nc.dram_tensor("toep_dram", [HEADS_A * P * SPAN], F32).ap()
    cw_dram = nc.dram_tensor("cw_dram", [2, EXPERTS, TOKENS], F32).ap()

    x_loaded, small_loaded, stored = sem("x_loaded"), sem("small_loaded"), sem("stored")
    landed = [sem(f"landed{i}") for i in range(SLOTS)]
    up_landed = [sem(f"up_landed{i}") for i in range(SLOTS)]
    down_landed = [sem(f"down_landed{i}") for i in range(SLOTS)]
    cleared = sem("cleared")
    squares_summed, roots_taken, rows_scaled = sem("squares_summed"), sem("roots_taken"), sem("rows_scaled")
    turned, act_turned, dve_turned = sem("turned"), sem("act_turned"), sem("dve_turned")
    lin_made, act_took, dve_took = sem("lin_made"), sem("act_took"), sem("dve_took")
    squared, sums_ready, scale_ready = sem("squared"), sem("sums_ready"), sem("scale_ready")
    dve_step, pool_step, mix_step = sem("dve_step"), sem("pool_step"), sem("mix_step")
    bias_row_made, bias_row_ready = sem("bias_row_made"), sem("bias_row_ready")
    gains_scaled = sem("gains_scaled")
    pos_turned, pos_ready = sem("pos_turned"), sem("pos_ready")
    toep_spread, toep_ready = sem("toep_spread"), sem("toep_ready")
    angle_ready, sines_ready, latent_ready = sem("angle_ready"), sem("sines_ready"), sem("latent_ready")
    NAMES = ("staged", "front_turned", "act_front", "dve_front", "scores_made", "biased", "maxed", "probs_made",
             "probs_turned", "probT_ready", "values_made", "mixed")
    at_sem = {n: sem(n) for n in NAMES}
    OPENED = ("front_turned", "scores_made", "biased", "mixed")
    OPEN = 2
    (staged, front_turned, act_front, dve_front, scores_made, biased, maxed, probs_made, probs_turned, probT_ready,
     values_made, mixed) = (at_sem[n] for n in NAMES)
    c_scores, c_scored, c_shifted, c_exped, c_probs, c_turned, cT_ready, c_values, c_taken = (
        sem(n) for n in ("c_scores", "c_scored", "c_shifted", "c_exped", "c_probs", "c_turned", "cT_ready",
                         "c_values", "c_taken"))
    doubled, cmp_turned, blocks_made, cmp_hid_made, gelu_done = (
        sem(n) for n in ("doubled", "cmp_turned", "blocks_made", "cmp_hid_made", "gelu_done"))
    cmp_out_made, cmp_rows_ready, kc_turned, kcT_ready, gates_ready = (
        sem(n) for n in ("cmp_out_made", "cmp_rows_ready", "kc_turned", "kcT_ready", "gates_ready"))
    blocks_cleared = sem("blocks_cleared")
    ff_relu_done = sem("ff_relu_done")
    acc_cleared, ff_up_made, ff_hid_ready, ff_down_made, ff_added = (
        sem(n) for n in ("acc_cleared", "ff_up_made", "ff_hid_ready", "ff_down_made", "ff_added"))
    logits_made, shifted, exped, cw_ready, cw_turned, cwT_ready, cw_stored, cw_spread = (
        sem(n) for n in ("logits_made", "shifted", "exped", "cw_ready", "cw_turned", "cwT_ready", "cw_stored",
                         "cw_spread"))
    gateup_made, silu_done, hid_scaled, hid_ready, down_made, moe_added = (
        sem(n) for n in ("gateup_made", "silu_done", "hid_scaled", "hid_ready", "down_made", "moe_added"))
    gated, ple_done = sem("gated"), sem("ple_done")

    chunks, freed = [], []

    def slot(n):
        return ring[:, n % SLOTS, :]

    def wait_landed(eng, n):
        eng.wait_ge(landed[n % SLOTS], 16 * (n // SLOTS + 1))

    lins = []
    took = {"act": 0, "dve": 0}

    def took_sem(engine):
        return act_took if engine == "act" else dve_took

    def linear(name, w, k, n_cols, operand, dest, kind, step=512):
        jobs = []
        for c0 in range(0, n_cols, step):
            width = min(step, n_cols - c0)
            n = len(chunks)
            src = w.rearrange("(p k) n -> p k n", k=k)[:, :, c0:c0 + width]
            view = slot(n)[:, 0:k * width].rearrange("p (k n) -> p k n", k=k)
            chunks.append((view, src))
            for s0 in range(0, width, 512):
                sw = min(512, width - s0)
                for t in range(TILES):
                    engine = "dve" if kind == "add" or (kind == "copy" and t == 1) else "act"
                    job = dict(m=len(lins), chunk=n, view=view[:, :, s0:s0 + sw], k=k, width=sw, t=t, operand=operand,
                               dest=dest[:, t, c0 + s0:c0 + s0 + sw], kind=kind, engine=engine, first=not jobs)
                    took[engine] += 1
                    job["took"] = took[engine]
                    lins.append(job)
                    jobs.append(job)
            freed.append((lin_made, len(lins)))
        return jobs

    turns = []
    turn_took = {"act": 0, "dve": 0}

    def turn(source, k, dests):
        jobs = []
        view = source.rearrange("p t (c k) -> p t k c", k=k)
        for j in range(0, k, 2):
            engine = ("act", "dve")[len(turns) % 2]
            turn_took[engine] += 1
            jobs.append(dict(m=len(turns), j=j, view=view, dests=dests, engine=engine, took=turn_took[engine]))
            turns.append(jobs[-1])
        return jobs

    roots = []
    stat_at = [0]

    def root(n, dim, n_part=P):
        w = stat_at[0]
        stat_at[0] += 6 * n
        v = [stat[0:n_part, w + i * n:w + (i + 1) * n] for i in range(6)]
        roots.append(dict(m=len(roots), sum=v[0], root=v[1], mean=v[2], tmp=v[3], first=v[4], scale=v[5], dim=dim))
        return roots[-1]

    norms = []

    def norm(sources):
        n = dict(m=len(norms), parts=[(s, d, w, root(TILES, w)) for s, d, w in sources],
                 sums=sum(len(x["parts"]) for x in norms) * TILES,
                 scaled=sum(len(x["parts"]) for x in norms) * TILES)
        norms.append(n)
        return n

    n_mix = norm([(h, rows, D_MODEL)])
    t_mix = turn(rows, KB, [(turned_x, gains["norm_mix_g"])])
    l_in = linear("in", a["w_in"], KB, IN_WIDTH, turned_x, proj, "copy")
    c_rows = rows
    n_lat = norm([(proj[:, :, 1536:2304], rows[:, :, 0:Q_RANK], Q_RANK),
                  (proj[:, :, 2304:2560], rows[:, :, Q_RANK:Q_RANK + KV_RANK], KV_RANK)])
    t_cq = turn(rows[:, :, 0:Q_RANK], 6, [(turned_x[:, 0:6, :], gain_cq)])
    t_ckv = turn(rows[:, :, Q_RANK:Q_RANK + KV_RANK], 2, [(turned_x[:, 6:8, :], gain_ckv)])
    l_uq = linear("uq", a["w_uq"], 6, Q_RANK, turned_x[:, 0:6, :], qb, "copy")
    l_ukv = linear("ukv", a["w_ukv"], 2, 1024, turned_x[:, 6:8, :], kvb, "copy", step=1024)
    r_a = root(32, DIM_A)
    r_bq = root(16, DIM_B)
    r_bk = root(16, DIM_B)
    t_mix1 = turn(mix, KB, [(turned_x, None)])
    l_o = linear("o", a["w_o"], KB, D_MODEL, turned_x, h, "add")
    n_ffn = norm([(h, rows, D_MODEL)])
    t_ffn = turn(rows, KB, [(turned_x, gains["norm_ffn_g"])])

    FF = 8
    ff_first = len(chunks)
    ff_order = [("up", 0)]
    for c in range(FF):
        ff_order += ([("up", c + 1)] if c + 1 < FF else []) + [("down", c)]
    for kind, c in ff_order:
        n = len(chunks)
        if kind == "up":
            chunks.append((slot(n).rearrange("p (k n) -> p k n", k=KB),
                           a["w_ff1"].rearrange("(p k) n -> p k n", k=KB)[:, :, c * 512:(c + 1) * 512]))
            freed.append((ff_up_made, 2 * (c + 1)))
        else:
            chunks.append((slot(n).rearrange("p (j n) -> p j n", j=4),
                           a["w_ff2"][c * 512:(c + 1) * 512, :].rearrange("(j p) n -> p j n", p=P)))
            freed.append((ff_down_made, c + 1))

    n_nsa = norm([(h, rows, D_MODEL)])
    t_nsa = turn(rows, KB, [(turned_x, gains["ln_mix0"])])
    l_nsa = linear("nsa", a["a_w_in_2"][0], KB, NSA_WIDTH, turned_x, proj, "copy")
    cmp_chunk = len(chunks)
    for i, w in enumerate(("a_ck_w1_2", "a_cv_w1_2")):
        chunks.append((slot(len(chunks)).rearrange("p (j n) -> p j n", j=16),
                       a[w][0].rearrange("(j p) n -> p j n", p=P)))
        freed.append((cmp_hid_made, i + 1))
    r_nsa = root(48, DIM)
    r_kc = root(4, DIM, CMP_PAD)
    t_mix2 = turn(mix, KB, [(turned_x, None)])
    l_nsa_o = linear("nsa_o", a["a_w_out_2"][0], KB, D_MODEL, turned_x, h, "add")

    def expert_chunks(layer):
        first = len(chunks)
        for e in range(EXPERTS):
            chunks.append(("expert", layer, e))
            freed.append((down_made, OPEN + layer * EXPERTS + e + 1))
        return first

    n_moe, t_moe, moe_first = [None, None], [None, None], [None, None]
    n_ple, t_ple, t_embed, l_embed, l_gate = ([None, None] for _ in range(5))

    def moe_and_ple(layer):
        n_moe[layer] = norm([(h, rows, D_MODEL)])
        t_moe[layer] = turn(rows, KB, [(turned_x, gains[f"ln_ffn{layer}"])])
        moe_first[layer] = expert_chunks(layer)
        t_embed[layer] = turn(embed[:, layer], 2, [(second_x[:, 0:2, :], None)])
        l_embed[layer] = linear("embed", a["ple_w_proj_2"][layer], 2, D_MODEL, second_x[:, 0:2, :], ple_y, "copy",
                                step=1024)
        n_ple[layer] = norm([(h, rows, D_MODEL)])
        t_ple[layer] = turn(rows, KB, [(turned_x, gains[f"ln_ple{layer}"])])
        l_gate[layer] = linear("gate", a["ple_w_gate_2"][layer], KB, D_MODEL, turned_x, ple_gate, "gate")

    moe_and_ple(0)
    n_moba = norm([(h, rows, D_MODEL)])
    t_moba = turn(rows, KB, [(turned_x, gains["ln_mix1"]), (second_x, gains["kv_norm"])])
    l_kv = linear("kv", a["w_kv_shared_2"], KB, 512, second_x, moba_kv, "copy")
    l_q = linear("q", a["b_w_q_2"][0], KB, D_MODEL, turned_x, moba_q, "copy")
    r_moba = root(40, DIM)
    t_mix3 = turn(mix, KB, [(turned_x, None)])
    l_moba_o = linear("moba_o", a["b_w_out_2"][0], KB, D_MODEL, turned_x, h, "add")
    moe_and_ple(1)
    assert stat_at[0] <= 1400

    attended = {n: int(n in OPENED) for n in NAMES}
    mix_steps = [0]

    def heads(view, n, d):
        return view.rearrange("p t (h d) -> p t h d", d=d)

    def scales(r, lo, n):
        return r["scale"].rearrange("p (t h) -> p t h", t=TILES)[:, :, lo:lo + n]

    def attention(times, dim, operands, cores, mix_at, mix_per_core):
        s = dict(times=times, dim=dim, operands=operands, cores=cores, mix_at=mix_at, base=dict(attended),
                 mix_base=mix_steps[0], mix_per=sum(mix_per_core), mix_before=[sum(mix_per_core[:i]) for i in
                                                                             range(len(mix_per_core))])
        n = len(cores)
        per = dict(staged=len(operands), front_turned=len(operands),
                   act_front=sum(o["engine"] == "act" for o in operands),
                   dve_front=sum(o["engine"] == "dve" for o in operands), mixed=n)
        for name in NAMES:
            attended[name] += per.get(name, 4 * n) * times
        s["per"] = per
        mix_steps[0] += s["mix_per"] * times
        return s

    def operand(src, scale, stage, dest, n, banks, gain, engine):
        return dict(src=src, scale=scale, stage=stage, dest=dest, n=n, banks=banks, gain=gain, engine=engine)

    qa = heads(proj[:, :, 0:512], 8, 64)
    ka = heads(proj[:, :, 512:1024], 8, 64)
    va = heads(proj[:, :, 1024:1536], 8, 64)
    att_a = attention(2, 64, [
        operand(qa, scales(r_a, 0, 8), staged_q[:, :, :, 0:64], qT, 4, (0, 1), head_gain[:, 0:1], "act"),
        operand(ka, scales(r_a, 8, 8), staged_k[:, :, :, 0:64], kT, 4, (2, 3), head_gain[:, 1:2], "dve"),
    ], [dict(kT=kT, shared=False, v=va, bias="toep", gate=None, add=False)], 0, [1])
    vb = heads(kvb, 8, 128)[:, :, :, 64:128]
    att_b = attention(2, DIM_B, [
        operand(heads(qb, 8, 96), scales(r_bq, 0, 8), staged_q, qT, 4, (0, 1), None, "act"),
        operand(heads(kb, 8, 96), scales(r_bk, 0, 8), staged_k, kT, 4, (2, 3), None, "dve"),
    ], [dict(kT=kT, shared=False, v=vb, bias="causal", gate=None, add=False)], 8, [1])
    nq = heads(proj[:, :, 0:1024], 16, 64)
    nks, nvs, nkw, nvw = (heads(proj[:, :, 1536 + 256 * i:1792 + 256 * i], 4, 64) for i in range(4))
    att_n = attention(4, 64, [
        operand(nq, scales(r_nsa, 0, 16), staged_q[:, :, :, 0:64], qT, 4, (0, 1), head_gain[:, 2:3], "act"),
        operand(nks, scales(r_nsa, 16, 4), staged_k[:, :, 0:1, 0:64], kT, 1, (2,), head_gain[:, 4:5], "dve"),
        operand(nkw, scales(r_nsa, 20, 4), staged_k2, kT2, 1, (3,), head_gain[:, 5:6], "act"),
    ], [dict(kT=kT, shared=True, v=nvs, bias="alibi", gate=1, add=True),
        dict(kT=kT2, shared=True, v=nvw, bias="alibi", gate=2, add=True)], 0, [3, 3])
    mq = heads(moba_q, 16, 64)
    mk = heads(moba_kv[:, :, 0:256], 4, 64)
    mv = heads(moba_kv[:, :, 256:512], 4, 64)
    att_m = attention(4, 64, [
        operand(mq, scales(r_moba, 0, 16), staged_q[:, :, :, 0:64], qT, 4, (0, 1), head_gain[:, 6:7], "act"),
        operand(mk, scales(r_moba, 16, 4), staged_k[:, :, 0:1, 0:64], kT, 1, (2,), head_gain[:, 7:8], "dve"),
    ], [dict(kT=kT, shared=True, v=mv, bias="alibi", gate=None, add=False)], 0, [1])

    small = []

    def load_small(dest, src):
        small.append((dest, src))

    load_small(table[:, :], a["table"])
    for name, src in (("norm_mix_g", a["norm_mix_g"]), ("norm_ffn_g", a["norm_ffn_g"]),
                      ("ln_mix0", a["ln_mix_2"][0]), ("ln_ffn0", a["ln_ffn_2"][0]), ("ln_ple0", a["ln_ple_2"][0]),
                      ("kv_norm", a["kv_norm_2"]), ("ln_mix1", a["ln_mix_2"][1]), ("ln_ffn1", a["ln_ffn_2"][1]),
                      ("ln_ple1", a["ln_ple_2"][1])):
        load_small(gains[name][:, :], src.rearrange("(p k) -> p k", k=KB))
    load_small(gain_cq[:, :], a["cq_norm_g"].rearrange("(p k) -> p k", k=6))
    load_small(gain_ckv[:, :], a["ckv_norm_g"].rearrange("(p k) -> p k", k=2))
    for i, src in enumerate((a["qnorm_a_g"], a["knorm_a_g"], a["a_q_norm_2"][0], a["a_k_norm_2"][0, 0],
                             a["a_k_norm_2"][0, 1], a["a_k_norm_2"][0, 2], a["b_q_norm_2"][0],
                             a["k_norm_shared_2"])):
        load_small(head_gain[:, i:i + 1], src.unsqueeze(1))
    load_small(gain_bq[:, :], a["qnorm_b_g"].partition_broadcast(P))
    load_small(gain_bk[:, :], a["knorm_b_g"].partition_broadcast(P))
    for i, (pos, w2) in enumerate((("a_ck_pos_2", "a_ck_w2_2"), ("a_cv_pos_2", "a_cv_w2_2"))):
        load_small(pos_rows[:, i, :], a[pos][0].rearrange("(j l) d -> j (l d)", l=2))
        load_small(cmp_w2[:, i], a[w2][0].rearrange("(c p) n -> p c n", p=P))
    for i in range(2):
        load_small(route_w[:, i, :, 0:4], a["moe_w_group_2"][i].rearrange("(p k) n -> p k n", k=KB))
        load_small(route_w[:, i, :, 4:36], a["moe_w_expert_2"][i].rearrange("(p k) n -> p k n", k=KB))
        load_small(route_b[:, i, 0:4], a["moe_b_group_2"][i].partition_broadcast(P))
        load_small(route_b[:, i, 4:36], a["moe_b_expert_2"][i].partition_broadcast(P))
        load_small(embed[:, i], a["p_2"][i, 0].rearrange("(t p) n -> p t n", p=P))
    load_small(rel[:, :], a["rel_bias"])
    load_small(pos_i[:, :], a["positions"][0].rearrange("(t p) -> p t", p=P))

    def wait_small(eng):
        eng.wait_ge(small_loaded, 16 * len(small))

    def act_norm(act, n):
        for i, (src, dest, width, r) in enumerate(n["parts"]):
            for t in range(TILES):
                nc.scalar.activation(dest[:, t, :], src[:, t, :], ACT.Square,
                                     accum_out=r["sum"][:, t:t + 1]).then_inc(squares_summed, 1)
            act.wait_ge(squares_summed, n["sums"] + TILES * (i + 1))
            act_root(act, r)

    def act_root(act, r):
        nc.scalar.activation(r["root"], r["sum"], ACT.Sqrt, scale=1.0 / r["dim"],
                             bias=eps[0:r["sum"].shape[0], 0:1]).then_inc(roots_taken, 1)

    dve_steps = [0]

    def dve_link(dve, ins):
        dve_steps[0] += 1
        ins.then_inc(dve_step, 1)
        dve.wait_ge(dve_step, dve_steps[0])

    def dve_root(dve, r, signal=None):
        dve.wait_ge(roots_taken, r["m"] + 1)
        dve_link(dve, nc.vector.reciprocal(r["first"], r["root"]))
        dve_link(dve, nc.vector.tensor_scalar(r["mean"], r["sum"], 1.0 / r["dim"], EPS, ALU.mult, ALU.add))
        dve_link(dve, nc.vector.tensor_tensor(r["tmp"], r["first"], r["first"], ALU.mult))
        dve_link(dve, nc.vector.tensor_tensor(r["mean"], r["tmp"], r["mean"], ALU.mult))
        dve_link(dve, nc.vector.tensor_scalar(r["tmp"], r["mean"], -0.5, 1.5, ALU.mult, ALU.add))
        last = nc.vector.tensor_tensor(r["scale"], r["first"], r["tmp"], ALU.mult)
        if signal is None:
            dve_link(dve, last)
        else:
            last.then_inc(signal, 1)

    def dve_norm(dve, n):
        for i, (src, dest, _, r) in enumerate(n["parts"]):
            dve_root(dve, r)
            for t in range(TILES):
                nc.vector.tensor_scalar(dest[:, t, :], src[:, t, :], r["scale"][:, t:t + 1], None,
                                        ALU.mult).then_inc(rows_scaled, 1)

    def pe_turn(pe, jobs):
        for j in jobs:
            if j["m"] >= 4:
                before = turns[j["m"] - 4]
                pe.wait_ge(act_turned if before["engine"] == "act" else dve_turned, before["took"])
            b = 4 + j["m"] % 4
            for kk in range(2):
                for t in range(TILES):
                    mm = nc.tensor.transpose(bank[:, b, kk * 256 + t * P:kk * 256 + (t + 1) * P],
                                             j["view"][:, t, j["j"] + kk, :], ident)
            mm.then_inc(turned, 1)

    def take_turn(eng, jobs, engine):
        for j in jobs:
            if j["engine"] != engine:
                continue
            eng.wait_ge(turned, j["m"] + 1)
            b = 4 + j["m"] % 4
            for dest, gain in j["dests"]:
                if gain is None:
                    src, to = bank[:, b, :], dest[:, j["j"]:j["j"] + 2, :].rearrange("p k n -> p (k n)")
                    last = (nc.scalar.copy(to, src) if engine == "act" else nc.vector.tensor_copy(to, src))
                    continue
                for kk in range(2):
                    k = j["j"] + kk
                    src = bank[:, b, kk * 256:kk * 256 + 256]
                    if engine == "act":
                        last = nc.scalar.activation(dest[:, k, :], src, ACT.Copy, scale=gain[:, k:k + 1])
                    else:
                        last = nc.vector.tensor_scalar(dest[:, k, :], src, gain[:, k:k + 1], None, ALU.mult)
            last.then_inc(act_turned if engine == "act" else dve_turned, 1)

    def wait_turned(eng, jobs):
        for engine, s in (("act", act_turned), ("dve", dve_turned)):
            n = max((j["took"] for j in jobs if j["engine"] == engine), default=0)
            if n:
                eng.wait_ge(s, n)

    def pe_linear(pe, jobs):
        chunk = None
        for j in jobs:
            if j["chunk"] != chunk:
                chunk = j["chunk"]
                wait_landed(pe, chunk)
            if j["m"] >= 4:
                before = lins[j["m"] - 4]
                pe.wait_ge(took_sem(before["engine"]), before["took"])
            for k in range(j["k"]):
                mm = nc.tensor.matmul(bank[:, j["m"] % 4, 0:j["width"]], j["operand"][:, k, j["t"] * P:(j["t"] + 1) * P],
                                      j["view"][:, k, :], start=k == 0, stop=k == j["k"] - 1)
            mm.then_inc(lin_made, 1)

    def take_linear(eng, jobs, engine):
        for j in jobs:
            if j["engine"] != engine:
                continue
            eng.wait_ge(lin_made, j["m"] + 1)
            src = bank[:, j["m"] % 4, 0:j["width"]]
            if j["kind"] == "add":
                nc.vector.tensor_tensor(j["dest"], j["dest"], src, ALU.add).then_inc(dve_took, 1)
            elif j["kind"] == "gate":
                nc.scalar.activation(j["dest"], src, ACT.Sigmoid).then_inc(act_took, 1)
            elif engine == "act":
                nc.scalar.copy(j["dest"], src).then_inc(act_took, 1)
            else:
                nc.vector.tensor_copy(j["dest"], src).then_inc(dve_took, 1)

    def wait_took(eng, jobs):
        for engine in ("act", "dve"):
            n = max((j["took"] for j in jobs if j["engine"] == engine), default=0)
            if n:
                eng.wait_ge(took_sem(engine), n)

    def pool_attention(pool, s):
        b, n_op = s["base"], len(s["operands"])
        with pool.Fori(0, s["times"]) as i:
            for o, x in enumerate(s["operands"]):
                pool.wait_ge(front_turned, b["front_turned"] + i * n_op)
                for t in range(TILES):
                    last = nc.gpsimd.tensor_tensor(
                        x["stage"][:, t], x["src"][:, t, ds(i * x["n"], x["n"]), :],
                        x["scale"][:, t, ds(i * x["n"], x["n"])].unsqueeze(2).to_broadcast([P, x["n"], s["dim"]]),
                        ALU.mult)
                last.then_inc(staged, 1)

    def pe_attention(pe, s, compressed=False):
        b, n_op, n_core, d = s["base"], len(s["operands"]), len(s["cores"]), s["dim"]
        with pe.Fori(0, s["times"]) as i:
            pe.wait_ge(biased, b["biased"] + i * (4 * n_core))
            for o, x in enumerate(s["operands"]):
                pe.wait_ge(staged, b["staged"] + i * n_op + (o + 1))
                for r in range(x["n"]):
                    for t in range(TILES):
                        to = bank[0:d, x["banks"][r // 2], (r % 2) * 256 + t * P:(r % 2) * 256 + (t + 1) * P]
                        if r == t == 0:
                            mm = nc.tensor.matmul(to, x["stage"][:, t, r, :], ident, start=True, stop=True)
                        else:
                            mm = nc.tensor.transpose(to, x["stage"][:, t, r, :], ident)
                mm.then_inc(front_turned, 1)
            pe.wait_ge(act_front, b["act_front"] + (i + 1) * s["per"]["act_front"])
            pe.wait_ge(dve_front, b["dve_front"] + (i + 1) * s["per"]["dve_front"])
            if compressed:
                pe_compressed(pe, i, b)
            for c, core in enumerate(s["cores"]):
                n0 = i * (4 * n_core) + 4 * c
                for r in range(4):
                    if c:
                        pe.wait_ge(biased, b["biased"] + n0 + (r - 3))
                    kr = 0 if core["shared"] else r
                    nc.tensor.matmul(bank[:, r, 0:P], qT[0:d, r, 0:P], core["kT"][0:d, kr, 0:P], start=True, stop=True)
                    nc.tensor.matmul(bank[:, r, P:SPAN], qT[0:d, r, P:2 * P], core["kT"][0:d, kr, :],
                                     start=True, stop=True).then_inc(scores_made, 1)

                def turn_probs(r):
                    pe.wait_ge(probs_made, b["probs_made"] + n0 + (r + 1))
                    if r >= 2:
                        pe.wait_ge(probT_ready, b["probT_ready"] + n0 + (r - 1))
                    for q in range(3):
                        mm = nc.tensor.transpose(bank[:, 4 + r % 2, q * P:(q + 1) * P],
                                                 prob[:, r, q * P:(q + 1) * P], ident)
                    mm.then_inc(probs_turned, 1)

                def values(r):
                    pe.wait_ge(probT_ready, b["probT_ready"] + n0 + (r + 1))
                    if r == 0:
                        pe.wait_ge(mixed, b["mixed"] + i * n_core + c)
                    v = core["v"]
                    head = i if core["shared"] else i * 4 + r
                    for t, q, kt, start, stop in ((0, 0, 0, True, True), (1, 1, 0, True, False), (1, 2, 1, False, True)):
                        mm = nc.tensor.matmul(bank[:, 6, t * 256 + r * 64:t * 256 + (r + 1) * 64],
                                              probT[:, r % 2, q * P:(q + 1) * P], v[:, kt, head, :],
                                              start=start, stop=stop)
                    mm.then_inc(values_made, 1)

                for r in range(4):
                    turn_probs(r)
                    if r:
                        values(r - 1)
                values(3)

    def act_attention(act, s, compressed=False):
        b, n_core, d = s["base"], len(s["cores"]), s["dim"]
        mine = [(o, x) for o, x in enumerate(s["operands"]) if x["engine"] == "act"]
        with act.Fori(0, s["times"]) as i:
            act.wait_ge(scores_made, b["scores_made"] + i * (4 * n_core))
            for o, x in mine:
                take_front(act, x, i, s, o)
            if compressed:
                act_compressed(act, i)
            for c in range(n_core):
                n0 = i * (4 * n_core) + 4 * c

                def exps(r):
                    act.wait_ge(maxed, b["maxed"] + n0 + (r + 1))
                    for t, (lo, hi) in enumerate(((0, P), (P, SPAN))):
                        last = nc.scalar.activation(prob[:, r, lo:hi], logit[:, r, lo:hi], ACT.Exp,
                                                    bias=neg_max[:, r, t:t + 1],
                                                    accum_out=total[:, t * 4 + r:t * 4 + r + 1])
                    last.then_inc(probs_made, 1)

                def take_probs(r):
                    act.wait_ge(probs_turned, b["probs_turned"] + n0 + (r + 1))
                    if r >= 2:
                        act.wait_ge(values_made, b["values_made"] + n0 + (r - 1))
                    nc.scalar.copy(probT[:, r % 2, :], bank[:, 4 + r % 2, 0:SPAN]).then_inc(probT_ready, 1)

                exps(0)
                for r in range(1, 4):
                    exps(r)
                    take_probs(r - 1)
                take_probs(3)

    def take_front(eng, x, i, s, o):
        d, b = s["dim"], s["base"]
        eng.wait_ge(front_turned, b["front_turned"] + i * len(s["operands"]) + (o + 1))
        for n, bk in enumerate(x["banks"]):
            heads_here = min(2, x["n"] - 2 * n)
            src = bank[0:d, bk, 0:heads_here * 256]
            to = x["dest"][0:d, 2 * n:2 * n + heads_here, :].rearrange("p h n -> p (h n)")
            if x["engine"] == "act":
                if x["gain"] is None:
                    last = nc.scalar.copy(to, src)
                else:
                    last = nc.scalar.activation(to, src, ACT.Copy, scale=x["gain"])
            elif x["gain"] is None:
                last = nc.vector.tensor_copy(to, src)
            else:
                last = nc.vector.tensor_scalar(to, src, x["gain"], None, ALU.mult)
        last.then_inc(act_front if x["engine"] == "act" else dve_front, 1)

    def dve_attention(dve, s, compressed=False):
        b, n_core, d = s["base"], len(s["cores"]), s["dim"]
        with dve.Fori(0, s["times"]) as i:
            dve.wait_ge(scores_made, b["scores_made"] + i * (4 * n_core))
            for o, x in enumerate(s["operands"]):
                if x["engine"] == "dve":
                    take_front(dve, x, i, s, o)
            if compressed:
                dve_compressed(dve, i)
            for c, core in enumerate(s["cores"]):
                n0 = i * (4 * n_core) + 4 * c
                for r in range(4):
                    dve.wait_ge(scores_made, b["scores_made"] + n0 + (r + 1))
                    src = bank[:, r, 0:SPAN]
                    if core["bias"] == "toep":
                        ins = nc.vector.scalar_tensor_tensor(out=logit[:, r, :], in0=src, scalar=DIM_A ** -0.5,
                                                             in1=toep[:, i * 4 + r, :], op0=ALU.mult, op1=ALU.add)
                    elif core["bias"] == "causal":
                        ins = nc.vector.scalar_tensor_tensor(out=logit[:, r, :], in0=src, scalar=DIM_B ** -0.5,
                                                             in1=const("causal"), op0=ALU.mult, op1=ALU.add)
                    else:
                        ins = nc.vector.scalar_tensor_tensor(out=logit[:, r, :], in0=const("dist"),
                                                             scalar=const("neg_slope")[:, ds(i * 4 + r, 1)], in1=src,
                                                             op0=ALU.mult, op1=ALU.add)
                    ins.then_inc(biased, 1)
                    dve.wait_ge(biased, b["biased"] + n0 + (r + 1))
                    nc.vector.tensor_reduce(neg_max[:, r, 0:1], logit[:, r, 0:P], AX.X, ALU.max, negate=True)
                    nc.vector.tensor_reduce(neg_max[:, r, 1:2], logit[:, r, P:SPAN], AX.X, ALU.max,
                                            negate=True).then_inc(maxed, 1)
                step = s["mix_base"] + i * s["mix_per"] + s["mix_before"][c]
                dve.wait_ge(values_made, b["values_made"] + n0 + 4)
                nc.vector.reciprocal(share[:, :], total[:, :]).then_inc(mix_step, 1)
                dve.wait_ge(mix_step, step + 1)
                here = mix.rearrange("p t (h d) -> p t h d", d=64)[:, :, ds(i * 4 + s["mix_at"], 4), :]
                values = bank[:, 6, :].rearrange("p (t h d) -> p t h d", t=TILES, h=4)
                share4 = share[:, :].rearrange("p (t h) -> p t h", t=TILES)
                shares = share4.unsqueeze(3).to_broadcast([P, TILES, 4, 64])
                if core["gate"] is None:
                    nc.vector.tensor_tensor(here, values, shares, ALU.mult).then_inc(mixed, 1)
                else:
                    nc.vector.tensor_tensor(share4, share4, gates[:, :, ds(i * 4, 4), core["gate"]],
                                            ALU.mult).then_inc(mix_step, 1)
                    dve.wait_ge(mix_step, step + 2)
                    nc.vector.tensor_tensor(part[:, :, :].rearrange("p (t h) d -> p t h d", t=TILES), values, shares,
                                            ALU.mult).then_inc(mixed, 1)
                    dve.wait_ge(mixed, b["mixed"] + i * n_core + (c + 1))
                    nc.vector.tensor_tensor(here, here, part[:, :, :].rearrange("p (t h) d -> p t h d", t=TILES),
                                            ALU.add).then_inc(mix_step, 1)
                    dve.wait_ge(mix_step, step + 3)

    def pe_compressed(pe, i, b):
        pe.wait_ge(c_scored, i + OPEN)
        for t in range(TILES):
            for r in range(4):
                at = (t * 4 + r) * CMP_PAD
                mm = nc.tensor.matmul(bank[:, 7, at:at + CMP_PAD], qT[0:64, r, t * P:(t + 1) * P],
                                      kcT[0:64, ds(i * CMP_PAD, CMP_PAD)], start=True, stop=True)
        mm.then_inc(c_scores, 1)
        pe.wait_ge(c_probs, i + 1)
        for j in range(8):
            mm = nc.tensor.transpose(bank[0:CMP_PAD, 4 + j // 4, (j % 4) * P:(j % 4 + 1) * P], cl[:, j, :], ident)
        mm.then_inc(c_turned, 1)
        pe.wait_ge(cT_ready, i + 1)
        pe.wait_ge(mixed, b["mixed"] + i * 2)
        for j in range(8):
            mm = nc.tensor.matmul(bank[:, 6, j * 64:(j + 1) * 64], cT[:, j, :], cmp_kv[:, 1, i, :], start=True,
                                  stop=True)
        mm.then_inc(c_values, 1)
        pe.wait_ge(c_taken, i + 1)

    def act_compressed(act, i):
        act.wait_ge(c_shifted, i + 1)
        nc.scalar.activation(cl[:, :, :], cl[:, :, :], ACT.Exp).then_inc(c_exped, 1)
        act.wait_ge(c_turned, i + 1)
        nc.scalar.copy(cT[:, 0:4, :].rearrange("p j n -> p (j n)"), bank[0:CMP_PAD, 4, :])
        nc.scalar.copy(cT[:, 4:8, :].rearrange("p j n -> p (j n)"), bank[0:CMP_PAD, 5, :]).then_inc(cT_ready, 1)

    c_steps = sem("c_steps")

    def dve_compressed(dve, i):
        n = [0]

        def link(ins):
            n[0] += 1
            ins.then_inc(c_steps, 1)
            dve.wait_ge(c_steps, i * 6 + n[0])

        dve.wait_ge(c_scores, i + 1)
        nc.vector.tensor_tensor(cl[:, :, :].rearrange("p j n -> p (j n)"), bank[:, 7, 0:128],
                                const("cmp_bias").rearrange("p (g n) -> p g n", g=4)[:, i, :],
                                ALU.add).then_inc(c_scored, 1)
        dve.wait_ge(c_scored, i + (OPEN + 1))
        link(nc.vector.tensor_reduce(share[:, :], cl[:, :, :], AX.X, ALU.max))
        nc.vector.tensor_tensor(cl[:, :, :], cl[:, :, :], share[:, :].unsqueeze(2).to_broadcast([P, 8, CMP_PAD]),
                                ALU.subtract).then_inc(c_shifted, 1)
        dve.wait_ge(c_exped, i + 1)
        nc.vector.tensor_tensor(cl[:, :, :].rearrange("p j n -> p (j n)"), cl[:, :, :].rearrange("p j n -> p (j n)"),
                                const("cmp_valid"), ALU.mult).then_inc(c_probs, 1)
        dve.wait_ge(c_probs, i + 1)
        link(nc.vector.tensor_reduce(share[:, :], cl[:, :, :], AX.X, ALU.add))
        link(nc.vector.tensor_scalar(share[:, :], share[:, :], 1e-30, None, ALU.max))
        link(nc.vector.reciprocal(share[:, :], share[:, :]))
        share4 = share[:, :].rearrange("p (t h) -> p t h", t=TILES)
        link(nc.vector.tensor_tensor(share4, share4, gates[:, :, ds(i * 4, 4), 0], ALU.mult))
        dve.wait_ge(c_values, i + 1)
        here = mix.rearrange("p t (h d) -> p t h d", d=64)[:, :, ds(i * 4, 4), :]
        nc.vector.tensor_tensor(here, bank[:, 6, :].rearrange("p (t h d) -> p t h d", t=TILES, h=4),
                                share4.unsqueeze(3).to_broadcast([P, TILES, 4, 64]), ALU.mult).then_inc(c_taken, 1)
        dve.wait_ge(c_taken, i + 1)
        link(nc.vector.memset(part[:, 0, 0:1], 0.0))

    def pe_clear(pe, n):
        for q in range(4):
            mm = nc.tensor.matmul(bank[:, q, :], zeros[0:32, 0:P], zeros[0:32, :], start=True, stop=False,
                                  skip_group_check=True)
        mm.then_inc(acc_cleared, 1)

    def pe_ffn(pe):
        def up(c, n, value, hid_value):
            pe.wait_ge(landed[n % SLOTS], value)
            for half in range(2):
                b = 4 + 2 * (c % 2) + half
                if hid_value is not None:
                    pe.wait_ge(ff_relu_done, hid_value + half)
                for q in range(2):
                    f = 2 * half + q
                    for k in range(KB):
                        mm = nc.tensor.matmul(bank[:, b, q * 256:(q + 1) * 256],
                                              slot(n)[:, k * 512 + f * P:k * 512 + (f + 1) * P], turned_x[:, k, :],
                                              start=k == 0, stop=k == KB - 1)
                mm.then_inc(ff_up_made, 1)

        def down(c, n, value, hid_value):
            pe.wait_ge(landed[n % SLOTS], value)
            pe.wait_ge(ff_hid_ready, hid_value)
            for j in range(4):
                for t in range(TILES):
                    for half in range(2):
                        mm = nc.tensor.matmul(bank[:, 2 * t + half, :], ff_hid(c)[:, j, t * P:(t + 1) * P],
                                              slot(n)[:, j * 1024 + half * 512:j * 1024 + (half + 1) * 512],
                                              start=False, stop=False, skip_group_check=True)
            mm.then_inc(ff_down_made, 1)

        def at(n, i=0):
            return 16 * (n // SLOTS + 1) + i * 16

        f = ff_first
        up(0, f, at(f), None)
        with pe.Fori(0, 3) as i:
            for u in range(2):
                up(u + 1, f + 1 + 2 * u, at(f + 1 + 2 * u, i), i * 4 + (2 * u - 1 + OPEN))
                down(u, f + 2 + 2 * u, at(f + 2 + 2 * u, i), i * 4 + 2 * u + 2)
        up(7, f + 13, at(f + 13), OPEN + 11)
        down(6, f + 14, at(f + 14), 14)
        down(7, f + 15, at(f + 15), 16)

    def ff_hid(c):
        return work[:, (c % 2) * 1024:(c % 2 + 1) * 1024].rearrange("p (j n) -> p j n", j=4)

    def act_ffn(act):
        def relu(c, made, down_value):
            for half in range(2):
                act.wait_ge(ff_up_made, made + half + 1)
                if down_value is not None and half == 0:
                    act.wait_ge(ff_down_made, down_value)
                nc.scalar.activation(ff_hid(c)[:, 2 * half:2 * half + 2, :].rearrange("p j n -> p (j n)"),
                                     bank[:, 4 + 2 * (c % 2) + half, :], ACT.Relu).then_inc(ff_relu_done, 1)

        relu(0, 0, None)
        relu(1, 2, None)
        with act.Fori(0, 3) as i:
            for u in range(2):
                relu(u, i * 4 + (4 + 2 * u), i * 2 + (u + 1))

    def dve_ffn(dve):
        with dve.Fori(0, FF // 2) as i:
            for c in range(2):
                for half in range(2):
                    dve.wait_ge(ff_relu_done, i * 4 + (OPEN + 2 * c + half + 1))
                    x = ff_hid(c)[:, 2 * half:2 * half + 2, :].rearrange("p j n -> p (j n)")
                    nc.vector.tensor_tensor(x, x, x, ALU.mult).then_inc(ff_hid_ready, 1)
        add_banks(dve, ff_down_made, FF, ff_added)

    def add_banks(dve, s, value, signal):
        dve.wait_ge(s, value)
        for t in range(TILES):
            for half in range(2):
                cols = h[:, t, half * 512:(half + 1) * 512]
                nc.vector.tensor_tensor(cols, cols, bank[:, 2 * t + half, :], ALU.add).then_inc(signal, 1)

    def expert(slot_n):
        s = slot(slot_n)
        return (s[:, 0:1024].rearrange("p (k f) -> p k f", k=KB), s[:, 1024:2048].rearrange("p (k f) -> p k f", k=KB),
                s[:, 2048:3072])

    def expert_views(layer):
        return (a["moe_w_gate_2"][layer].rearrange("e (p k) f -> p e (k f)", k=KB),
                a["moe_w_up_2"][layer].rearrange("e (p k) f -> p e (k f)", k=KB),
                a["moe_w_down_2"][layer].rearrange("e p n -> p e n"))

    def sp_experts(sp, layer):
        first = moe_first[layer]
        views = expert_views(layer)

        def load(u, e, before):
            s, n = (first + u) % SLOTS, first + u
            sp.wait_ge(*before)
            sp.dma_start(ring[:, s, 0:1024], views[0][:, e, :]).then_inc(landed[s], 16)
            sp.dma_start(ring[:, s, 1024:2048], views[1][:, e, :]).then_inc(up_landed[s], 16)
            sp.dma_start(ring[:, s, 2048:3072], views[2][:, e, :]).then_inc(down_landed[s], 16)

        for u in range(SLOTS):
            load(u, u, freed[first + u - SLOTS])
        with sp.Fori(0, EXPERTS // SLOTS - 1) as i:
            for u in range(SLOTS):
                load(u, i * SLOTS + (SLOTS + u), (down_made, OPEN + layer * EXPERTS + u + 1 + i * SLOTS))

    def pe_experts(pe, layer):
        first, e0 = moe_first[layer], layer * EXPERTS

        def gate_up(u, i):
            n = first + u
            s = n % SLOTS
            gate, up, _ = expert(n)
            b = 4 + u % 2
            pe.wait_ge(landed[s], 16 * (n // SLOTS + 1) + i * 16)
            if not (isinstance(i, int) and i == 0 and u < 2):
                pe.wait_ge(hid_scaled, e0 + u - 1 + i * SLOTS)
            for k in range(KB):
                nc.tensor.matmul(bank[:, b, 0:256], gate[:, k, :], turned_x[:, k, :], start=k == 0, stop=k == KB - 1)
            pe.wait_ge(up_landed[s], 16 * (8 * layer + u // SLOTS + 1) + i * 16)
            for k in range(KB):
                mm = nc.tensor.matmul(bank[:, b, 256:512], up[:, k, :], turned_x[:, k, :], start=k == 0,
                                      stop=k == KB - 1)
            mm.then_inc(gateup_made, 1)

        def down(u, i):
            n = first + u
            s = n % SLOTS
            w = expert(n)[2]
            pe.wait_ge(down_landed[s], 16 * (8 * layer + u // SLOTS + 1) + i * 16)
            pe.wait_ge(hid_ready, e0 + u + 1 + i * SLOTS)
            for t in range(TILES):
                for half in range(2):
                    mm = nc.tensor.matmul(bank[:, 2 * t + half, :], moe_hid(u)[:, t * P:(t + 1) * P],
                                          w[:, half * 512:(half + 1) * 512], start=False, stop=False,
                                          skip_group_check=True)
            mm.then_inc(down_made, 1)

        gate_up(0, 0)
        gate_up(1, 0)
        down(0, 0)
        with pe.Fori(0, EXPERTS // SLOTS - 1) as i:
            for u in range(SLOTS):
                gate_up(u + 2, i)
                down(u + 1, i)
        last = EXPERTS - SLOTS
        for u in range(2, SLOTS):
            gate_up(last + u, 0)
            down(last + u - 1, 0)
        down(last + 3, 0)

    def moe_hid(u):
        return work[:, (u % 2) * 256:(u % 2 + 1) * 256]

    def silu_rows(u):
        return work[:, 512 + (u % 2) * 256:512 + (u % 2 + 1) * 256]

    def act_experts(act, layer):
        e0 = layer * EXPERTS
        with act.Fori(0, EXPERTS // 2) as i:
            for u in range(2):
                act.wait_ge(gateup_made, e0 + u + 1 + i * 2)
                nc.scalar.activation(silu_rows(u), bank[:, 4 + u, 0:256], ACT.Silu).then_inc(silu_done, 1)

    def dve_experts(dve, layer):
        e0 = layer * EXPERTS
        with dve.Fori(0, EXPERTS // SLOTS) as i:
            dve.wait_ge(cw_spread, 16 * (8 * layer + 1) + i * 16)
            for u in range(SLOTS):
                dve.wait_ge(silu_done, e0 + u + 1 + i * SLOTS)
                nc.vector.tensor_tensor(silu_rows(u), silu_rows(u), bank[:, 4 + u % 2, 256:512],
                                        ALU.mult).then_inc(hid_scaled, 1)
                dve.wait_ge(hid_scaled, e0 + u + 1 + i * SLOTS)
                dve.wait_ge(down_made, OPEN + e0 + u - 1 + i * SLOTS)
                nc.vector.tensor_tensor(moe_hid(u), silu_rows(u), token_weight[:, i * SLOTS + u, :],
                                        ALU.mult).then_inc(hid_ready, 1)
        add_banks(dve, down_made, OPEN + e0 + EXPERTS, moe_added)

    def pool_spread(pool, layer):
        pool.wait_ge(cwT_ready, layer + 1)
        pool.dma_start(cw_dram[layer], cwT[:, :]).then_inc(cw_stored, 16)
        pool.wait_ge(cw_stored, 16 * (layer + 1))
        src = cw_dram[layer].rearrange("e n -> (e n)")
        with pool.Fori(0, EXPERTS // SLOTS) as i:
            pool.dma_start(arena[:, ds(i * (SLOTS * TOKENS), SLOTS * TOKENS)],
                           src[ds(i * (SLOTS * TOKENS), SLOTS * TOKENS)].partition_broadcast(P)).then_inc(cw_spread, 16)
            pool.wait_ge(cw_spread, 16 * (8 * layer + 1) + i * 16)

    def pe_route(pe, layer):
        for t in range(TILES):
            for k in range(KB):
                mm = nc.tensor.matmul(bank[:, 6, t * 64:t * 64 + 36], turned_x[:, k, t * P:(t + 1) * P],
                                      route_w[:, layer, k, :], start=k == 0, stop=k == KB - 1)
        mm.then_inc(logits_made, 1)
        pe.wait_ge(cw_ready, layer + 1)
        for t in range(TILES):
            mm = nc.tensor.transpose(bank[0:32, 7, t * P:(t + 1) * P], cw[:, t, :], ident)
        mm.then_inc(cw_turned, 1)

    def act_route(act, layer):
        for q, (lo, hi) in enumerate(((40, 44), (48, 56))):
            act.wait_ge(shifted, 2 * layer + q + 1)
            nc.scalar.activation(rt[:, :, lo + 20:hi + 20], rt[:, :, lo:hi], ACT.Exp).then_inc(exped, 1)
        act.wait_ge(cw_turned, layer + 1)
        nc.scalar.copy(cwT[:, :], bank[0:32, 7, 0:256]).then_inc(cwT_ready, 1)

    def dve_route(dve, layer):
        v = nc.vector

        def link(ins):
            dve_link(dve, ins)

        def c1(at):
            return rt[:, :, at]

        def wide(x, n):
            return x.unsqueeze(2).to_broadcast([P, TILES, n])

        dve.wait_ge(logits_made, layer + 1)
        link(v.tensor_tensor(rt[:, :, 0:36], bank[:, 6, 0:128].rearrange("p (t n) -> p t n", t=TILES)[:, :, 0:36],
                             route_b[:, layer, :].unsqueeze(1).to_broadcast([P, TILES, 36]), ALU.add))
        link(v.tensor_reduce(c1(36), rt[:, :, 0:4], AX.X, ALU.max))
        v.tensor_tensor(rt[:, :, 40:44], rt[:, :, 0:4], wide(c1(36), 4), ALU.subtract).then_inc(shifted, 1)
        dve.wait_ge(exped, 2 * layer + 1)
        group_p = rt[:, :, 60:64]
        link(v.tensor_reduce(c1(37), group_p, AX.X, ALU.add))
        link(v.reciprocal(c1(38), c1(37)))

        def first_best(values, best, n, rank, out_at, tmp_at):
            tmp, hot = rt[:, :, tmp_at:tmp_at + n], rt[:, :, out_at:out_at + n]
            link(v.tensor_tensor(tmp, values, wide(best, n), ALU.is_equal))
            link(v.tensor_tensor(tmp, tmp, rank.unsqueeze(1).to_broadcast([P, TILES, n]), ALU.mult))
            link(v.tensor_reduce(c1(39), tmp, AX.X, ALU.max))
            link(v.tensor_tensor(hot, tmp, wide(c1(39), n), ALU.is_equal))
            return hot

        link(v.tensor_reduce(c1(45), group_p, AX.X, ALU.max))
        group_hot = first_best(group_p, c1(45), 4, const("rank4"), 80, 84)
        for t in range(TILES):
            link(v.tensor_tensor(rt[:, t, 96:128].rearrange("p (g j) -> p g j", g=4),
                                 rt[:, t, 4:36].rearrange("p (g j) -> p g j", g=4),
                                 group_hot[:, t].unsqueeze(2).to_broadcast([P, 4, 8]), ALU.mult))
            link(v.tensor_reduce(rt[:, t, 88:96], rt[:, t, 96:128].rearrange("p (g j) -> p j g", g=4), AX.X, ALU.add))
        link(v.tensor_reduce(c1(46), rt[:, :, 88:96], AX.X, ALU.max))
        v.tensor_tensor(rt[:, :, 48:56], rt[:, :, 88:96], wide(c1(46), 8), ALU.subtract).then_inc(shifted, 1)
        dve.wait_ge(exped, 2 * layer + 2)
        e = rt[:, :, 68:76]
        link(v.tensor_reduce(c1(47), e, AX.X, ALU.max))
        hot1 = first_best(e, c1(47), 8, const("rank8"), 128, 136)
        link(v.scalar_tensor_tensor(out=rt[:, :, 144:152], in0=hot1, scalar=-4.0, in1=e, op0=ALU.mult, op1=ALU.add))
        link(v.tensor_reduce(c1(56), rt[:, :, 144:152], AX.X, ALU.max))
        hot2 = first_best(rt[:, :, 144:152], c1(56), 8, const("rank8"), 152, 160)
        link(v.tensor_tensor(c1(57), c1(47), c1(56), ALU.add))
        link(v.reciprocal(c1(57), c1(57)))
        link(v.tensor_tensor(c1(57), c1(57), c1(38), ALU.mult))
        link(v.tensor_tensor(c1(58), c1(57), c1(56), ALU.mult))
        link(v.tensor_tensor(c1(57), c1(57), c1(47), ALU.mult))
        link(v.tensor_tensor(hot1, hot1, wide(c1(57), 8), ALU.mult))
        link(v.tensor_tensor(hot2, hot2, wide(c1(58), 8), ALU.mult))
        link(v.tensor_tensor(hot1, hot1, hot2, ALU.add))
        for t in range(TILES):
            last = v.tensor_tensor(cw[:, t, :].rearrange("p (g j) -> p g j", g=4),
                                   group_hot[:, t].unsqueeze(2).to_broadcast([P, 4, 8]),
                                   hot1[:, t].unsqueeze(1).to_broadcast([P, 4, 8]), ALU.mult)
        last.then_inc(cw_ready, 1)

    def pe_moe_and_ple(pe, layer):
        pe.wait_ge(rows_scaled, n_moe[layer]["scaled"] + 2)
        pe_turn(pe, t_moe[layer])
        wait_turned(pe, t_moe[layer])
        pe_route(pe, layer)
        pe_clear(pe, layer + 1)
        pe_experts(pe, layer)
        pe_turn(pe, t_embed[layer])
        wait_turned(pe, t_embed[layer])
        pe.wait_ge(moe_added, 4 * (layer + 1))
        pe_linear(pe, l_embed[layer])
        pe.wait_ge(rows_scaled, n_ple[layer]["scaled"] + 2)
        pe_turn(pe, t_ple[layer])
        wait_turned(pe, t_ple[layer])
        pe_linear(pe, l_gate[layer])

    def act_moe_and_ple(act, layer):
        act_norm(act, n_moe[layer])
        take_turn(act, t_moe[layer], "act")
        act_route(act, layer)
        act_experts(act, layer)
        take_turn(act, t_embed[layer], "act")
        act.wait_ge(moe_added, 4 * (layer + 1))
        act_norm(act, n_ple[layer])
        take_linear(act, l_embed[layer], "act")
        take_turn(act, t_ple[layer], "act")
        take_linear(act, l_gate[layer], "act")
        act.wait_ge(ple_done, 2 * (layer + 1))

    def dve_moe_and_ple(dve, layer):
        dve_norm(dve, n_moe[layer])
        take_turn(dve, t_moe[layer], "dve")
        dve_route(dve, layer)
        dve_experts(dve, layer)
        take_turn(dve, t_embed[layer], "dve")
        dve.wait_ge(moe_added, 4 * (layer + 1))
        dve_norm(dve, n_ple[layer])
        take_linear(dve, l_embed[layer], "dve")
        take_turn(dve, t_ple[layer], "dve")
        wait_took(dve, l_embed[layer])
        wait_took(dve, l_gate[layer])
        for t in range(TILES):
            nc.vector.tensor_tensor(ple_tmp[:, t], ple_gate[:, t], ple_y[:, t], ALU.mult).then_inc(gated, 1)
        for t in range(TILES):
            dve.wait_ge(gated, 2 * layer + t + 1)
            nc.vector.tensor_tensor(h[:, t], h[:, t], ple_tmp[:, t], ALU.add).then_inc(ple_done, 1)
        dve.wait_ge(ple_done, 2 * (layer + 1))

    block = ctx.enter_context(nc.Block())

    def sp_chunk(sp, n):
        if n >= SLOTS:
            sp.wait_ge(*freed[n - SLOTS])
        view, src = chunks[n]
        sp.dma_start(view, src).then_inc(landed[n % SLOTS], 16)

    @block.sync
    def _(sp):
        for t in range(TILES):
            sp.dma_start(h[:, t, :], a["x"][0, t * P:(t + 1) * P, :]).then_inc(x_loaded, 16)
        for n in range(moe_first[0]):
            sp_chunk(sp, n)
        sp_experts(sp, 0)
        for n in range(moe_first[0] + EXPERTS, moe_first[1]):
            sp_chunk(sp, n)
        sp_experts(sp, 1)
        for n in range(moe_first[1] + EXPERTS, len(chunks)):
            sp_chunk(sp, n)
        sp.wait_ge(ple_done, 4)
        for t in range(TILES):
            sp.dma_start(out[0, t * P:(t + 1) * P, :], h[:, t, :]).then_inc(stored, 16)
        sp.wait_ge(stored, 32)

    @block.gpsimd
    def _(pool):
        steps = [0]

        def link(ins):
            steps[0] += 1
            ins.then_inc(pool_step, 1)
            pool.wait_ge(pool_step, steps[0])

        g = nc.gpsimd
        g.memset(zeros[:, :], 0.0)
        g.memset(eps[:, :], EPS).then_inc(cleared, 1)
        for dest, src in small:
            pool.dma_start(dest, src, allow_slow_non_contiguous=True).then_inc(small_loaded, 16)

        pool.wait_ge(bias_row_ready, 1)
        pool.dma_start(toep_dram.rearrange("(h p n) -> h p n", h=HEADS_A, p=P),
                       bias_row[:, :].unsqueeze(1).to_broadcast([HEADS_A, P, SPAN])).then_inc(toep_spread, 16)
        pool.wait_ge(toep_spread, 16)
        pool.dma_start(toep[:, :, P:SPAN], bass.AP(toep_dram.tensor, 127, [[SPAN - 1, P], [P * SPAN, HEADS_A], [1, 256]])
                       ).then_inc(toep_ready, 16)
        pool.dma_start(toep[:, :, 0:P], bass.AP(toep_dram.tensor, 255, [[SPAN - 1, P], [P * SPAN, HEADS_A], [1, P]])
                       ).then_inc(toep_ready, 16)

        wait_took(pool, l_ukv)
        pool.wait_ge(squared, 4)
        pool.wait_ge(sines_ready, 2)
        wait_small(pool)
        q4, k4, kv4 = heads(qb, 8, 96), heads(kb, 8, 96), heads(kvb, 8, 128)
        sine, cosine = rope[:, 6], rope[:, 7]
        for t in range(TILES):
            g.tensor_tensor(k4[:, t, :, 0:NOPE], kv4[:, t, :, 0:NOPE],
                            gain_bk[:, 0:NOPE].unsqueeze(1).to_broadcast([P, 8, NOPE]), ALU.mult)
            g.tensor_tensor(rope_k[:, t, :], proj[:, t, 2560:2592], gain_bk[:, NOPE:DIM_B], ALU.mult)
            link(g.tensor_tensor(q4[:, t], q4[:, t], gain_bq[:, :].unsqueeze(1).to_broadcast([P, 8, DIM_B]), ALU.mult))
            for x1, x2, n in ((q4[:, t, :, NOPE:NOPE + 16], q4[:, t, :, NOPE + 16:DIM_B], 8),
                              (rope_k[:, t, 0:16].unsqueeze(1), rope_k[:, t, 16:32].unsqueeze(1), 1)):
                cos = cosine[:, t].unsqueeze(1).to_broadcast([P, n, 16])
                sin = sine[:, t].unsqueeze(1).to_broadcast([P, n, 16])
                tmp = rope_tmp[:, :, 0:n, :]
                g.tensor_tensor(tmp[:, 0], x1, cos, ALU.mult)
                g.tensor_tensor(tmp[:, 1], x2, sin, ALU.mult)
                g.tensor_tensor(tmp[:, 2], x2, cos, ALU.mult)
                link(g.tensor_tensor(tmp[:, 3], x1, sin, ALU.mult))
                g.tensor_tensor(x1, tmp[:, 0], tmp[:, 1], ALU.subtract)
                link(g.tensor_tensor(x2, tmp[:, 2], tmp[:, 3], ALU.add))
            link(g.tensor_copy(k4[:, t, :, NOPE:DIM_B], rope_k[:, t].unsqueeze(1).to_broadcast([P, 8, ROPE])))
        pool.wait_ge(scale_ready, 1)
        pool_attention(pool, att_a)
        pool.wait_ge(scale_ready, 3)
        pool_attention(pool, att_b)

        wait_took(pool, l_nsa)
        g.memset(blocks, 0.0).then_inc(blocks_cleared, 1)
        for i in range(2):
            for t in range(TILES):
                src = proj[:, t, 1024 + 256 * i:1280 + 256 * i].rearrange("p (g d) -> p g d", d=64)
                last = g.tensor_copy(rows[:, i, t * 512:(t + 1) * 512].rearrange("p (g x d) -> p g x d", g=4, x=2),
                                     src.unsqueeze(2).to_broadcast([P, 4, 2, 64]))
            last.then_inc(doubled, 1)
        pool.wait_ge(scale_ready, 4)
        pool_attention(pool, att_n)
        pool_spread(pool, 0)
        pool.wait_ge(scale_ready, 5)
        pool_attention(pool, att_m)
        pool_spread(pool, 1)

    @block.tensor
    def _(pe):
        for s in (front_turned, scores_made):
            pe.sem_inc(s, 1)
        pe.sem_inc(down_made, OPEN)
        pe.wait_ge(cleared, 1)
        wait_small(pe)
        nc.tensor.matmul(bank[0:HEADS_A, 0, 0:SPAN], rel[:, :], const("onehot", 32), start=True,
                         stop=True).then_inc(bias_row_made, 1)
        for i in range(2):
            mm = nc.tensor.transpose(bank[:, 1, i * 16:(i + 1) * 16], pos_rows[:, i, :], ident[0:16, 0:16])
        mm.then_inc(pos_turned, 1)
        pe.wait_ge(bias_row_ready, 1)
        pe.wait_ge(pos_ready, 1)
        pe.wait_ge(rows_scaled, n_mix["scaled"] + 2)
        pe_turn(pe, t_mix)
        wait_turned(pe, t_mix)
        pe_linear(pe, l_in)
        pe.wait_ge(rows_scaled, n_lat["scaled"] + 4)
        pe_turn(pe, t_cq)
        pe_turn(pe, t_ckv)
        wait_turned(pe, t_cq + t_ckv)
        pe_linear(pe, l_uq)
        pe_linear(pe, l_ukv)
        wait_took(pe, l_ukv)
        pe_attention(pe, att_a)
        pe_attention(pe, att_b)
        pe.wait_ge(mixed, att_n["base"]["mixed"])
        pe_turn(pe, t_mix1)
        wait_turned(pe, t_mix1)
        pe_linear(pe, l_o)
        pe.wait_ge(rows_scaled, n_ffn["scaled"] + 2)
        pe_turn(pe, t_ffn)
        wait_turned(pe, t_ffn)
        pe_clear(pe, 0)
        pe_ffn(pe)
        pe.wait_ge(rows_scaled, n_nsa["scaled"] + 2)
        pe_turn(pe, t_nsa)
        wait_turned(pe, t_nsa)
        pe_linear(pe, l_nsa)
        wait_took(pe, l_nsa)
        for i in range(2):
            pe.wait_ge(doubled, i + 1)
            for gr in range(4):
                for t in range(TILES):
                    mm = nc.tensor.transpose(
                        bank[:, 2 * i + gr // 2, (gr % 2) * 256 + t * P:(gr % 2) * 256 + (t + 1) * P],
                        rows[:, i, t * 512 + gr * P:t * 512 + (gr + 1) * P], ident)
            mm.then_inc(cmp_turned, 1)
        for i in range(2):
            n = cmp_chunk + i
            wait_landed(pe, n)
            pe.wait_ge(blocks_made, i + 1)
            for c in range(2):
                for j in range(16):
                    mm = nc.tensor.matmul(bank[:, 4 + i, c * 64:(c + 1) * 64],
                                          slot(n)[:, j * 256 + c * P:j * 256 + (c + 1) * P],
                                          blocks[:, j, :, :].rearrange("p g n -> p (g n)"), start=j == 0, stop=j == 15)
            mm.then_inc(cmp_hid_made, 1)
        for i in range(2):
            pe.wait_ge(gelu_done, i + 1)
            for gr in range(4):
                for c in range(2):
                    mm = nc.tensor.matmul(bank[0:CMP_PAD, 6 + i, gr * 64:(gr + 1) * 64],
                                          cmp_hid[:, i, c, gr * CMP_PAD:(gr + 1) * CMP_PAD], cmp_w2[:, i, c, :],
                                          start=c == 0, stop=c == 1)
            mm.then_inc(cmp_out_made, 1)
        pe.wait_ge(cmp_rows_ready, 1)
        for gr in range(4):
            mm = nc.tensor.transpose(bank[0:64, 4, gr * CMP_PAD:(gr + 1) * CMP_PAD], cmp_kv[:, 0, gr, :],
                                     ident[0:CMP_PAD, 0:CMP_PAD])
        mm.then_inc(kc_turned, 1)
        pe.wait_ge(kcT_ready, 1)
        pe_attention(pe, att_n, compressed=True)
        pe.wait_ge(mix_step, att_n["mix_base"] + 4 * att_n["mix_per"])
        pe_turn(pe, t_mix2)
        wait_turned(pe, t_mix2)
        pe_linear(pe, l_nsa_o)
        pe_moe_and_ple(pe, 0)
        pe.wait_ge(rows_scaled, n_moba["scaled"] + 2)
        pe_turn(pe, t_moba)
        wait_turned(pe, t_moba)
        pe_linear(pe, l_kv)
        pe_linear(pe, l_q)
        wait_took(pe, l_kv + l_q)
        pe_attention(pe, att_m)
        pe.wait_ge(mixed, attended["mixed"])
        pe_turn(pe, t_mix3)
        wait_turned(pe, t_mix3)
        pe_linear(pe, l_moba_o)
        pe_moe_and_ple(pe, 1)

    @block.scalar
    def _(act):
        def squares(dest, src, last=False):
            ins = nc.scalar.activation(dest, src, ACT.Square)
            if last:
                ins.then_inc(squared, 1)

        act.sem_inc(ff_relu_done, OPEN)
        act.wait_ge(cleared, 1)
        act.wait_ge(x_loaded, 32)
        act_norm(act, n_mix)
        act.wait_ge(angle_ready, 1)
        nc.scalar.activation(rope[:, 6], rope[:, 4], ACT.Sin).then_inc(sines_ready, 1)
        nc.scalar.activation(rope[:, 7], rope[:, 5], ACT.Sin).then_inc(sines_ready, 1)
        wait_small(act)
        act.wait_ge(gains_scaled, 2)
        take_turn(act, t_mix, "act")
        take_linear(act, l_in, "act")
        wait_took(act, l_in)
        act_norm(act, n_lat)
        work_a = work[:, 0:2048].rearrange("p (t n) -> p t n", t=TILES)
        for t in range(TILES):
            squares(work_a[:, t], proj[:, t, 0:1024], last=t == 1)
        take_turn(act, t_cq, "act")
        take_turn(act, t_ckv, "act")
        take_linear(act, l_uq, "act")
        take_linear(act, l_ukv, "act")
        wait_took(act, l_uq + l_ukv)
        act.wait_ge(sums_ready, 1)
        act_root(act, r_a)
        squares(work[:, 0:1536], arena[:, 5248:6784], last=True)
        for t in range(TILES):
            squares(work[:, 1536 + t * 512:2048 + t * 512].rearrange("p (h d) -> p h d", d=64),
                    heads(kvb, 8, 128)[:, t, :, 0:NOPE], last=t == 1)
        squares(work[:, 2560:2624].rearrange("p (t d) -> p t d", t=TILES), proj[:, :, 2560:2592], last=True)
        act.wait_ge(sums_ready, 3)
        act_root(act, r_bq)
        act_root(act, r_bk)
        act_attention(act, att_a)
        act_attention(act, att_b)
        take_turn(act, t_mix1, "act")
        wait_took(act, l_o)
        act_norm(act, n_ffn)
        take_turn(act, t_ffn, "act")
        act_ffn(act)
        act.wait_ge(ff_added, 4)
        act_norm(act, n_nsa)
        take_turn(act, t_nsa, "act")
        take_linear(act, l_nsa, "act")
        wait_took(act, l_nsa)
        for t in range(TILES):
            squares(work[:, t * 1024:(t + 1) * 1024], proj[:, t, 0:1024])
        for t in range(TILES):
            for q, c0 in enumerate((1536, 2048)):
                squares(work[:, 2048 + q * 512 + t * 256:2304 + q * 512 + t * 256], proj[:, t, c0:c0 + 256],
                        last=t == 1 and q == 1)
        nc.scalar.activation(gates[:, :, :, :].rearrange("p t h b -> p t (h b)"), proj[:, :, 2560:2608],
                             ACT.Sigmoid).then_inc(gates_ready, 1)
        for i in range(2):
            act.wait_ge(cmp_hid_made, i + 1)
            nc.scalar.activation(cmp_hid[:, i].rearrange("p c n -> p (c n)"), bank[:, 4 + i, 0:128],
                                 ACT.Gelu_apprx_tanh).then_inc(gelu_done, 1)
        act.wait_ge(sums_ready, 4)
        act_root(act, r_nsa)
        act.wait_ge(sums_ready, 5)
        act_root(act, r_kc)
        act_attention(act, att_n, compressed=True)
        take_turn(act, t_mix2, "act")
        wait_took(act, l_nsa_o)
        act_moe_and_ple(act, 0)
        act_norm(act, n_moba)
        take_turn(act, t_moba, "act")
        take_linear(act, l_kv, "act")
        take_linear(act, l_q, "act")
        wait_took(act, l_kv + l_q)
        for t in range(TILES):
            squares(work[:, t * 1024:(t + 1) * 1024], moba_q[:, t, :])
        for t in range(TILES):
            squares(work[:, 2048 + t * 256:2304 + t * 256], moba_kv[:, t, 0:256], last=t == 1)
        act.wait_ge(sums_ready, 6)
        act_root(act, r_moba)
        act_attention(act, att_m)
        take_turn(act, t_mix3, "act")
        wait_took(act, l_moba_o)
        act_moe_and_ple(act, 1)

    @block.vector
    def _(dve):
        v = nc.vector

        def link(ins):
            dve_link(dve, ins)

        for s in (biased, mixed):
            dve.sem_inc(s, 1)
        dve.sem_inc(c_scored, OPEN)
        dve.wait_ge(x_loaded, 32)
        dve_norm(dve, n_mix)
        wait_small(dve)
        dve.wait_ge(bias_row_made, 1)
        v.tensor_tensor(bias_row[:, :], bank[0:HEADS_A, 0, 0:SPAN], const("log_count", HEADS_A),
                        ALU.add).then_inc(bias_row_ready, 1)
        dve.wait_ge(pos_turned, 1)
        v.tensor_copy(cmp_pos[:, :, :].rearrange("p i j -> p (i j)"), bank[:, 1, 0:32]).then_inc(pos_ready, 1)
        for col in (2, 6):
            v.tensor_scalar(head_gain[:, col:col + 1], head_gain[:, col:col + 1], DIM ** -0.5, None,
                            ALU.mult).then_inc(gains_scaled, 1)
        link(v.tensor_copy(posf[:, :], pos_i[:, :]))
        for t in range(TILES):
            last = v.tensor_scalar(rope[:, 0, t], const("inv_freq"), posf[:, t:t + 1], None, ALU.mult)
        link(last)
        magic = 12582912.0
        p1 = 6.28125
        p2 = float(np.float32(2 * math.pi - p1))
        p2 = float(np.frombuffer((np.float32(p2).view(np.uint32) & np.uint32(0xFFFFF000)).tobytes(), np.float32)[0])
        p3 = float(np.float32(2 * math.pi - p1 - p2))
        link(v.tensor_scalar(rope[:, 1], rope[:, 0], 1 / (2 * math.pi), magic, ALU.mult, ALU.add))
        link(v.tensor_scalar(rope[:, 1], rope[:, 1], magic, None, ALU.subtract))
        for src, part_of, dest in ((0, p1, 2), (2, p2, 3), (3, p3, 2)):
            link(v.scalar_tensor_tensor(out=rope[:, dest], in0=rope[:, 1], scalar=-part_of, in1=rope[:, src],
                                        op0=ALU.mult, op1=ALU.add))
        link(v.tensor_scalar(rope[:, 4], rope[:, 2], 3.1415925, -3.1415925, ALU.min, ALU.max))
        link(v.scalar_tensor_tensor(out=rope[:, 3], in0=rope[:, 4], scalar=-1.0, in1=rope[:, 4], op0=ALU.mult,
                                    op1=ALU.max))
        v.tensor_scalar(rope[:, 5], rope[:, 3], -1.0, math.pi / 2, ALU.mult, ALU.add).then_inc(angle_ready, 1)
        take_turn(dve, t_mix, "dve")
        take_linear(dve, l_in, "dve")
        wait_took(dve, l_in)
        dve_norm(dve, n_lat)
        dve.wait_ge(squared, 1)
        v.tensor_reduce(r_a["sum"], work[:, 0:2048].rearrange("p (h d) -> p h d", d=64), AX.X,
                        ALU.add).then_inc(sums_ready, 1)
        take_turn(dve, t_cq, "dve")
        take_turn(dve, t_ckv, "dve")
        take_linear(dve, l_uq, "dve")
        take_linear(dve, l_ukv, "dve")
        dve_root(dve, r_a, scale_ready)
        dve.wait_ge(squared, 4)
        v.tensor_reduce(r_bq["sum"], work[:, 0:1536].rearrange("p (h d) -> p h d", d=96), AX.X,
                        ALU.add).then_inc(sums_ready, 1)
        v.tensor_reduce(stat[:, 1390:1392], work[:, 2560:2624].rearrange("p (h d) -> p h d", d=32), AX.X, ALU.add)
        link(v.tensor_reduce(r_bk["sum"], work[:, 1536:2560].rearrange("p (h d) -> p h d", d=64), AX.X, ALU.add))
        v.tensor_tensor(r_bk["sum"].rearrange("p (t h) -> p t h", t=TILES),
                        r_bk["sum"].rearrange("p (t h) -> p t h", t=TILES),
                        stat[:, 1390:1392].unsqueeze(2).to_broadcast([P, TILES, 8]), ALU.add).then_inc(sums_ready, 1)
        dve_root(dve, r_bq, scale_ready)
        dve_root(dve, r_bk, scale_ready)
        dve.wait_ge(toep_ready, 32)
        dve_attention(dve, att_a)
        dve_attention(dve, att_b)
        take_turn(dve, t_mix1, "dve")
        take_linear(dve, l_o, "dve")
        wait_took(dve, l_o)
        dve_norm(dve, n_ffn)
        take_turn(dve, t_ffn, "dve")
        dve_ffn(dve)
        dve.wait_ge(ff_added, 4)
        dve_norm(dve, n_nsa)
        take_turn(dve, t_nsa, "dve")
        take_linear(dve, l_nsa, "dve")
        dve.wait_ge(squared, 5)
        r3 = r_nsa["sum"].rearrange("p (t h) -> p t h", t=TILES)
        v.tensor_reduce(r3[:, :, 0:16], work[:, 0:2048].rearrange("p (t h d) -> p t h d", t=TILES, d=64), AX.X, ALU.add)
        for q in range(2):
            last = v.tensor_reduce(r3[:, :, 16 + 4 * q:20 + 4 * q],
                                   work[:, 2048 + q * 512:2560 + q * 512].rearrange("p (t h d) -> p t h d", t=TILES,
                                                                                    d=64), AX.X, ALU.add)
        last.then_inc(sums_ready, 1)
        dve.wait_ge(blocks_cleared, 1)
        for i in range(2):
            dve.wait_ge(cmp_turned, i + 1)
            if i:
                dve.wait_ge(cmp_hid_made, 1)
            for gr in range(4):
                for half in range(2):
                    lo = 64 * half
                    at = bank[lo:lo + 64, 2 * i + gr // 2, (gr % 2) * 256 + half:(gr % 2) * 256 + half + 1]
                    src = bass.AP(at.tensor, at.offset, [list(at.ap[0]), [2, 16], [16, N_CMP]])
                    last = v.tensor_tensor(blocks[lo:lo + 64, :, gr, 0:N_CMP], src,
                                           cmp_pos[lo:lo + 64, i, :].unsqueeze(2).to_broadcast([64, 16, N_CMP]),
                                           ALU.add)
            last.then_inc(blocks_made, 1)
        dve_root(dve, r_nsa, scale_ready)
        for i in range(2):
            dve.wait_ge(cmp_out_made, i + 1)
            link(v.tensor_copy(cmp_kv[:, i].rearrange("p g d -> p (g d)"), bank[0:CMP_PAD, 6 + i, 0:256]))
        link(v.tensor_tensor(cmp_sq[:, :, :], cmp_kv[:, 0], cmp_kv[:, 0], ALU.mult))
        v.tensor_reduce(r_kc["sum"], cmp_sq[:, :, :], AX.X, ALU.add).then_inc(sums_ready, 1)
        dve_root(dve, r_kc)
        v.tensor_tensor(cmp_kv[:, 0], cmp_kv[:, 0], r_kc["scale"].unsqueeze(2).to_broadcast([CMP_PAD, 4, 64]),
                        ALU.mult).then_inc(cmp_rows_ready, 1)
        dve.wait_ge(kc_turned, 1)
        v.tensor_scalar(kcT[:, :], bank[0:64, 4, 0:64], head_gain[:, 3:4], None, ALU.mult).then_inc(kcT_ready, 1)
        dve.wait_ge(gates_ready, 1)
        dve_attention(dve, att_n, compressed=True)
        take_turn(dve, t_mix2, "dve")
        take_linear(dve, l_nsa_o, "dve")
        wait_took(dve, l_nsa_o)
        dve_moe_and_ple(dve, 0)
        dve_norm(dve, n_moba)
        take_turn(dve, t_moba, "dve")
        take_linear(dve, l_kv, "dve")
        take_linear(dve, l_q, "dve")
        dve.wait_ge(squared, 6)
        r3 = r_moba["sum"].rearrange("p (t h) -> p t h", t=TILES)
        v.tensor_reduce(r3[:, :, 0:16], work[:, 0:2048].rearrange("p (t h d) -> p t h d", t=TILES, d=64), AX.X, ALU.add)
        v.tensor_reduce(r3[:, :, 16:20], work[:, 2048:2560].rearrange("p (t h d) -> p t h d", t=TILES, d=64), AX.X,
                        ALU.add).then_inc(sums_ready, 1)
        dve_root(dve, r_moba, scale_ready)
        dve_attention(dve, att_m)
        take_turn(dve, t_mix3, "dve")
        take_linear(dve, l_moba_o, "dve")
        wait_took(dve, l_moba_o)
        dve_moe_and_ple(dve, 1)

    ctx.close()


INPUTS = (
    "x", "positions", "norm_mix_g", "w_in", "qnorm_a_g", "knorm_a_g", "rel_bias", "cq_norm_g", "ckv_norm_g", "w_uq",
    "w_ukv", "qnorm_b_g", "knorm_b_g", "w_o", "norm_ffn_g", "w_ff1", "w_ff2", "p_2", "ln_mix_2", "ln_ffn_2",
    "ln_ple_2", "a_w_in_2", "a_q_norm_2", "a_k_norm_2", "a_ck_pos_2", "a_ck_w1_2", "a_ck_w2_2", "a_cv_pos_2",
    "a_cv_w1_2", "a_cv_w2_2", "a_w_out_2", "kv_norm_2", "w_kv_shared_2", "k_norm_shared_2", "b_w_q_2",
    "b_q_norm_2", "b_w_out_2", "moe_w_group_2", "moe_b_group_2", "moe_w_expert_2", "moe_b_expert_2",
    "moe_w_gate_2", "moe_w_up_2", "moe_w_down_2", "ple_w_proj_2", "ple_w_gate_2",
)


def kernel(**inputs):
    import concourse.bacc as bacc
    from concourse import mybir
    from concourse.bass_utils import run_bass_kernel_spmd

    nc = bacc.Bacc("TRN2", target_bir_lowering=False, num_devices=1)
    arrays, aps = {}, {}
    given = {name: np.ascontiguousarray(inputs[name]) for name in INPUTS}
    given["table"] = constant_table()
    for name, value in given.items():
        arrays[f"in_{name}"] = value
        aps[name] = nc.dram_tensor(f"in_{name}", value.shape, mybir.dt.from_np(value.dtype),
                                   kind="ExternalInput").ap()
    out = nc.dram_tensor("out_0", (1, TOKENS, D_MODEL), mybir.dt.float32, kind="ExternalOutput").ap()
    build_program(nc, aps, out)
    result = run_bass_kernel_spmd(nc, [arrays], core_ids=[0])
    return result.results[0]["out_0"]
```

```python
import math

import numpy as np

TOKENS, TILES, P = 256, 2, 128
D_MODEL, KB = 1024, 8
HEADS_A, DIM_A = 8, 64
Q_RANK, KV_RANK, NOPE, ROPE = 768, 256, 64, 32
DIM_B = NOPE + ROPE
IN_WIDTH = 3 * HEADS_A * DIM_A + Q_RANK + KV_RANK + ROPE
NSA_WIDTH = 1024 + 6 * 256 + 48
HEADS, KV_HEADS, DIM = 16, 4, 64
N_CMP, CMP_PAD = 15, 16
EXPERTS, GROUPS, PER_GROUP = 32, 4, 8
SPAN = 384
MASKED = -1e30
EPS = 1e-6
SLOTS, SLOT, PAIRS = 8, 1024, 4
UNITS, RAW, UNIT = 32, 3, 3072

TABLE = {}
_at = 0
for _name, _width in (("ident", 128), ("dist", SPAN), ("causal", SPAN), ("cmp_bias", 512), ("cmp_valid", 128),
                      ("onehot", SPAN), ("log_count", SPAN), ("inv_freq", 16), ("neg_slope", 16),
                      ("rank4", 4), ("rank8", 8)):
    TABLE[_name] = (_at, _width)
    _at += _width
TABLE_WIDTH = _at


def t5_bucket(dist):
    exact = 16
    safe = np.maximum(dist, 1).astype(np.float32)
    large = exact + (np.log(safe / exact) / math.log(2048 / exact) * 16).astype(np.int64)
    return np.where(dist < exact, dist, np.minimum(large, 31))


def constant_table():
    t = np.zeros((P, TABLE_WIDTH), np.float32)

    def put(name, value, rows=P):
        at, width = TABLE[name]
        t[:rows, at:at + width] = value.reshape(rows, width)

    q = np.arange(P)[:, None]
    dist = np.concatenate([q - np.arange(128)[None], 128 + q - np.arange(256)[None]], 1)
    put("ident", np.eye(P, dtype=np.float32))
    put("dist", np.where(dist >= 0, dist, -MASKED).astype(np.float32))
    put("causal", np.where(dist >= 0, 0, MASKED).astype(np.float32))
    slopes = (2.0 ** (-8.0 * np.arange(1, HEADS + 1) / HEADS)).astype(np.float32)
    put("neg_slope", np.broadcast_to(-slopes, (P, HEADS)))
    end = np.arange(CMP_PAD) * 16 + 31
    token = np.arange(TILES)[None, :] * P + np.arange(P)[:, None]
    cd = (token[:, :, None] - end).astype(np.float32)
    ok = (cd >= 0) & (np.arange(CMP_PAD) < N_CMP)
    bias = np.where(ok[:, None, :, None], -slopes.reshape(1, 4, 1, 4, 1) * cd[:, None, :, None], np.float32(MASKED))
    put("cmp_bias", bias.astype(np.float32))
    put("cmp_valid", np.broadcast_to(ok[:, :, None], (P, 2, 4, CMP_PAD)).astype(np.float32))
    d = 255 - np.arange(SPAN)
    real = (d >= 0)
    onehot = (t5_bucket(np.maximum(d, 0))[None] == np.arange(32)[:, None]) & real
    count = ((d <= 128).astype(int) + (d % 4 == 0) + (d % 16 == 0)) * real
    put("onehot", (onehot & (count > 0)).astype(np.float32), 32)
    logs = np.where(count > 0, np.log(np.maximum(count, 1)), MASKED).astype(np.float32)
    put("log_count", np.broadcast_to(logs, (HEADS_A, SPAN)), HEADS_A)
    inv = 1.0 / (10000.0 ** (np.arange(0, ROPE, 2) / ROPE))
    put("inv_freq", np.broadcast_to(inv.astype(np.float32), (P, 16)))
    put("rank4", np.broadcast_to(4.0 - np.arange(4), (P, 4)))
    put("rank8", np.broadcast_to(8.0 - np.arange(8), (P, 8)))
    return t


def build_program(nc, a, out):
    import concourse.bass as bass
    from concourse import mybir
    from contextlib import ExitStack

    F32, F32R = mybir.dt.float32, mybir.dt.float32r
    ALU, ACT, AX = mybir.AluOpType, mybir.ActivationFunctionType, mybir.AxisListType
    ds = bass.ds
    ctx = ExitStack()

    def sb(name, shape, dt=F32):
        return ctx.enter_context(nc.sbuf_tensor(name, shape, dt))

    def sem(name):
        return ctx.enter_context(nc.semaphore(name))

    bank = ctx.enter_context(nc.psum_tensor("bank", [P, 8, 512], F32))
    region = -(-nc.sbuf_base // 32) * 32
    ring = sb("ring", [P, SLOTS * SLOT + PAIRS * 2 * SLOT])
    mix_at = -(-nc.sbuf_base // 32) * 32
    mix = sb("mix", [P, TILES, D_MODEL])
    toep = sb("toep", [P, HEADS_A, SPAN])
    h = sb("h", [P, TILES, D_MODEL])
    rows = sb("rows", [P, TILES, D_MODEL])
    second_at = -(-nc.sbuf_base // 32) * 32
    second = sb("second", [P, 2048])
    x_high = sb("x_high", [P, KB, TOKENS], F32R)
    arena = sb("arena", [P, 8320])
    work_at = -(-nc.sbuf_base // 32) * 32
    work = sb("work", [P, 3072])
    table = sb("table", [P, TABLE_WIDTH])
    stat = sb("stat", [P, 1400])
    zeros = sb("zeros", [P, 512])
    junk = sb("junk", [P, 768])
    eps = sb("eps", [P, 1])

    raw = ring[:, 0:RAW * UNIT].rearrange("p (s n) -> p s n", s=RAW)
    weight_parts = nc.alloc_sbuf_tensor_at("weight_parts", [P, PAIRS, 2, SLOT], F32R,
                                           offset=region + SLOTS * SLOT * 4)
    parts = nc.alloc_sbuf_tensor_at("parts", [P, 2, 2, UNIT], F32R, offset=region + RAW * UNIT * 4)
    turned_x = second[:, :].rearrange("p (k n) -> p k n", k=KB)
    x_low = nc.alloc_sbuf_tensor_at("x_low", [P, KB, TOKENS], F32R, offset=work_at + 4096)
    hid_parts = nc.alloc_sbuf_tensor_at("hid_parts", [P, 2, 2, TOKENS], F32R, offset=work_at)
    embed_high = nc.alloc_sbuf_tensor_at("embed_high", [P, 2, TOKENS], F32R, offset=second_at)
    embed_low = nc.alloc_sbuf_tensor_at("embed_low", [P, 2, TOKENS], F32R, offset=second_at + 2048)
    kv_high = nc.alloc_sbuf_tensor_at("kv_high", [P, KB, TOKENS], F32R, offset=second_at)
    kv_low = nc.alloc_sbuf_tensor_at("kv_low", [P, KB, TOKENS], F32R, offset=mix_at)
    HIGH, LOW = 0, 1

    value_banks = bank[:, 6:8, :].rearrange("p t (h x d) -> p t h x d", h=4, x=2)

    def const(name, n=P):
        at, width = TABLE[name]
        return table[0:n, at:at + width]

    ident = const("ident")
    proj = arena[:, 0:2 * 2624].rearrange("p (t n) -> p t n", t=TILES)
    qb = arena[:, 5248:6784].rearrange("p (t n) -> p t n", t=TILES)
    kb = arena[:, 6784:8320].rearrange("p (t n) -> p t n", t=TILES)
    kvb = second[:, :].rearrange("p (t n) -> p t n", t=TILES)
    moba_q = arena[:, 0:2048].rearrange("p (t n) -> p t n", t=TILES)
    moba_kv = arena[:, 2048:3072].rearrange("p (t n) -> p t n", t=TILES)
    ple_y = arena[:, 0:2048].rearrange("p (t n) -> p t n", t=TILES)
    ple_gate = arena[:, 2048:4096].rearrange("p (t n) -> p t n", t=TILES)
    ple_tmp = arena[:, 4096:6144].rearrange("p (t n) -> p t n", t=TILES)
    token_weight = arena[:, 0:EXPERTS * TOKENS].rearrange("p (e n) -> p e n", e=EXPERTS)

    gains = {}
    for name in ("norm_mix_g", "norm_ffn_g", "ln_mix0", "ln_ffn0", "ln_ple0", "kv_norm", "ln_mix1", "ln_ffn1",
                 "ln_ple1"):
        gains[name] = sb(f"gain_{name}", [P, KB])
    gain_cq, gain_ckv = sb("gain_cq", [P, 6]), sb("gain_ckv", [P, 2])
    head_gain = sb("head_gain", [64, 8])
    gain_bq, gain_bk = sb("gain_bq", [P, DIM_B]), sb("gain_bk", [P, DIM_B])
    pos_rows = sb("pos_rows", [16, 2, P])
    cmp_pos = sb("cmp_pos", [P, 2, 16])
    cmp_w2 = sb("cmp_w2", [P, 2, 2, 64])
    route_w = sb("route_w", [P, 2, KB, 36])
    route_b = sb("route_b", [P, 2, 36])
    rel = sb("rel", [32, HEADS_A])
    pos_i = sb("pos_i", [P, TILES], mybir.dt.int32)
    embed = sb("embed", [P, 2, TILES, 256])

    staged_q = junk[:, 0:768].rearrange("p (t h d) -> p t h d", t=TILES, h=4)
    staged_k = sb("staged_k", [P, TILES, 4, DIM_B])
    staged_k2 = sb("staged_k2", [P, TILES, 1, 64])
    qT = rows[0:DIM_B, 0, :].rearrange("p (h n) -> p h n", h=4)
    kT = rows[0:DIM_B, 1, :].rearrange("p (h n) -> p h n", h=4)
    kT2 = sb("kT2", [64, 1, TOKENS])
    logit = work[:, 0:1536].rearrange("p (h n) -> p h n", h=4)
    prob = work[:, 1536:3072].rearrange("p (h n) -> p h n", h=4)
    probT = sb("probT", [P, 2, SPAN])
    neg_max = sb("neg_max", [P, 4, 2])
    total = sb("total", [P, 8])
    share = sb("share", [P, 8])
    part = sb("part", [P, 8, 64])
    rope = sb("rope", [P, 8, TILES, 16])
    posf = sb("posf", [P, TILES])
    rope_tmp = mix[:, 1, 0:512].rearrange("p (x h d) -> p x h d", x=4, h=8)
    rope_k = sb("rope_k", [P, TILES, ROPE])
    bias_row = mix[0:HEADS_A, 0, 0:SPAN]
    spare = toep[:, :, :].rearrange("p h n -> p (h n)")
    blocks = spare[:, 0:1024].rearrange("p (j g n) -> p j g n", j=16, g=KV_HEADS)
    cmp_hid = spare[:, 1024:1280].rearrange("p (i c n) -> p i c n", i=2, c=2)
    cmp_kv = spare[0:CMP_PAD, 1280:1792].rearrange("p (i g d) -> p i g d", i=2, g=KV_HEADS)
    cmp_rows = spare[0:CMP_PAD, 1280:1792]
    cmp_sq = spare[0:CMP_PAD, 1792:2048].rearrange("p (g d) -> p g d", g=KV_HEADS)
    kcT = sb("kcT", [64, 64 + P - CMP_PAD])
    gates = sb("gates", [P, TILES, HEADS, 3])
    cl = sb("cl", [P, 8, CMP_PAD])
    hid_rows = spare[0:64, 2048:2560].rearrange("p (i n) -> p i n", i=2)
    cT = spare[0:CMP_PAD, 2048:3072].rearrange("p (j n) -> p j n", j=8)
    rt = sb("rt", [P, TILES, 256])
    cwT = junk[0:32, 0:TOKENS]
    cw = sb("cw", [P, TILES, EXPERTS])

    toep_dram = nc.dram_tensor("toep_dram", [HEADS_A * P * SPAN], F32).ap()
    cw_dram = nc.dram_tensor("cw_dram", [2, EXPERTS, TOKENS], F32).ap()

    x_loaded, table_loaded, small_loaded, stored = (
        sem(n) for n in ("x_loaded", "table_loaded", "small_loaded", "stored"))
    landed = [sem(f"landed{i}") for i in range(SLOTS)]
    in_landed = [sem(f"in_landed{i}") for i in range(RAW)]
    down_landed = [sem(f"down_landed{i}") for i in range(RAW)]
    weights_high, weights_split = sem("weights_high"), sem("weights_split")
    x_split, x_high_made = sem("x_split"), sem("x_high_made")
    in_high, in_split, down_high, down_split = (sem(n) for n in ("in_high", "in_split", "down_high", "down_split"))
    cleared = sem("cleared")
    squares_summed, roots_taken, rooted, rows_scaled = (
        sem(n) for n in ("squares_summed", "roots_taken", "rooted", "rows_scaled"))
    turned, act_turned, dve_turned = sem("turned"), sem("act_turned"), sem("dve_turned")
    lin_made, act_took, dve_took = sem("lin_made"), sem("act_took"), sem("dve_took")
    squared, sums_ready, scale_ready = sem("squared"), sem("sums_ready"), sem("scale_ready")
    dve_step, pool_step, mix_step = sem("dve_step"), sem("pool_step"), sem("mix_step")
    bias_row_made, bias_row_ready = sem("bias_row_made"), sem("bias_row_ready")
    gains_scaled = sem("gains_scaled")
    pos_turned, pos_ready = sem("pos_turned"), sem("pos_ready")
    toep_spread, toep_ready = sem("toep_spread"), sem("toep_ready")
    angle_ready, sines_ready, latent_ready = sem("angle_ready"), sem("sines_ready"), sem("latent_ready")
    NAMES = ("staged", "front_turned", "act_front", "dve_front", "scores_made", "biased", "maxed", "probs_made",
             "probs_turned", "probT_ready", "values_made", "mixed")
    at_sem = {n: sem(n) for n in NAMES}
    OPENED = ("front_turned", "scores_made", "biased", "mixed")
    OPEN = 2
    (staged, front_turned, act_front, dve_front, scores_made, biased, maxed, probs_made, probs_turned, probT_ready,
     values_made, mixed) = (at_sem[n] for n in NAMES)
    c_scores, c_scored, c_shifted, c_exped, c_probs, c_turned, cT_ready, c_values, c_taken = (
        sem(n) for n in ("c_scores", "c_scored", "c_shifted", "c_exped", "c_probs", "c_turned", "cT_ready",
                         "c_values", "c_taken"))
    doubled, cmp_turned, blocks_made, cmp_hid_made, gelu_done = (
        sem(n) for n in ("doubled", "cmp_turned", "blocks_made", "cmp_hid_made", "gelu_done"))
    cmp_out_made, cmp_rows_ready, kc_turned, kcT_ready, gates_ready = (
        sem(n) for n in ("cmp_out_made", "cmp_rows_ready", "kc_turned", "kcT_ready", "gates_ready"))
    blocks_cleared, hid_turned, hid_kept = sem("blocks_cleared"), sem("hid_turned"), sem("hid_kept")
    acc_cleared = sem("acc_cleared")
    logits_made, shifted, exped, cw_ready, cw_turned, cwT_ready, cw_stored, cw_spread = (
        sem(n) for n in ("logits_made", "shifted", "exped", "cw_ready", "cw_turned", "cwT_ready", "cw_stored",
                         "cw_spread"))
    hid_made, bent, hid_scaled, hid_high, hid_ready, down_made, units_added = (
        sem(n) for n in ("hid_made", "bent", "hid_scaled", "hid_high", "hid_ready", "down_made", "units_added"))
    weighted = sem("weighted")
    gated, ple_done = sem("gated"), sem("ple_done")

    chunks = []
    last_user = [None] * SLOTS
    uses = [0] * SLOTS
    next_place = [0]
    splits = []
    unit_at = []
    unit_waits = []

    def chunk(view_of, src, n_places, user):
        at = next_place[0]
        places = list(range(at, at + n_places))
        next_place[0] = (at + n_places) % SLOTS
        waits = []
        for q in places:
            if last_user[q] is not None and last_user[q] not in waits:
                waits.append(last_user[q])
            last_user[q] = user
        uses[at] += 1
        view = view_of(ring[:, at * SLOT:(at + n_places) * SLOT])
        chunks.append(dict(view=view, src=src, waits=waits, landed=(landed[at], 16 * uses[at])))
        return chunks[-1]

    def units():
        stage = len(unit_at)
        unit_at.append(len(chunks))
        per = UNIT // SLOT
        waits = [[u for u in last_user[per * q:per * (q + 1)] if u] for q in range(RAW)]
        waits[RAW - 1].append((lin_made, splits[-1]["made"]))
        unit_waits.append(waits)
        for q in range(SLOTS):
            last_user[q] = (down_split, OPEN + UNITS * (stage + 1))
        next_place[0] = 0

    lins = []
    made = [0]
    took = {"act": 0, "dve": 0}

    def took_sem(engine):
        return act_took if engine == "act" else dve_took

    def linear(w, k, n_cols, operand, dest, kind, norm=None, norm_part=0):
        jobs = []
        wide = [512] * (n_cols // 512)
        if n_cols % 512:
            rest = n_cols % 512 + (wide.pop() if n_cols % 512 < 256 else 0)
            wide += [rest] if rest <= 512 else [rest // 2, rest - rest // 2]
        c0 = 0
        for width in wide:
            group = []
            for t in range(TILES):
                engine = "dve" if kind == "add" or (kind == "copy" and t == 1) else "act"
                took[engine] += 1
                group.append(dict(m=len(lins), width=width, t=t, operand=operand, dest=dest[:, t, c0:c0 + width],
                                  kind=kind, engine=engine, took=took[engine],
                                  scale=norm and norm["parts"][norm_part][3]["scale"][:, t:t + 1],
                                  rooted=norm and norm["rooted"] + norm_part + 1))
                lins.append(group[-1])
            numbers = []
            for kp in range(0, k, 2):
                number = len(splits)
                c = chunk(lambda x: x[:, 0:2 * width].rearrange("p (k n) -> p k n", k=2),
                          w.rearrange("(p k) n -> p k n", k=k)[:, kp:kp + 2, c0:c0 + width], 1,
                          (weights_split, number + 1))
                splits.append(dict(chunk=c, width=width, made=made[0] + TILES, stage=len(unit_at)))
                numbers.append(number)
                for t, job in enumerate(group):
                    job["made"] = made[0] + t + 1
                made[0] += TILES
            for job in group:
                job["splits"] = numbers
            jobs += group
            c0 += width
        return run(jobs)

    def run(jobs):
        for job in jobs:
            job["end"] = jobs[-1]["splits"][-1]
        return jobs

    turns = []
    turn_took = {"act": 0, "dve": 0}

    def turn(source, k, dests):
        jobs = []
        view = source.rearrange("p t (c k) -> p t k c", k=k)
        for j in range(0, k, 2):
            engines = ("act", "dve") if len(dests[0]) == 3 else (("act", "dve")[len(turns) % 2],)
            counts = {}
            for engine in engines:
                turn_took[engine] += 1
                counts[engine] = turn_took[engine]
            jobs.append(dict(m=len(turns), j=j, view=view, dests=dests, counts=counts))
            turns.append(jobs[-1])
        return jobs

    roots = []
    stat_at = [0]

    def root(n, dim, n_part=P):
        w = stat_at[0]
        stat_at[0] += 6 * n
        v = [stat[0:n_part, w + i * n:w + (i + 1) * n] for i in range(6)]
        roots.append(dict(m=len(roots), sum=v[0], root=v[1], mean=v[2], tmp=v[3], first=v[4], scale=v[5], dim=dim))
        return roots[-1]

    norms = []

    def norm(sources, late=False):
        n = dict(m=len(norms), parts=[(s, d, w, root(TILES, w)) for s, d, w in sources], late=late,
                 sums=sum(len(x["parts"]) for x in norms) * TILES,
                 scaled=sum(len(x["parts"]) for x in norms if not x["late"]) * TILES,
                 rooted=sum(len(x["parts"]) for x in norms if x["late"]))
        norms.append(n)
        return n

    n_mix = norm([(h, rows, D_MODEL)], late=True)
    t_mix = turn(h, KB, [(x_high, gains["norm_mix_g"], x_low)])
    x_parts = (x_high, x_low)
    l_in = linear(a["w_in"], KB, IN_WIDTH, x_parts, proj, "copy", n_mix)
    n_lat = norm([(proj[:, :, 1536:2304], rows[:, :, 0:Q_RANK], Q_RANK),
                  (proj[:, :, 2304:2560], rows[:, :, Q_RANK:Q_RANK + KV_RANK], KV_RANK)], late=True)
    t_cq = turn(proj[:, :, 1536:2304], 6, [(x_high[:, 0:6, :], gain_cq, x_low[:, 0:6, :])])
    t_ckv = turn(proj[:, :, 2304:2560], 2, [(x_high[:, 6:8, :], gain_ckv, x_low[:, 6:8, :])])
    l_uq = linear(a["w_uq"], 6, Q_RANK, x_parts, qb, "copy", n_lat, 0)
    l_ukv = linear(a["w_ukv"], 2, 1024, (x_high[:, 6:8, :], x_low[:, 6:8, :]), kvb, "copy",
                   n_lat, 1)
    run(l_uq + l_ukv)
    r_a = root(32, DIM_A)
    r_bq = root(16, DIM_B)
    r_bk = root(16, DIM_B)
    t_mix1 = turn(mix, KB, [(x_high, None, x_low)])
    l_o = linear(a["w_o"], KB, D_MODEL, x_parts, h, "add")
    n_ffn = norm([(h, rows, D_MODEL)], late=True)
    t_ffn = turn(h, KB, [(x_high, gains["norm_ffn_g"], x_low)])

    units()

    n_nsa = norm([(h, rows, D_MODEL)], late=True)
    t_nsa = turn(h, KB, [(x_high, gains["ln_mix0"], x_low)])
    l_nsa = linear(a["a_w_in_2"][0], KB, NSA_WIDTH, x_parts, proj, "copy", n_nsa)
    next_place[0] = 0
    cmp_chunks = [chunk(lambda x: x.rearrange("p (j n) -> p j n", j=16),
                        a[w][0].rearrange("(j p) n -> p j n", p=P), 4, (cmp_hid_made, i + 1))
                  for i, w in enumerate(("a_ck_w1_2", "a_cv_w1_2"))]
    r_nsa = root(48, DIM)
    r_kc = root(4, DIM, CMP_PAD)
    t_mix2 = turn(mix, KB, [(x_high, None, x_low)])
    l_nsa_o = linear(a["a_w_out_2"][0], KB, D_MODEL, x_parts, h, "add")

    n_moe, t_moe = [None, None], [None, None]
    n_ple, t_ple, t_embed, l_embed, l_gate = ([None, None] for _ in range(5))

    def moe_and_ple(layer):
        n_moe[layer] = norm([(h, rows, D_MODEL)])
        t_moe[layer] = turn(rows, KB, [(turned_x, gains[f"ln_ffn{layer}"])])
        units()
        t_embed[layer] = turn(embed[:, layer], 2, [(embed_high, None, embed_low)])
        l_embed[layer] = linear(a["ple_w_proj_2"][layer], 2, D_MODEL, (embed_high, embed_low), ple_y, "copy")
        n_ple[layer] = norm([(h, rows, D_MODEL)], late=True)
        t_ple[layer] = turn(h, KB, [(x_high, gains[f"ln_ple{layer}"], x_low)])
        l_gate[layer] = linear(a["ple_w_gate_2"][layer], KB, D_MODEL, x_parts, ple_gate, "gate", n_ple[layer])
        run(l_embed[layer] + l_gate[layer])

    moe_and_ple(0)
    n_moba = norm([(h, rows, D_MODEL)], late=True)
    t_moba = turn(h, KB, [(x_high, gains["ln_mix1"], x_low), (kv_high, gains["kv_norm"], kv_low)])
    l_kv = linear(a["w_kv_shared_2"], KB, 512, (kv_high, kv_low), moba_kv, "copy", n_moba)
    l_q = linear(a["b_w_q_2"][0], KB, D_MODEL, x_parts, moba_q, "copy", n_moba)
    run(l_kv + l_q)
    r_moba = root(40, DIM)
    t_mix3 = turn(mix, KB, [(x_high, None, x_low)])
    l_moba_o = linear(a["b_w_out_2"][0], KB, D_MODEL, x_parts, h, "add")
    moe_and_ple(1)
    assert stat_at[0] <= 1400

    attended = {n: int(n in OPENED) for n in NAMES}
    mix_steps = [0]

    def heads(view, n, d):
        return view.rearrange("p t (h d) -> p t h d", d=d)

    def scales(r, lo, n):
        return r["scale"].rearrange("p (t h) -> p t h", t=TILES)[:, :, lo:lo + n]

    def attention(times, dim, operands, cores, mix_at, mix_per_core):
        s = dict(times=times, dim=dim, operands=operands, cores=cores, mix_at=mix_at, base=dict(attended),
                 mix_base=mix_steps[0], mix_per=sum(mix_per_core), mix_before=[sum(mix_per_core[:i]) for i in
                                                                             range(len(mix_per_core))])
        n = len(cores)
        per = dict(staged=len(operands), front_turned=len(operands),
                   act_front=sum(o["engine"] == "act" for o in operands),
                   dve_front=sum(o["engine"] == "dve" for o in operands), mixed=n)
        for name in NAMES:
            attended[name] += per.get(name, 4 * n) * times
        s["per"] = per
        mix_steps[0] += s["mix_per"] * times
        return s

    def operand(src, scale, stage, dest, n, banks, gain, engine):
        return dict(src=src, scale=scale, stage=stage, dest=dest, n=n, banks=banks, gain=gain, engine=engine)

    qa = heads(proj[:, :, 0:512], 8, 64)
    ka = heads(proj[:, :, 512:1024], 8, 64)
    att_a = attention(2, 64, [
        operand(qa, scales(r_a, 0, 8), staged_q[:, :, :, 0:64], qT, 4, (0, 1), head_gain[:, 0:1], "act"),
        operand(ka, scales(r_a, 8, 8), staged_k[:, :, :, 0:64], kT, 4, (2, 3), head_gain[:, 1:2], "dve"),
    ], [dict(kT=kT, shared=False, v=(proj, 1024, 64), bias="toep", gate=None, add=False)], 0, [1])
    att_b = attention(2, DIM_B, [
        operand(heads(qb, 8, 96), scales(r_bq, 0, 8), staged_q, qT, 4, (0, 1), None, "act"),
        operand(heads(kb, 8, 96), scales(r_bk, 0, 8), staged_k, kT, 4, (2, 3), None, "dve"),
    ], [dict(kT=kT, shared=False, v=(kvb, 64, 128), bias="causal", gate=None, add=False)], 8, [1])
    nq = heads(proj[:, :, 0:1024], 16, 64)
    nks, nkw = (heads(proj[:, :, at:at + 256], 4, 64) for at in (1536, 2048))
    att_n = attention(4, 64, [
        operand(nq, scales(r_nsa, 0, 16), staged_q[:, :, :, 0:64], qT, 4, (0, 1), head_gain[:, 2:3], "act"),
        operand(nks, scales(r_nsa, 16, 4), staged_k[:, :, 0:1, 0:64], kT, 1, (2,), head_gain[:, 4:5], "dve"),
        operand(nkw, scales(r_nsa, 20, 4), staged_k2, kT2, 1, (3,), head_gain[:, 5:6], "act"),
    ], [dict(kT=kT, shared=True, v=(proj, 1792, 64), bias="alibi", gate=1, add=True),
        dict(kT=kT2, shared=True, v=(proj, 2304, 64), bias="alibi", gate=2, add=True)], 0, [3, 3])
    mq = heads(moba_q, 16, 64)
    mk = heads(moba_kv[:, :, 0:256], 4, 64)
    att_m = attention(4, 64, [
        operand(mq, scales(r_moba, 0, 16), staged_q[:, :, :, 0:64], qT, 4, (0, 1), head_gain[:, 6:7], "act"),
        operand(mk, scales(r_moba, 16, 4), staged_k[:, :, 0:1, 0:64], kT, 1, (2,), head_gain[:, 7:8], "dve"),
    ], [dict(kT=kT, shared=True, v=(moba_kv, 256, 64), bias="alibi", gate=None, add=False)], 0, [1])

    small = []

    def load_small(dest, src):
        small.append((dest, src))

    for name, src in (("norm_ffn_g", a["norm_ffn_g"]),
                      ("ln_mix0", a["ln_mix_2"][0]), ("ln_ffn0", a["ln_ffn_2"][0]), ("ln_ple0", a["ln_ple_2"][0]),
                      ("kv_norm", a["kv_norm_2"]), ("ln_mix1", a["ln_mix_2"][1]), ("ln_ffn1", a["ln_ffn_2"][1]),
                      ("ln_ple1", a["ln_ple_2"][1])):
        load_small(gains[name][:, :], src.rearrange("(p k) -> p k", k=KB))
    load_small(gain_cq[:, :], a["cq_norm_g"].rearrange("(p k) -> p k", k=6))
    load_small(gain_ckv[:, :], a["ckv_norm_g"].rearrange("(p k) -> p k", k=2))
    for i, src in enumerate((a["qnorm_a_g"], a["knorm_a_g"], a["a_q_norm_2"][0], a["a_k_norm_2"][0, 0],
                             a["a_k_norm_2"][0, 1], a["a_k_norm_2"][0, 2], a["b_q_norm_2"][0],
                             a["k_norm_shared_2"])):
        load_small(head_gain[:, i:i + 1], src.unsqueeze(1))
    load_small(gain_bq[:, :], a["qnorm_b_g"].partition_broadcast(P))
    load_small(gain_bk[:, :], a["knorm_b_g"].partition_broadcast(P))
    for i, (pos, w2) in enumerate((("a_ck_pos_2", "a_ck_w2_2"), ("a_cv_pos_2", "a_cv_w2_2"))):
        load_small(pos_rows[:, i, :], a[pos][0].rearrange("(j l) d -> j (l d)", l=2))
        load_small(cmp_w2[:, i], a[w2][0].rearrange("(c p) n -> p c n", p=P))
    for i in range(2):
        load_small(route_w[:, i, :, 0:4], a["moe_w_group_2"][i].rearrange("(p k) n -> p k n", k=KB))
        load_small(route_w[:, i, :, 4:36], a["moe_w_expert_2"][i].rearrange("(p k) n -> p k n", k=KB))
        load_small(route_b[:, i, 0:4], a["moe_b_group_2"][i].partition_broadcast(P))
        load_small(route_b[:, i, 4:36], a["moe_b_expert_2"][i].partition_broadcast(P))
        load_small(embed[:, i], a["p_2"][i, 0].rearrange("(t p) n -> p t n", p=P))
    load_small(rel[:, :], a["rel_bias"])
    load_small(pos_i[:, :], a["positions"][0].rearrange("(t p) -> p t", p=P))

    def wait_small(eng):
        eng.wait_ge(small_loaded, 16 * len(small))

    def wait_table(eng):
        eng.wait_ge(table_loaded, 32)

    def act_norm(act, n):
        for i, (src, dest, width, r) in enumerate(n["parts"]):
            for t in range(TILES):
                nc.scalar.activation(dest[:, t, :], src[:, t, :], ACT.Square,
                                     accum_out=r["sum"][:, t:t + 1]).then_inc(squares_summed, 1)
            act.wait_ge(squares_summed, n["sums"] + TILES * (i + 1))
            act_root(act, r)

    def act_root(act, r):
        nc.scalar.activation(r["root"], r["sum"], ACT.Sqrt, scale=1.0 / r["dim"],
                             bias=eps[0:r["sum"].shape[0], 0:1]).then_inc(roots_taken, 1)

    dve_steps = [0]

    def dve_link(dve, ins):
        dve_steps[0] += 1
        ins.then_inc(dve_step, 1)
        dve.wait_ge(dve_step, dve_steps[0])

    def dve_root(dve, r, signal=None):
        dve.wait_ge(roots_taken, r["m"] + 1)
        dve_link(dve, nc.vector.reciprocal(r["first"], r["root"]))
        dve_link(dve, nc.vector.tensor_scalar(r["mean"], r["sum"], 1.0 / r["dim"], EPS, ALU.mult, ALU.add))
        dve_link(dve, nc.vector.tensor_tensor(r["tmp"], r["first"], r["first"], ALU.mult))
        dve_link(dve, nc.vector.tensor_tensor(r["mean"], r["tmp"], r["mean"], ALU.mult))
        dve_link(dve, nc.vector.tensor_scalar(r["tmp"], r["mean"], -0.5, 1.5, ALU.mult, ALU.add))
        last = nc.vector.tensor_tensor(r["scale"], r["first"], r["tmp"], ALU.mult)
        if signal is None:
            dve_link(dve, last)
        else:
            last.then_inc(signal, 1)

    def dve_norm(dve, n):
        for i, (src, dest, _, r) in enumerate(n["parts"]):
            dve_root(dve, r, rooted if n["late"] else None)
            if n["late"]:
                continue
            for t in range(TILES):
                nc.vector.tensor_scalar(dest[:, t, :], src[:, t, :], r["scale"][:, t:t + 1], None,
                                        ALU.mult).then_inc(rows_scaled, 1)

    def pe_turn(pe, jobs):
        for j in jobs:
            if j["m"] >= 4:
                before = turns[j["m"] - 4]["counts"]
                last = "dve" if "dve" in before else "act"
                pe.wait_ge(dve_turned if last == "dve" else act_turned, before[last])
            b = 4 + j["m"] % 4
            for kk in range(2):
                for t in range(TILES):
                    mm = nc.tensor.transpose(bank[:, b, kk * 256 + t * P:kk * 256 + (t + 1) * P],
                                             j["view"][:, t, j["j"] + kk, :], ident)
            mm.then_inc(turned, 1)

    def take_turn(eng, jobs, engine):
        for j in jobs:
            if engine not in j["counts"]:
                continue
            eng.wait_ge(turned, j["m"] + 1)
            b = 4 + j["m"] % 4
            split = len(j["dests"][0]) == 3
            if split and engine == "dve":
                eng.wait_ge(act_turned, j["counts"]["act"])
            for d in j["dests"]:
                dest, gain = d[0], d[1]
                if gain is None:
                    src = bank[:, b, :].rearrange("p (k n) -> p k n", k=2)
                    to = dest[:, j["j"]:j["j"] + 2, :]
                    if engine == "act":
                        last = nc.scalar.copy(to, src)
                    elif split:
                        last = nc.vector.tensor_tensor(d[2][:, j["j"]:j["j"] + 2, :], src, to, ALU.subtract)
                    else:
                        last = nc.vector.tensor_copy(to, src)
                    continue
                for kk in range(2):
                    k = j["j"] + kk
                    src = bank[:, b, kk * 256:kk * 256 + 256]
                    if engine == "act":
                        last = nc.scalar.activation(dest[:, k, :], src, ACT.Copy, scale=gain[:, k:k + 1])
                    elif split:
                        last = nc.vector.scalar_tensor_tensor(out=d[2][:, k, :], in0=src, scalar=gain[:, k:k + 1],
                                                              in1=dest[:, k, :], op0=ALU.mult, op1=ALU.subtract)
                    else:
                        last = nc.vector.tensor_scalar(dest[:, k, :], src, gain[:, k:k + 1], None, ALU.mult)
            last.then_inc(act_turned if engine == "act" else dve_turned, 1)

    def wait_turned(eng, jobs):
        for engine, s in (("act", act_turned), ("dve", dve_turned)):
            n = max((j["counts"].get(engine, 0) for j in jobs), default=0)
            if n:
                eng.wait_ge(s, n)

    def pe_linear(pe, jobs):
        for group in zip(jobs[0::2], jobs[1::2]):
            for c, number in enumerate(group[0]["splits"]):
                pe.wait_ge(weights_split, number + 1)
                for j in group:
                    if c == 0 and j["m"] >= 4:
                        before = lins[j["m"] - 4]
                        pe.wait_ge(took_sem(before["engine"]), before["took"])
                    n = j["width"]
                    at = (j["t"] * P, (j["t"] + 1) * P)
                    for kk in range(2):
                        for i, (x, w) in enumerate(((HIGH, HIGH), (HIGH, LOW), (LOW, HIGH))):
                            mm = nc.tensor.matmul(bank[:, j["m"] % 4, 0:n], j["operand"][x][:, 2 * c + kk, at[0]:at[1]],
                                                  weight_parts[:, number % PAIRS, w, kk * n:(kk + 1) * n],
                                                  start=c == kk == i == 0,
                                                  stop=c == len(j["splits"]) - 1 and kk == 1 and i == 2)
                    mm.then_inc(lin_made, 1)

    def split(eng, number, engine):
        x = splits[number]
        n = 2 * x["width"]
        raw_weights = x["chunk"]["view"].rearrange("p k n -> p (k n)")
        high, low = (weight_parts[:, number % PAIRS, w, 0:n] for w in (HIGH, LOW))
        if engine == "act":
            eng.wait_ge(*x["chunk"]["landed"])
            if number >= PAIRS:
                eng.wait_ge(lin_made, splits[number - PAIRS]["made"])
            if x["stage"] and (number < PAIRS or splits[number - PAIRS]["stage"] < x["stage"]):
                eng.wait_ge(down_made, OPEN + UNITS * x["stage"])
            nc.scalar.copy(high, raw_weights).then_inc(weights_high, 1)
        else:
            eng.wait_ge(weights_high, number + 1)
            nc.vector.tensor_tensor(low, raw_weights, high, ALU.subtract).then_inc(weights_split, 1)

    def split_first(eng, jobs, engine, lo=0, hi=PAIRS):
        first = jobs[0]["splits"][0]
        for number in range(first + lo, min(first + hi, jobs[0]["end"] + 1)):
            split(eng, number, engine)

    def take_linear(eng, jobs, engine):
        for group in zip(jobs[0::2], jobs[1::2]):
            for number in group[0]["splits"]:
                if number + PAIRS <= group[0]["end"]:
                    split(eng, number + PAIRS, engine)
            for j in group:
                if j["engine"] != engine:
                    continue
                eng.wait_ge(lin_made, j["made"])
                if j["rooted"]:
                    eng.wait_ge(rooted, j["rooted"])
                src = bank[:, j["m"] % 4, 0:j["width"]]
                if j["kind"] == "add":
                    nc.vector.tensor_tensor(j["dest"], j["dest"], src, ALU.add).then_inc(dve_took, 1)
                elif j["kind"] == "gate":
                    nc.scalar.activation(j["dest"], src, ACT.Sigmoid, scale=j["scale"]).then_inc(act_took, 1)
                elif j["rooted"] and engine == "act":
                    nc.scalar.activation(j["dest"], src, ACT.Copy, scale=j["scale"]).then_inc(act_took, 1)
                elif j["rooted"]:
                    nc.vector.tensor_scalar(j["dest"], src, j["scale"], None, ALU.mult).then_inc(dve_took, 1)
                elif engine == "act":
                    nc.scalar.copy(j["dest"], src).then_inc(act_took, 1)
                else:
                    nc.vector.tensor_copy(j["dest"], src).then_inc(dve_took, 1)

    def wait_took(eng, jobs):
        for engine in ("act", "dve"):
            n = max((j["took"] for j in jobs if j["engine"] == engine), default=0)
            if n:
                eng.wait_ge(took_sem(engine), n)

    def pool_attention(pool, s):
        b, n_op = s["base"], len(s["operands"])
        with pool.Fori(0, s["times"]) as i:
            for o, x in enumerate(s["operands"]):
                pool.wait_ge(front_turned, b["front_turned"] + i * n_op)
                for t in range(TILES):
                    last = nc.gpsimd.tensor_tensor(
                        x["stage"][:, t], x["src"][:, t, ds(i * x["n"], x["n"]), :],
                        x["scale"][:, t, ds(i * x["n"], x["n"])].unsqueeze(2).to_broadcast([P, x["n"], s["dim"]]),
                        ALU.mult)
                last.then_inc(staged, 1)

    def pe_attention(pe, s, compressed=False):
        b, n_op, n_core, d = s["base"], len(s["operands"]), len(s["cores"]), s["dim"]
        with pe.Fori(0, s["times"]) as i:
            pe.wait_ge(biased, b["biased"] + i * (4 * n_core))
            for o, x in enumerate(s["operands"]):
                pe.wait_ge(staged, b["staged"] + i * n_op + (o + 1))
                for r in range(x["n"]):
                    for t in range(TILES):
                        to = bank[0:d, x["banks"][r // 2], (r % 2) * 256 + t * P:(r % 2) * 256 + (t + 1) * P]
                        if r == t == 0:
                            mm = nc.tensor.matmul(to, x["stage"][:, t, r, :], ident, start=True, stop=True)
                        else:
                            mm = nc.tensor.transpose(to, x["stage"][:, t, r, :], ident)
                mm.then_inc(front_turned, 1)
            pe.wait_ge(act_front, b["act_front"] + (i + 1) * s["per"]["act_front"])
            pe.wait_ge(dve_front, b["dve_front"] + (i + 1) * s["per"]["dve_front"])
            if compressed:
                pe_compressed(pe, i, b)
            for c, core in enumerate(s["cores"]):
                n0 = i * (4 * n_core) + 4 * c
                for r in range(4):
                    if c:
                        pe.wait_ge(biased, b["biased"] + n0 + (r - 3))
                    kr = 0 if core["shared"] else r
                    nc.tensor.matmul(bank[:, r, 0:P], qT[0:d, r, 0:P], core["kT"][0:d, kr, 0:P], start=True, stop=True)
                    nc.tensor.matmul(bank[:, r, P:SPAN], qT[0:d, r, P:2 * P], core["kT"][0:d, kr, :],
                                     start=True, stop=True).then_inc(scores_made, 1)

                def turn_probs(r):
                    pe.wait_ge(probs_made, b["probs_made"] + n0 + (r + 1))
                    if r >= 2:
                        pe.wait_ge(probT_ready, b["probT_ready"] + n0 + (r - 1))
                    for q in range(3):
                        mm = nc.tensor.transpose(bank[:, 4 + r % 2, q * P:(q + 1) * P],
                                                 prob[:, r, q * P:(q + 1) * P], ident)
                    mm.then_inc(probs_turned, 1)

                def values(r):
                    pe.wait_ge(probT_ready, b["probT_ready"] + n0 + (r + 1))
                    if r == 0:
                        pe.wait_ge(mixed, b["mixed"] + i * n_core + c)
                    v, v_at, pitch = core["v"]
                    at = i * pitch + (v_at - 64) if core["shared"] else i * (4 * pitch) + (v_at - 64 + r * pitch)
                    for t, q, kt, start, stop in ((0, 0, 0, True, True), (1, 1, 0, True, False), (1, 2, 1, False, True)):
                        mm = nc.tensor.matmul(bank[:, 6 + t, r * P:(r + 1) * P],
                                              probT[:, r % 2, q * P:(q + 1) * P], v[:, kt, ds(at, P)],
                                              start=start, stop=stop)
                    mm.then_inc(values_made, 1)

                for r in range(4):
                    turn_probs(r)
                    if r:
                        values(r - 1)
                values(3)

    def act_attention(act, s, compressed=False):
        b, n_core, d = s["base"], len(s["cores"]), s["dim"]
        mine = [(o, x) for o, x in enumerate(s["operands"]) if x["engine"] == "act"]
        with act.Fori(0, s["times"]) as i:
            act.wait_ge(scores_made, b["scores_made"] + i * (4 * n_core))
            for o, x in mine:
                take_front(act, x, i, s, o)
            if compressed:
                act_compressed(act, i)
            for c in range(n_core):
                n0 = i * (4 * n_core) + 4 * c

                def exps(r):
                    act.wait_ge(maxed, b["maxed"] + n0 + (r + 1))
                    for t, (lo, hi) in enumerate(((0, P), (P, SPAN))):
                        last = nc.scalar.activation(prob[:, r, lo:hi], logit[:, r, lo:hi], ACT.Exp,
                                                    bias=neg_max[:, r, t:t + 1],
                                                    accum_out=total[:, t * 4 + r:t * 4 + r + 1])
                    last.then_inc(probs_made, 1)

                def take_probs(r):
                    act.wait_ge(probs_turned, b["probs_turned"] + n0 + (r + 1))
                    if r >= 2:
                        act.wait_ge(values_made, b["values_made"] + n0 + (r - 1))
                    nc.scalar.copy(probT[:, r % 2, :], bank[:, 4 + r % 2, 0:SPAN]).then_inc(probT_ready, 1)

                exps(0)
                for r in range(1, 4):
                    exps(r)
                    take_probs(r - 1)
                take_probs(3)

    def take_front(eng, x, i, s, o):
        d, b = s["dim"], s["base"]
        eng.wait_ge(front_turned, b["front_turned"] + i * len(s["operands"]) + (o + 1))
        for n, bk in enumerate(x["banks"]):
            heads_here = min(2, x["n"] - 2 * n)
            src = bank[0:d, bk, 0:heads_here * 256]
            to = x["dest"][0:d, 2 * n:2 * n + heads_here, :].rearrange("p h n -> p (h n)")
            if x["engine"] == "act":
                if x["gain"] is None:
                    last = nc.scalar.copy(to, src)
                else:
                    last = nc.scalar.activation(to, src, ACT.Copy, scale=x["gain"])
            elif x["gain"] is None:
                last = nc.vector.tensor_copy(to, src)
            else:
                last = nc.vector.tensor_scalar(to, src, x["gain"], None, ALU.mult)
        last.then_inc(act_front if x["engine"] == "act" else dve_front, 1)

    def dve_attention(dve, s, compressed=False):
        b, n_core, d = s["base"], len(s["cores"]), s["dim"]
        with dve.Fori(0, s["times"]) as i:
            dve.wait_ge(scores_made, b["scores_made"] + i * (4 * n_core))
            for o, x in enumerate(s["operands"]):
                if x["engine"] == "dve":
                    take_front(dve, x, i, s, o)
            if compressed:
                dve_compressed(dve, i)
            for c, core in enumerate(s["cores"]):
                n0 = i * (4 * n_core) + 4 * c
                for r in range(4):
                    dve.wait_ge(scores_made, b["scores_made"] + n0 + (r + 1))
                    src = bank[:, r, 0:SPAN]
                    if core["bias"] == "toep":
                        ins = nc.vector.scalar_tensor_tensor(out=logit[:, r, :], in0=src, scalar=DIM_A ** -0.5,
                                                             in1=toep[:, i * 4 + r, :], op0=ALU.mult, op1=ALU.add)
                    elif core["bias"] == "causal":
                        ins = nc.vector.scalar_tensor_tensor(out=logit[:, r, :], in0=src, scalar=DIM_B ** -0.5,
                                                             in1=const("causal"), op0=ALU.mult, op1=ALU.add)
                    else:
                        ins = nc.vector.scalar_tensor_tensor(out=logit[:, r, :], in0=const("dist"),
                                                             scalar=const("neg_slope")[:, ds(i * 4 + r, 1)], in1=src,
                                                             op0=ALU.mult, op1=ALU.add)
                    ins.then_inc(biased, 1)
                    dve.wait_ge(biased, b["biased"] + n0 + (r + 1))
                    nc.vector.tensor_reduce(neg_max[:, r, 0:1], logit[:, r, 0:P], AX.X, ALU.max, negate=True)
                    nc.vector.tensor_reduce(neg_max[:, r, 1:2], logit[:, r, P:SPAN], AX.X, ALU.max,
                                            negate=True).then_inc(maxed, 1)
                step = s["mix_base"] + i * s["mix_per"] + s["mix_before"][c]
                dve.wait_ge(values_made, b["values_made"] + n0 + 4)
                nc.vector.reciprocal(share[:, :], total[:, :]).then_inc(mix_step, 1)
                dve.wait_ge(mix_step, step + 1)
                here = mix.rearrange("p t (h d) -> p t h d", d=64)[:, :, ds(i * 4 + s["mix_at"], 4), :]
                values = value_banks[:, :, :, 1, :]
                share4 = share[:, :].rearrange("p (t h) -> p t h", t=TILES)
                shares = share4.unsqueeze(3).to_broadcast([P, TILES, 4, 64])
                if core["gate"] is None:
                    nc.vector.tensor_tensor(here, values, shares, ALU.mult).then_inc(mixed, 1)
                else:
                    nc.vector.tensor_tensor(share4, share4, gates[:, :, ds(i * 4, 4), core["gate"]],
                                            ALU.mult).then_inc(mix_step, 1)
                    dve.wait_ge(mix_step, step + 2)
                    nc.vector.tensor_tensor(part[:, :, :].rearrange("p (t h) d -> p t h d", t=TILES), values, shares,
                                            ALU.mult).then_inc(mixed, 1)
                    dve.wait_ge(mixed, b["mixed"] + i * n_core + (c + 1))
                    nc.vector.tensor_tensor(here, here, part[:, :, :].rearrange("p (t h) d -> p t h d", t=TILES),
                                            ALU.add).then_inc(mix_step, 1)
                    dve.wait_ge(mix_step, step + 3)

    def pe_compressed(pe, i, b):
        pe.wait_ge(mixed, b["mixed"] + i * 2)
        for t in range(TILES):
            for r in range(4):
                mm = nc.tensor.matmul(bank[:, 6 + t, r * P:(r + 1) * P], qT[0:64, r, t * P:(t + 1) * P],
                                      kcT[0:64, ds(i * CMP_PAD, P)], start=True, stop=True)
        mm.then_inc(c_scores, 1)
        pe.wait_ge(c_probs, i + 1)
        for j in range(8):
            mm = nc.tensor.transpose(bank[0:CMP_PAD, 4 + j // 4, (j % 4) * P:(j % 4 + 1) * P], cl[:, j, :], ident)
        mm.then_inc(c_turned, 1)
        pe.wait_ge(cT_ready, i + 1)
        for j in range(8):
            mm = nc.tensor.matmul(bank[:, 6 + j // 4, (j % 4) * P:(j % 4 + 1) * P], cT[:, j, :],
                                  cmp_rows[:, ds(i * 64 + 192, P)], start=True, stop=True)
        mm.then_inc(c_values, 1)
        pe.wait_ge(c_taken, i + 1)

    def act_compressed(act, i):
        act.wait_ge(c_shifted, i + 1)
        nc.scalar.activation(cl[:, :, :], cl[:, :, :], ACT.Exp).then_inc(c_exped, 1)
        act.wait_ge(c_turned, i + 1)
        nc.scalar.copy(cT[:, 0:4, :].rearrange("p j n -> p (j n)"), bank[0:CMP_PAD, 4, :])
        nc.scalar.copy(cT[:, 4:8, :].rearrange("p j n -> p (j n)"), bank[0:CMP_PAD, 5, :]).then_inc(cT_ready, 1)

    c_steps = sem("c_steps")

    def dve_compressed(dve, i):
        n = [0]

        def link(ins):
            n[0] += 1
            ins.then_inc(c_steps, 1)
            dve.wait_ge(c_steps, i * 6 + n[0])

        dve.wait_ge(c_scores, i + 1)
        nc.vector.tensor_tensor(cl[:, :, :].rearrange("p (t r) n -> p t r n", t=TILES),
                                bank[:, 6:8, :].rearrange("p t (r n) -> p t r n", r=4)[:, :, :, 0:CMP_PAD],
                                const("cmp_bias").rearrange("p (g t r n) -> p g t r n", g=4, t=2, r=4)[:, i],
                                ALU.add).then_inc(c_scored, 1)
        dve.wait_ge(c_scored, i + (OPEN + 1))
        link(nc.vector.tensor_reduce(share[:, :], cl[:, :, :], AX.X, ALU.max))
        nc.vector.tensor_tensor(cl[:, :, :], cl[:, :, :], share[:, :].unsqueeze(2).to_broadcast([P, 8, CMP_PAD]),
                                ALU.subtract).then_inc(c_shifted, 1)
        dve.wait_ge(c_exped, i + 1)
        nc.vector.tensor_tensor(cl[:, :, :].rearrange("p j n -> p (j n)"), cl[:, :, :].rearrange("p j n -> p (j n)"),
                                const("cmp_valid"), ALU.mult).then_inc(c_probs, 1)
        dve.wait_ge(c_probs, i + 1)
        link(nc.vector.tensor_reduce(share[:, :], cl[:, :, :], AX.X, ALU.add))
        link(nc.vector.tensor_scalar(share[:, :], share[:, :], 1e-30, None, ALU.max))
        link(nc.vector.reciprocal(share[:, :], share[:, :]))
        share4 = share[:, :].rearrange("p (t h) -> p t h", t=TILES)
        link(nc.vector.tensor_tensor(share4, share4, gates[:, :, ds(i * 4, 4), 0], ALU.mult))
        dve.wait_ge(c_values, i + 1)
        here = mix.rearrange("p t (h d) -> p t h d", d=64)[:, :, ds(i * 4, 4), :]
        nc.vector.tensor_tensor(here, value_banks[:, :, :, 1, :],
                                share4.unsqueeze(3).to_broadcast([P, TILES, 4, 64]), ALU.mult).then_inc(c_taken, 1)
        dve.wait_ge(c_taken, i + 1)
        link(nc.vector.memset(part[:, 0, 0:1], 0.0))

    def pe_clear(pe, n):
        for q in range(4):
            mm = nc.tensor.matmul(bank[:, q, :], zeros[0:32, 0:P], zeros[0:32, :], start=True, stop=False,
                                  skip_group_check=True)
        mm.then_inc(acc_cleared, 1)

    def in_width(s):
        return 1024 if s == 0 else 2048

    def unit_slot(u):
        return u % RAW, u // RAW + 1

    def in_landed_at(s, u):
        place_of, uses = unit_slot(u)
        per_stage = (UNITS - place_of + RAW - 1) // RAW
        return sum(per_stage * in_width(q) // 64 for q in range(s)) + uses * in_width(s) // 64

    def down_landed_at(s, u):
        place_of, uses = unit_slot(u)
        return 16 * (s * ((UNITS - place_of + RAW - 1) // RAW) + uses)

    def sp_units(sp, s):
        if s == 0:
            w_in = [a["w_ff1"].rearrange("(p k) (u n) -> p u k n", k=KB, n=P)]
            w_down = a["w_ff2"].rearrange("(u p) n -> p u n", p=P)
        else:
            w_in = [a[w][s - 1].rearrange("e (p k) f -> p e k f", k=KB) for w in ("moe_w_gate_2", "moe_w_up_2")]
            w_down = a["moe_w_down_2"][s - 1].rearrange("e p n -> p e n")

        def load_in(at, u):
            for q, w in enumerate(w_in):
                sp.dma_start(raw[:, at, q * 1024:(q + 1) * 1024].rearrange("p (k n) -> p k n", k=KB),
                             w[:, u]).then_inc(in_landed[at], 16)

        def load_down(at, u):
            sp.dma_start(raw[:, at, 2048:3072], w_down[:, u, :]).then_inc(down_landed[at], 16)

        def free_slot(at):
            for wait in unit_waits[s][at]:
                sp.wait_ge(*wait)

        for at in range(RAW):
            free_slot(at)
            load_in(at, at)
            if at < RAW - 1:
                load_down(at, at)
        with sp.Fori(0, 9) as i:
            for u in range(RAW):
                sp.wait_ge(in_split, UNITS * s + u + 1 + i * RAW)
                load_in(u, i * RAW + (u + RAW))
                sp.wait_ge(down_split, OPEN + UNITS * s + u + i * RAW)
                load_down((u + 2) % RAW, i * RAW + (u + 2))
        for u in (27, 28):
            sp.wait_ge(in_split, UNITS * s + u + 1)
            load_in(u % RAW, u + RAW)
            sp.wait_ge(down_split, OPEN + UNITS * s + u)
            load_down((u + 2) % RAW, u + 2)
        sp.wait_ge(down_split, OPEN + UNITS * s + 29)
        load_down(31 % RAW, 31)

    BODY, ROUNDS = 6, 5

    def step_in(s):
        return BODY // RAW * in_width(s) // 64, BODY // RAW * 16

    def pe_in(pe, s, u, i=0):
        b = 4 + u % 2
        pe.wait_ge(in_split, UNITS * s + u + 1 + i * BODY)
        if u >= 2:
            pe.wait_ge(hid_scaled, UNITS * s + u - 1 + i * BODY)
        for q in range(in_width(s) // 1024):
            for k in range(KB):
                for n, (w, x) in enumerate(((HIGH, x_high), (HIGH, x_low), (LOW, x_high))):
                    mm = nc.tensor.matmul(bank[:, b, q * 256:(q + 1) * 256],
                                          parts[:, u % 2, w, q * 1024 + k * P:q * 1024 + (k + 1) * P], x[:, k, :],
                                          start=k == 0 and n == 0, stop=k == KB - 1 and n == 2)
        mm.then_inc(hid_made, 1)

    def pe_down(pe, s, u, i=0):
        pe.wait_ge(down_split, OPEN + UNITS * s + u + 1 + i * BODY)
        pe.wait_ge(hid_ready, UNITS * s + u + 1 + i * BODY)
        for t in range(TILES):
            for x, w in ((HIGH, HIGH), (HIGH, LOW), (LOW, HIGH)):
                for half in range(2):
                    mm = nc.tensor.matmul(bank[:, 2 * t + half, :], hid_parts[:, u % 2, x, t * P:(t + 1) * P],
                                          parts[:, u % 2, w, 2048 + half * 512:2048 + (half + 1) * 512],
                                          start=False, stop=False, skip_group_check=True)
        mm.then_inc(down_made, 1)

    def pe_units(pe, s):
        with pe.Fori(0, ROUNDS) as i:
            for u in range(BODY):
                pe_in(pe, s, u + 1, i)
                pe_down(pe, s, u, i)
        for u in range(ROUNDS * BODY, UNITS):
            if u + 1 < UNITS:
                pe_in(pe, s, u + 1)
            pe_down(pe, s, u)

    def bent_rows(u):
        return junk[:, 256 + (u % 2) * 256:512 + (u % 2) * 256]

    def act_high_in(act, s, u, i=0):
        act.wait_ge(in_landed[u % RAW], in_landed_at(s, u) + i * step_in(s)[0])
        nc.scalar.copy(parts[:, u % 2, HIGH, 0:in_width(s)], raw[:, u % RAW, 0:in_width(s)]).then_inc(in_high, 1)

    def act_high_down(act, s, u, i=0):
        act.wait_ge(down_landed[u % RAW], down_landed_at(s, u) + i * step_in(s)[1])
        act.wait_ge(down_made, OPEN + UNITS * s + u - 1 + i * BODY)
        nc.scalar.copy(parts[:, u % 2, HIGH, 2048:3072], raw[:, u % RAW, 2048:3072]).then_inc(down_high, 1)

    def act_first_units(act, s):
        act_high_in(act, s, 0)
        act_high_down(act, s, 0)
        act_high_in(act, s, 1)

    def act_units(act, s):
        def step(u, i=0, last=UNITS):
            act.wait_ge(hid_made, UNITS * s + u + 1 + i * BODY)
            nc.scalar.activation(bent_rows(u), bank[:, 4 + u % 2, 0:256],
                                 ACT.Relu if s == 0 else ACT.Silu).then_inc(bent, 1)
            if u + 2 < last:
                act_high_in(act, s, u + 2, i)
            if u + 1 < last:
                act_high_down(act, s, u + 1, i)

        with act.Fori(0, ROUNDS) as i:
            for u in range(BODY):
                step(u, i)
        for u in range(ROUNDS * BODY, UNITS):
            step(u)

    def dve_low_in(dve, s, u, i=0):
        dve.wait_ge(in_high, UNITS * s + u + 1 + i * BODY)
        n = in_width(s)
        nc.vector.tensor_tensor(parts[:, u % 2, LOW, 0:n], raw[:, u % RAW, 0:n], parts[:, u % 2, HIGH, 0:n],
                                ALU.subtract).then_inc(in_split, 1)

    def dve_low_down(dve, s, u, i=0):
        dve.wait_ge(down_high, UNITS * s + u + 1 + i * BODY)
        nc.vector.tensor_tensor(parts[:, u % 2, LOW, 2048:3072], raw[:, u % RAW, 2048:3072],
                                parts[:, u % 2, HIGH, 2048:3072], ALU.subtract).then_inc(down_split, 1)

    def dve_first_units(dve, s):
        dve_low_in(dve, s, 0)
        dve_low_down(dve, s, 0)
        dve_low_in(dve, s, 1)

    def dve_units(dve, s):
        def step(u, i=0):
            dve.wait_ge(bent, UNITS * s + u + 1 + i * BODY)
            rows_here = bent_rows(u)
            if s == 0:
                nc.vector.tensor_tensor(rows_here, rows_here, rows_here, ALU.mult).then_inc(hid_scaled, 1)
                dve.wait_ge(hid_scaled, UNITS * s + u + 1 + i * BODY)
            else:
                if isinstance(i, int) or u % 2 == 0:
                    dve.wait_ge(cw_spread, 16 * (UNITS // 2 * (s - 1) + u // 2 + 1) + i * (16 * BODY // 2))
                nc.vector.tensor_tensor(rows_here, rows_here, bank[:, 4 + u % 2, 256:512],
                                        ALU.mult).then_inc(hid_scaled, 1)
                dve.wait_ge(hid_scaled, UNITS * s + u + 1 + i * BODY)
                dve_scaled = nc.vector.tensor_tensor(rows_here, rows_here, token_weight[:, i * BODY + u, :], ALU.mult)
                dve_scaled.then_inc(weighted, 1)
                dve.wait_ge(weighted, UNITS * (s - 1) + u + 1 + i * BODY)
            dve.wait_ge(down_made, OPEN + UNITS * s + u - 1 + i * BODY)
            nc.vector.tensor_copy(hid_parts[:, u % 2, HIGH, :], rows_here).then_inc(hid_high, 1)
            dve.wait_ge(hid_high, UNITS * s + u + 1 + i * BODY)
            nc.vector.tensor_tensor(hid_parts[:, u % 2, LOW, :], rows_here, hid_parts[:, u % 2, HIGH, :],
                                    ALU.subtract).then_inc(hid_ready, 1)
            if u + 2 < UNITS:
                dve_low_in(dve, s, u + 2, i)
            if u + 1 < UNITS:
                dve_low_down(dve, s, u + 1, i)

        with dve.Fori(0, ROUNDS) as i:
            for u in range(BODY):
                step(u, i)
        for u in range(ROUNDS * BODY, UNITS):
            step(u)
        scale = None
        if s == 0:
            r = n_ffn["parts"][0][3]
            dve.wait_ge(rooted, n_ffn["rooted"] + 1)
            dve_link(dve, nc.vector.tensor_tensor(r["mean"], r["scale"], r["scale"], ALU.mult))
            scale = r["mean"]
        dve.wait_ge(down_made, OPEN + UNITS * (s + 1))
        for t in range(TILES):
            for half in range(2):
                cols = h[:, t, half * 512:(half + 1) * 512]
                if scale is None:
                    ins = nc.vector.tensor_tensor(cols, cols, bank[:, 2 * t + half, :], ALU.add)
                else:
                    ins = nc.vector.scalar_tensor_tensor(out=cols, in0=bank[:, 2 * t + half, :],
                                                         scalar=scale[:, t:t + 1], in1=cols, op0=ALU.mult, op1=ALU.add)
                ins.then_inc(units_added, 1)

    def wait_units_added(eng, s):
        eng.wait_ge(units_added, 4 * (s + 1))

    def act_split_rows(act, jobs, s):
        wait_turned(act, jobs)
        nc.scalar.copy(x_high[:, :, :], turned_x[:, :, :]).then_inc(x_high_made, 1)

    def dve_split_rows(dve, s):
        dve.wait_ge(x_high_made, s)
        nc.vector.tensor_tensor(x_low[:, :, :], turned_x[:, :, :], x_high[:, :, :], ALU.subtract).then_inc(x_split, 1)

    def pool_spread(pool, layer):
        pool.wait_ge(cwT_ready, layer + 1)
        pool.dma_start(cw_dram[layer], cwT[:, :]).then_inc(cw_stored, 16)
        pool.wait_ge(cw_stored, 16 * (layer + 1))
        src = cw_dram[layer].rearrange("e n -> (e n)")
        with pool.Fori(0, EXPERTS // 2) as i:
            pool.dma_start(arena[:, ds(i * (2 * TOKENS), 2 * TOKENS)],
                           src[ds(i * (2 * TOKENS), 2 * TOKENS)].partition_broadcast(P)).then_inc(cw_spread, 16)
            pool.wait_ge(cw_spread, 16 * (EXPERTS // 2 * layer + 1) + i * 16)

    def pe_route(pe, layer):
        for t in range(TILES):
            for k in range(KB):
                mm = nc.tensor.matmul(bank[:, 6, t * 64:t * 64 + 36], turned_x[:, k, t * P:(t + 1) * P],
                                      route_w[:, layer, k, :], start=k == 0, stop=k == KB - 1)
        mm.then_inc(logits_made, 1)

    def pe_turn_weights(pe, layer):
        pe.wait_ge(cw_ready, layer + 1)
        for t in range(TILES):
            mm = nc.tensor.transpose(bank[0:32, 7, t * P:(t + 1) * P], cw[:, t, :], ident)
        mm.then_inc(cw_turned, 1)

    def act_route(act, layer):
        for q, (lo, hi) in enumerate(((40, 44), (48, 56))):
            act.wait_ge(shifted, 2 * layer + q + 1)
            nc.scalar.activation(rt[:, :, lo + 20:hi + 20], rt[:, :, lo:hi], ACT.Exp).then_inc(exped, 1)
        act.wait_ge(cw_turned, layer + 1)
        nc.scalar.copy(cwT[:, :], bank[0:32, 7, 0:256]).then_inc(cwT_ready, 1)

    def dve_route(dve, layer):
        v = nc.vector

        def link(ins):
            dve_link(dve, ins)

        def c1(at):
            return rt[:, :, at]

        def wide(x, n):
            return x.unsqueeze(2).to_broadcast([P, TILES, n])

        dve.wait_ge(logits_made, layer + 1)
        link(v.tensor_tensor(rt[:, :, 0:36], bank[:, 6, 0:128].rearrange("p (t n) -> p t n", t=TILES)[:, :, 0:36],
                             route_b[:, layer, :].unsqueeze(1).to_broadcast([P, TILES, 36]), ALU.add))
        link(v.tensor_reduce(c1(36), rt[:, :, 0:4], AX.X, ALU.max))
        v.tensor_tensor(rt[:, :, 40:44], rt[:, :, 0:4], wide(c1(36), 4), ALU.subtract).then_inc(shifted, 1)
        dve.wait_ge(exped, 2 * layer + 1)
        group_p = rt[:, :, 60:64]
        link(v.tensor_reduce(c1(37), group_p, AX.X, ALU.add))
        link(v.reciprocal(c1(38), c1(37)))

        def first_best(values, best, n, rank, out_at, tmp_at):
            tmp, hot = rt[:, :, tmp_at:tmp_at + n], rt[:, :, out_at:out_at + n]
            link(v.tensor_tensor(tmp, values, wide(best, n), ALU.is_equal))
            link(v.tensor_tensor(tmp, tmp, rank.unsqueeze(1).to_broadcast([P, TILES, n]), ALU.mult))
            link(v.tensor_reduce(c1(39), tmp, AX.X, ALU.max))
            link(v.tensor_tensor(hot, tmp, wide(c1(39), n), ALU.is_equal))
            return hot

        link(v.tensor_reduce(c1(45), group_p, AX.X, ALU.max))
        group_hot = first_best(group_p, c1(45), 4, const("rank4"), 80, 84)
        for t in range(TILES):
            link(v.tensor_tensor(rt[:, t, 96:128].rearrange("p (g j) -> p g j", g=4),
                                 rt[:, t, 4:36].rearrange("p (g j) -> p g j", g=4),
                                 group_hot[:, t].unsqueeze(2).to_broadcast([P, 4, 8]), ALU.mult))
            link(v.tensor_reduce(rt[:, t, 88:96], rt[:, t, 96:128].rearrange("p (g j) -> p j g", g=4), AX.X, ALU.add))
        link(v.tensor_reduce(c1(46), rt[:, :, 88:96], AX.X, ALU.max))
        v.tensor_tensor(rt[:, :, 48:56], rt[:, :, 88:96], wide(c1(46), 8), ALU.subtract).then_inc(shifted, 1)
        dve.wait_ge(exped, 2 * layer + 2)
        e = rt[:, :, 68:76]
        link(v.tensor_reduce(c1(47), e, AX.X, ALU.max))
        hot1 = first_best(e, c1(47), 8, const("rank8"), 128, 136)
        link(v.scalar_tensor_tensor(out=rt[:, :, 144:152], in0=hot1, scalar=-4.0, in1=e, op0=ALU.mult, op1=ALU.add))
        link(v.tensor_reduce(c1(56), rt[:, :, 144:152], AX.X, ALU.max))
        hot2 = first_best(rt[:, :, 144:152], c1(56), 8, const("rank8"), 152, 160)
        link(v.tensor_tensor(c1(57), c1(47), c1(56), ALU.add))
        link(v.reciprocal(c1(57), c1(57)))
        link(v.tensor_tensor(c1(57), c1(57), c1(38), ALU.mult))
        link(v.tensor_tensor(c1(58), c1(57), c1(56), ALU.mult))
        link(v.tensor_tensor(c1(57), c1(57), c1(47), ALU.mult))
        link(v.tensor_tensor(hot1, hot1, wide(c1(57), 8), ALU.mult))
        link(v.tensor_tensor(hot2, hot2, wide(c1(58), 8), ALU.mult))
        link(v.tensor_tensor(hot1, hot1, hot2, ALU.add))
        for t in range(TILES):
            last = v.tensor_tensor(cw[:, t, :].rearrange("p (g j) -> p g j", g=4),
                                   group_hot[:, t].unsqueeze(2).to_broadcast([P, 4, 8]),
                                   hot1[:, t].unsqueeze(1).to_broadcast([P, 4, 8]), ALU.mult)
        last.then_inc(cw_ready, 1)

    def pe_moe_and_ple(pe, layer):
        pe.wait_ge(rows_scaled, n_moe[layer]["scaled"] + 2)
        pe_turn(pe, t_moe[layer])
        wait_turned(pe, t_moe[layer])
        pe_route(pe, layer)
        pe_clear(pe, layer + 1)
        pe.wait_ge(x_split, layer + 1)
        pe_in(pe, layer + 1, 0)
        pe_turn_weights(pe, layer)
        pe_units(pe, layer + 1)
        pe_turn(pe, t_embed[layer])
        wait_turned(pe, t_embed[layer])
        wait_units_added(pe, layer + 1)
        pe_linear(pe, l_embed[layer])
        pe_turn(pe, t_ple[layer])
        wait_turned(pe, t_ple[layer])
        pe_linear(pe, l_gate[layer])

    def act_moe_and_ple(act, layer):
        act_norm(act, n_moe[layer])
        take_turn(act, t_moe[layer], "act")
        act_split_rows(act, t_moe[layer], layer + 1)
        act_first_units(act, layer + 1)
        act_route(act, layer)
        act_units(act, layer + 1)
        split_first(act, l_embed[layer], "act")
        take_turn(act, t_embed[layer], "act")
        wait_units_added(act, layer + 1)
        take_linear(act, l_embed[layer], "act")
        take_turn(act, t_ple[layer], "act")
        act_norm(act, n_ple[layer])
        take_linear(act, l_gate[layer], "act")
        act.wait_ge(ple_done, 2 * (layer + 1))

    def dve_moe_and_ple(dve, layer):
        dve_norm(dve, n_moe[layer])
        take_turn(dve, t_moe[layer], "dve")
        dve_split_rows(dve, layer + 1)
        dve_first_units(dve, layer + 1)
        dve_route(dve, layer)
        dve_units(dve, layer + 1)
        split_first(dve, l_embed[layer], "dve")
        take_turn(dve, t_embed[layer], "dve")
        wait_units_added(dve, layer + 1)
        take_linear(dve, l_embed[layer], "dve")
        take_turn(dve, t_ple[layer], "dve")
        dve_norm(dve, n_ple[layer])
        take_linear(dve, l_gate[layer], "dve")
        wait_took(dve, l_embed[layer])
        wait_took(dve, l_gate[layer])
        for t in range(TILES):
            nc.vector.tensor_tensor(ple_tmp[:, t], ple_gate[:, t], ple_y[:, t], ALU.mult).then_inc(gated, 1)
        for t in range(TILES):
            dve.wait_ge(gated, 2 * layer + t + 1)
            nc.vector.tensor_tensor(h[:, t], h[:, t], ple_tmp[:, t], ALU.add).then_inc(ple_done, 1)
        dve.wait_ge(ple_done, 2 * (layer + 1))

    block = ctx.enter_context(nc.Block())

    def sp_chunk(sp, n):
        c = chunks[n]
        for wait in c["waits"]:
            sp.wait_ge(*wait)
        sp.dma_start(c["view"], c["src"]).then_inc(c["landed"][0], 16)

    @block.sync
    def _(sp):
        for t in range(TILES):
            sp.dma_start(h[:, t, :], a["x"][0, t * P:(t + 1) * P, :]).then_inc(x_loaded, 16)
        for n in range(unit_at[0]):
            sp_chunk(sp, n)
        sp_units(sp, 0)
        for n in range(unit_at[0], unit_at[1]):
            sp_chunk(sp, n)
        sp_units(sp, 1)
        for n in range(unit_at[1], unit_at[2]):
            sp_chunk(sp, n)
        sp_units(sp, 2)
        for n in range(unit_at[2], len(chunks)):
            sp_chunk(sp, n)
        sp.wait_ge(ple_done, 4)
        for t in range(TILES):
            sp.dma_start(out[0, t * P:(t + 1) * P, :], h[:, t, :]).then_inc(stored, 16)
        sp.wait_ge(stored, 32)

    @block.gpsimd
    def _(pool):
        steps = [0]

        def link(ins):
            steps[0] += 1
            ins.then_inc(pool_step, 1)
            pool.wait_ge(pool_step, steps[0])

        g = nc.gpsimd
        g.memset(zeros[:, :], 0.0)
        g.memset(kcT[:, 64:], 0.0)
        g.memset(eps[:, :], EPS).then_inc(cleared, 1)
        for dest, src in small:
            pool.dma_start(dest, src, allow_slow_non_contiguous=True).then_inc(small_loaded, 16)

        pool.wait_ge(bias_row_ready, 1)
        pool.dma_start(toep_dram.rearrange("(h p n) -> h p n", h=HEADS_A, p=P),
                       bias_row[:, :].unsqueeze(1).to_broadcast([HEADS_A, P, SPAN])).then_inc(toep_spread, 16)
        pool.wait_ge(toep_spread, 16)
        pool.dma_start(toep[:, :, P:SPAN], bass.AP(toep_dram.tensor, 127, [[SPAN - 1, P], [P * SPAN, HEADS_A], [1, 256]])
                       ).then_inc(toep_ready, 16)
        pool.dma_start(toep[:, :, 0:P], bass.AP(toep_dram.tensor, 255, [[SPAN - 1, P], [P * SPAN, HEADS_A], [1, P]])
                       ).then_inc(toep_ready, 16)

        wait_took(pool, l_ukv)
        pool.wait_ge(squared, 4)
        pool.wait_ge(sines_ready, 2)
        wait_small(pool)
        q4, k4, kv4 = heads(qb, 8, 96), heads(kb, 8, 96), heads(kvb, 8, 128)
        sine, cosine = rope[:, 6], rope[:, 7]
        for t in range(TILES):
            g.tensor_tensor(k4[:, t, :, 0:NOPE], kv4[:, t, :, 0:NOPE],
                            gain_bk[:, 0:NOPE].unsqueeze(1).to_broadcast([P, 8, NOPE]), ALU.mult)
            g.tensor_tensor(rope_k[:, t, :], proj[:, t, 2560:2592], gain_bk[:, NOPE:DIM_B], ALU.mult)
            link(g.tensor_tensor(q4[:, t], q4[:, t], gain_bq[:, :].unsqueeze(1).to_broadcast([P, 8, DIM_B]), ALU.mult))
            for x1, x2, n in ((q4[:, t, :, NOPE:NOPE + 16], q4[:, t, :, NOPE + 16:DIM_B], 8),
                              (rope_k[:, t, 0:16].unsqueeze(1), rope_k[:, t, 16:32].unsqueeze(1), 1)):
                cos = cosine[:, t].unsqueeze(1).to_broadcast([P, n, 16])
                sin = sine[:, t].unsqueeze(1).to_broadcast([P, n, 16])
                tmp = rope_tmp[:, :, 0:n, :]
                g.tensor_tensor(tmp[:, 0], x1, cos, ALU.mult)
                g.tensor_tensor(tmp[:, 1], x2, sin, ALU.mult)
                g.tensor_tensor(tmp[:, 2], x2, cos, ALU.mult)
                link(g.tensor_tensor(tmp[:, 3], x1, sin, ALU.mult))
                g.tensor_tensor(x1, tmp[:, 0], tmp[:, 1], ALU.subtract)
                link(g.tensor_tensor(x2, tmp[:, 2], tmp[:, 3], ALU.add))
            link(g.tensor_copy(k4[:, t, :, NOPE:DIM_B], rope_k[:, t].unsqueeze(1).to_broadcast([P, 8, ROPE])))
        pool.wait_ge(scale_ready, 1)
        pool_attention(pool, att_a)
        pool.wait_ge(scale_ready, 3)
        pool_attention(pool, att_b)

        wait_took(pool, l_nsa)
        g.memset(blocks, 0.0).then_inc(blocks_cleared, 1)
        for i in range(2):
            for t in range(TILES):
                src = proj[:, t, 1024 + 256 * i:1280 + 256 * i].rearrange("p (g d) -> p g d", d=64)
                last = g.tensor_copy(rows[:, i, t * 512:(t + 1) * 512].rearrange("p (g x d) -> p g x d", g=4, x=2),
                                     src.unsqueeze(2).to_broadcast([P, 4, 2, 64]))
            last.then_inc(doubled, 1)
        pool.wait_ge(scale_ready, 4)
        pool_attention(pool, att_n)
        pool_spread(pool, 0)
        pool.wait_ge(scale_ready, 5)
        pool_attention(pool, att_m)
        pool_spread(pool, 1)

    @block.tensor
    def _(pe):
        for s in (front_turned, scores_made):
            pe.sem_inc(s, 1)
        pe.sem_inc(down_made, OPEN)
        pe.wait_ge(cleared, 1)
        wait_table(pe)
        pe.wait_ge(x_loaded, 32)
        pe_turn(pe, t_mix)
        wait_turned(pe, t_mix)
        pe_linear(pe, l_in[:4])
        wait_small(pe)
        nc.tensor.matmul(bank[0:HEADS_A, 4, 0:SPAN], rel[:, :], const("onehot", 32), start=True,
                         stop=True).then_inc(bias_row_made, 1)
        for i in range(2):
            mm = nc.tensor.transpose(bank[:, 5, i * 16:(i + 1) * 16], pos_rows[:, i, :], ident[0:16, 0:16])
        mm.then_inc(pos_turned, 1)
        pe_linear(pe, l_in[4:])
        pe.wait_ge(bias_row_ready, 1)
        pe.wait_ge(pos_ready, 1)
        wait_took(pe, l_in)
        pe_turn(pe, t_cq)
        pe_turn(pe, t_ckv)
        wait_turned(pe, t_cq + t_ckv)
        pe_linear(pe, l_uq)
        pe_linear(pe, l_ukv)
        wait_took(pe, l_ukv)
        pe_attention(pe, att_a)
        pe_attention(pe, att_b)
        pe.wait_ge(mixed, att_n["base"]["mixed"])
        pe_turn(pe, t_mix1)
        wait_turned(pe, t_mix1)
        pe_linear(pe, l_o)
        wait_took(pe, l_o)
        pe_turn(pe, t_ffn)
        wait_turned(pe, t_ffn)
        pe_clear(pe, 0)
        pe_in(pe, 0, 0)
        pe_units(pe, 0)
        wait_units_added(pe, 0)
        pe_turn(pe, t_nsa)
        wait_turned(pe, t_nsa)
        pe_linear(pe, l_nsa)
        wait_took(pe, l_nsa)
        for i in range(2):
            pe.wait_ge(doubled, i + 1)
            for gr in range(4):
                for t in range(TILES):
                    mm = nc.tensor.transpose(
                        bank[:, 2 * i + gr // 2, (gr % 2) * 256 + t * P:(gr % 2) * 256 + (t + 1) * P],
                        rows[:, i, t * 512 + gr * P:t * 512 + (gr + 1) * P], ident)
            mm.then_inc(cmp_turned, 1)
        for i in range(2):
            w1 = cmp_chunks[i]["view"]
            pe.wait_ge(*cmp_chunks[i]["landed"])
            pe.wait_ge(blocks_made, i + 1)
            for j in range(16):
                mm = nc.tensor.matmul(bank[0:64, 4 + i, 0:256], blocks[:, j, :, :].rearrange("p g n -> p (g n)"),
                                      w1[:, j, :], start=j == 0, stop=j == 15)
            mm.then_inc(cmp_hid_made, 1)
        for i in range(2):
            pe.wait_ge(gelu_done, i + 1)
            for c in range(2):
                mm = nc.tensor.transpose(bank[:, 2 + i, c * 64:(c + 1) * 64], hid_rows[:, i, c * P:(c + 1) * P],
                                         ident[0:64, 0:64])
            mm.then_inc(hid_turned, 1)
        for i in range(2):
            pe.wait_ge(hid_kept, i + 1)
            for gr in range(4):
                for c in range(2):
                    mm = nc.tensor.matmul(bank[0:CMP_PAD, 6 + i, gr * 64:(gr + 1) * 64],
                                          cmp_hid[:, i, c, gr * CMP_PAD:(gr + 1) * CMP_PAD], cmp_w2[:, i, c, :],
                                          start=c == 0, stop=c == 1)
            mm.then_inc(cmp_out_made, 1)
        pe.wait_ge(cmp_rows_ready, 1)
        for gr in range(4):
            mm = nc.tensor.transpose(bank[0:64, 4, gr * CMP_PAD:(gr + 1) * CMP_PAD], cmp_kv[:, 0, gr, :],
                                     ident[0:CMP_PAD, 0:CMP_PAD])
        mm.then_inc(kc_turned, 1)
        pe.wait_ge(kcT_ready, 1)
        pe_attention(pe, att_n, compressed=True)
        pe.wait_ge(mix_step, att_n["mix_base"] + 4 * att_n["mix_per"])
        pe_turn(pe, t_mix2)
        wait_turned(pe, t_mix2)
        pe_linear(pe, l_nsa_o)
        pe_moe_and_ple(pe, 0)
        pe.wait_ge(ple_done, 2)
        pe_turn(pe, t_moba)
        wait_turned(pe, t_moba)
        pe_linear(pe, l_kv)
        pe_linear(pe, l_q)
        wait_took(pe, l_kv + l_q)
        pe_attention(pe, att_m)
        pe.wait_ge(mixed, attended["mixed"])
        pe_turn(pe, t_mix3)
        wait_turned(pe, t_mix3)
        pe_linear(pe, l_moba_o)
        pe_moe_and_ple(pe, 1)

    @block.scalar
    def _(act):
        def squares(dest, src, last=False):
            ins = nc.scalar.activation(dest, src, ACT.Square)
            if last:
                ins.then_inc(squared, 1)

        act.dma_start(table[:, :], a["table"]).then_inc(table_loaded, 16)
        act.dma_start(gains["norm_mix_g"][:, :], a["norm_mix_g"].rearrange("(p k) -> p k", k=KB),
                      allow_slow_non_contiguous=True).then_inc(table_loaded, 16)
        act.wait_ge(cleared, 1)
        act.wait_ge(x_loaded, 32)
        wait_table(act)
        take_turn(act, t_mix, "act")
        split_first(act, l_in, "act")
        act_norm(act, n_mix)
        take_linear(act, l_in[:8], "act")
        act.wait_ge(angle_ready, 1)
        nc.scalar.activation(rope[:, 6], rope[:, 4], ACT.Sin).then_inc(sines_ready, 1)
        nc.scalar.activation(rope[:, 7], rope[:, 5], ACT.Sin).then_inc(sines_ready, 1)
        wait_small(act)
        act.wait_ge(gains_scaled, 2)
        take_linear(act, l_in[8:], "act")
        wait_took(act, l_in)
        work_a = work[:, 0:2048].rearrange("p (t n) -> p t n", t=TILES)
        for t in range(TILES):
            squares(work_a[:, t], proj[:, t, 0:1024], last=t == 1)
        split_first(act, l_uq, "act")
        take_turn(act, t_cq, "act")
        take_turn(act, t_ckv, "act")
        act_norm(act, n_lat)
        take_linear(act, l_uq, "act")
        take_linear(act, l_ukv, "act")
        wait_took(act, l_uq + l_ukv)
        act.wait_ge(sums_ready, 1)
        act_root(act, r_a)
        squares(work[:, 0:1536], arena[:, 5248:6784], last=True)
        for t in range(TILES):
            squares(work[:, 1536 + t * 512:2048 + t * 512].rearrange("p (h d) -> p h d", d=64),
                    heads(kvb, 8, 128)[:, t, :, 0:NOPE], last=t == 1)
        squares(work[:, 2560:2624].rearrange("p (t d) -> p t d", t=TILES), proj[:, :, 2560:2592], last=True)
        act.wait_ge(sums_ready, 3)
        act_root(act, r_bq)
        act_root(act, r_bk)
        act_attention(act, att_a)
        act_attention(act, att_b)
        split_first(act, l_o, "act")
        take_turn(act, t_mix1, "act")
        take_linear(act, l_o, "act")
        wait_took(act, l_o)
        take_turn(act, t_ffn, "act")
        act_first_units(act, 0)
        act_norm(act, n_ffn)
        act_units(act, 0)
        split_first(act, l_nsa, "act", 0, 1)
        take_turn(act, t_nsa, "act")
        split_first(act, l_nsa, "act", 1)
        wait_units_added(act, 0)
        act_norm(act, n_nsa)
        take_linear(act, l_nsa, "act")
        wait_took(act, l_nsa)
        for t in range(TILES):
            squares(work[:, t * 1024:(t + 1) * 1024], proj[:, t, 0:1024])
        for t in range(TILES):
            for q, c0 in enumerate((1536, 2048)):
                squares(work[:, 2048 + q * 512 + t * 256:2304 + q * 512 + t * 256], proj[:, t, c0:c0 + 256],
                        last=t == 1 and q == 1)
        nc.scalar.activation(gates[:, :, :, :].rearrange("p t h b -> p t (h b)"), proj[:, :, 2560:2608],
                             ACT.Sigmoid).then_inc(gates_ready, 1)
        for i in range(2):
            act.wait_ge(cmp_hid_made, i + 1)
            nc.scalar.activation(hid_rows[:, i, :], bank[0:64, 4 + i, 0:256], ACT.Gelu_apprx_tanh).then_inc(gelu_done, 1)
        for i in range(2):
            act.wait_ge(hid_turned, i + 1)
            nc.scalar.copy(cmp_hid[:, i].rearrange("p c n -> p (c n)"), bank[:, 2 + i, 0:128]).then_inc(hid_kept, 1)
        act.wait_ge(sums_ready, 4)
        act_root(act, r_nsa)
        act.wait_ge(sums_ready, 5)
        act_root(act, r_kc)
        act_attention(act, att_n, compressed=True)
        split_first(act, l_nsa_o, "act")
        take_turn(act, t_mix2, "act")
        take_linear(act, l_nsa_o, "act")
        wait_took(act, l_nsa_o)
        act_moe_and_ple(act, 0)
        split_first(act, l_kv, "act", 0, 2)
        take_turn(act, t_moba, "act")
        split_first(act, l_kv, "act", 2)
        act_norm(act, n_moba)
        take_linear(act, l_kv, "act")
        take_linear(act, l_q, "act")
        wait_took(act, l_kv + l_q)
        for t in range(TILES):
            squares(work[:, t * 1024:(t + 1) * 1024], moba_q[:, t, :])
        for t in range(TILES):
            squares(work[:, 2048 + t * 256:2304 + t * 256], moba_kv[:, t, 0:256], last=t == 1)
        act.wait_ge(sums_ready, 6)
        act_root(act, r_moba)
        act_attention(act, att_m)
        split_first(act, l_moba_o, "act")
        take_turn(act, t_mix3, "act")
        take_linear(act, l_moba_o, "act")
        wait_took(act, l_moba_o)
        act_moe_and_ple(act, 1)

    @block.vector
    def _(dve):
        v = nc.vector

        def link(ins):
            dve_link(dve, ins)

        for s in (biased, mixed):
            dve.sem_inc(s, 1)
        dve.sem_inc(c_scored, OPEN)
        dve.sem_inc(down_split, OPEN)
        dve.wait_ge(x_loaded, 32)
        wait_table(dve)
        take_turn(dve, t_mix, "dve")
        split_first(dve, l_in, "dve")
        dve_norm(dve, n_mix)
        take_linear(dve, l_in[:4], "dve")
        wait_small(dve)
        dve.wait_ge(bias_row_made, 1)
        v.tensor_tensor(bias_row[:, :], bank[0:HEADS_A, 4, 0:SPAN], const("log_count", HEADS_A),
                        ALU.add).then_inc(bias_row_ready, 1)
        dve.wait_ge(pos_turned, 1)
        v.tensor_copy(cmp_pos[:, :, :].rearrange("p i j -> p (i j)"), bank[:, 5, 0:32]).then_inc(pos_ready, 1)
        for col in (2, 6):
            v.tensor_scalar(head_gain[:, col:col + 1], head_gain[:, col:col + 1], DIM ** -0.5, None,
                            ALU.mult).then_inc(gains_scaled, 1)
        link(v.tensor_copy(posf[:, :], pos_i[:, :]))
        for t in range(TILES):
            last = v.tensor_scalar(rope[:, 0, t], const("inv_freq"), posf[:, t:t + 1], None, ALU.mult)
        link(last)
        magic = 12582912.0
        p1 = 6.28125
        p2 = float(np.float32(2 * math.pi - p1))
        p2 = float(np.frombuffer((np.float32(p2).view(np.uint32) & np.uint32(0xFFFFF000)).tobytes(), np.float32)[0])
        p3 = float(np.float32(2 * math.pi - p1 - p2))
        link(v.tensor_scalar(rope[:, 1], rope[:, 0], 1 / (2 * math.pi), magic, ALU.mult, ALU.add))
        link(v.tensor_scalar(rope[:, 1], rope[:, 1], magic, None, ALU.subtract))
        for src, part_of, dest in ((0, p1, 2), (2, p2, 3), (3, p3, 2)):
            link(v.scalar_tensor_tensor(out=rope[:, dest], in0=rope[:, 1], scalar=-part_of, in1=rope[:, src],
                                        op0=ALU.mult, op1=ALU.add))
        link(v.tensor_scalar(rope[:, 4], rope[:, 2], 3.1415925, -3.1415925, ALU.min, ALU.max))
        link(v.scalar_tensor_tensor(out=rope[:, 3], in0=rope[:, 4], scalar=-1.0, in1=rope[:, 4], op0=ALU.mult,
                                    op1=ALU.max))
        v.tensor_scalar(rope[:, 5], rope[:, 3], -1.0, math.pi / 2, ALU.mult, ALU.add).then_inc(angle_ready, 1)
        take_linear(dve, l_in[4:], "dve")
        wait_took(dve, l_in)
        dve.wait_ge(squared, 1)
        v.tensor_reduce(r_a["sum"], work[:, 0:2048].rearrange("p (h d) -> p h d", d=64), AX.X,
                        ALU.add).then_inc(sums_ready, 1)
        split_first(dve, l_uq, "dve")
        dve.wait_ge(sums_ready, 1)
        take_turn(dve, t_cq, "dve")
        take_turn(dve, t_ckv, "dve")
        dve_norm(dve, n_lat)
        take_linear(dve, l_uq, "dve")
        take_linear(dve, l_ukv, "dve")
        dve_root(dve, r_a, scale_ready)
        dve.wait_ge(squared, 4)
        v.tensor_reduce(r_bq["sum"], work[:, 0:1536].rearrange("p (h d) -> p h d", d=96), AX.X,
                        ALU.add).then_inc(sums_ready, 1)
        v.tensor_reduce(stat[:, 1390:1392], work[:, 2560:2624].rearrange("p (h d) -> p h d", d=32), AX.X, ALU.add)
        link(v.tensor_reduce(r_bk["sum"], work[:, 1536:2560].rearrange("p (h d) -> p h d", d=64), AX.X, ALU.add))
        v.tensor_tensor(r_bk["sum"].rearrange("p (t h) -> p t h", t=TILES),
                        r_bk["sum"].rearrange("p (t h) -> p t h", t=TILES),
                        stat[:, 1390:1392].unsqueeze(2).to_broadcast([P, TILES, 8]), ALU.add).then_inc(sums_ready, 1)
        dve_root(dve, r_bq, scale_ready)
        dve_root(dve, r_bk, scale_ready)
        dve.wait_ge(toep_ready, 32)
        dve_attention(dve, att_a)
        dve_attention(dve, att_b)
        split_first(dve, l_o, "dve")
        take_turn(dve, t_mix1, "dve")
        take_linear(dve, l_o, "dve")
        wait_took(dve, l_o)
        take_turn(dve, t_ffn, "dve")
        dve_first_units(dve, 0)
        dve_norm(dve, n_ffn)
        dve_units(dve, 0)
        split_first(dve, l_nsa, "dve", 0, 1)
        take_turn(dve, t_nsa, "dve")
        split_first(dve, l_nsa, "dve", 1)
        wait_units_added(dve, 0)
        dve_norm(dve, n_nsa)
        take_linear(dve, l_nsa, "dve")
        dve.wait_ge(squared, 5)
        r3 = r_nsa["sum"].rearrange("p (t h) -> p t h", t=TILES)
        v.tensor_reduce(r3[:, :, 0:16], work[:, 0:2048].rearrange("p (t h d) -> p t h d", t=TILES, d=64), AX.X, ALU.add)
        for q in range(2):
            last = v.tensor_reduce(r3[:, :, 16 + 4 * q:20 + 4 * q],
                                   work[:, 2048 + q * 512:2560 + q * 512].rearrange("p (t h d) -> p t h d", t=TILES,
                                                                                    d=64), AX.X, ALU.add)
        last.then_inc(sums_ready, 1)
        dve.wait_ge(blocks_cleared, 1)
        for i in range(2):
            dve.wait_ge(cmp_turned, i + 1)
            if i:
                dve.wait_ge(cmp_hid_made, 1)
            for gr in range(4):
                for half in range(2):
                    lo = 64 * half
                    at = bank[lo:lo + 64, 2 * i + gr // 2, (gr % 2) * 256 + half:(gr % 2) * 256 + half + 1]
                    src = bass.AP(at.tensor, at.offset, [list(at.ap[0]), [2, 16], [16, N_CMP]])
                    last = v.tensor_tensor(blocks[lo:lo + 64, :, gr, 0:N_CMP], src,
                                           cmp_pos[lo:lo + 64, i, :].unsqueeze(2).to_broadcast([64, 16, N_CMP]),
                                           ALU.add)
            last.then_inc(blocks_made, 1)
        dve_root(dve, r_nsa, scale_ready)
        for i in range(2):
            dve.wait_ge(cmp_out_made, i + 1)
            link(v.tensor_copy(cmp_kv[:, i].rearrange("p g d -> p (g d)"), bank[0:CMP_PAD, 6 + i, 0:256]))
        link(v.tensor_tensor(cmp_sq[:, :, :], cmp_kv[:, 0], cmp_kv[:, 0], ALU.mult))
        v.tensor_reduce(r_kc["sum"], cmp_sq[:, :, :], AX.X, ALU.add).then_inc(sums_ready, 1)
        dve_root(dve, r_kc)
        v.tensor_tensor(cmp_kv[:, 0], cmp_kv[:, 0], r_kc["scale"].unsqueeze(2).to_broadcast([CMP_PAD, 4, 64]),
                        ALU.mult).then_inc(cmp_rows_ready, 1)
        dve.wait_ge(kc_turned, 1)
        v.tensor_scalar(kcT[:, 0:64], bank[0:64, 4, 0:64], head_gain[:, 3:4], None, ALU.mult).then_inc(kcT_ready, 1)
        dve.wait_ge(gates_ready, 1)
        dve_attention(dve, att_n, compressed=True)
        split_first(dve, l_nsa_o, "dve")
        take_turn(dve, t_mix2, "dve")
        take_linear(dve, l_nsa_o, "dve")
        wait_took(dve, l_nsa_o)
        dve_moe_and_ple(dve, 0)
        split_first(dve, l_kv, "dve", 0, 2)
        take_turn(dve, t_moba, "dve")
        split_first(dve, l_kv, "dve", 2)
        dve_norm(dve, n_moba)
        take_linear(dve, l_kv, "dve")
        take_linear(dve, l_q, "dve")
        dve.wait_ge(squared, 6)
        r3 = r_moba["sum"].rearrange("p (t h) -> p t h", t=TILES)
        v.tensor_reduce(r3[:, :, 0:16], work[:, 0:2048].rearrange("p (t h d) -> p t h d", t=TILES, d=64), AX.X, ALU.add)
        v.tensor_reduce(r3[:, :, 16:20], work[:, 2048:2560].rearrange("p (t h d) -> p t h d", t=TILES, d=64), AX.X,
                        ALU.add).then_inc(sums_ready, 1)
        dve_root(dve, r_moba, scale_ready)
        dve_attention(dve, att_m)
        split_first(dve, l_moba_o, "dve")
        take_turn(dve, t_mix3, "dve")
        take_linear(dve, l_moba_o, "dve")
        wait_took(dve, l_moba_o)
        dve_moe_and_ple(dve, 1)

    ctx.close()


INPUTS = (
    "x", "positions", "norm_mix_g", "w_in", "qnorm_a_g", "knorm_a_g", "rel_bias", "cq_norm_g", "ckv_norm_g", "w_uq",
    "w_ukv", "qnorm_b_g", "knorm_b_g", "w_o", "norm_ffn_g", "w_ff1", "w_ff2", "p_2", "ln_mix_2", "ln_ffn_2",
    "ln_ple_2", "a_w_in_2", "a_q_norm_2", "a_k_norm_2", "a_ck_pos_2", "a_ck_w1_2", "a_ck_w2_2", "a_cv_pos_2",
    "a_cv_w1_2", "a_cv_w2_2", "a_w_out_2", "kv_norm_2", "w_kv_shared_2", "k_norm_shared_2", "b_w_q_2",
    "b_q_norm_2", "b_w_out_2", "moe_w_group_2", "moe_b_group_2", "moe_w_expert_2", "moe_b_expert_2",
    "moe_w_gate_2", "moe_w_up_2", "moe_w_down_2", "ple_w_proj_2", "ple_w_gate_2",
)


def kernel(**inputs):
    import concourse.bacc as bacc
    from concourse import mybir
    from concourse.bass_utils import run_bass_kernel_spmd

    nc = bacc.Bacc("TRN2", target_bir_lowering=False, num_devices=1)
    arrays, aps = {}, {}
    given = {name: np.ascontiguousarray(inputs[name]) for name in INPUTS}
    given["table"] = constant_table()
    for name, value in given.items():
        arrays[f"in_{name}"] = value
        aps[name] = nc.dram_tensor(f"in_{name}", value.shape, mybir.dt.from_np(value.dtype),
                                   kind="ExternalInput").ap()
    out = nc.dram_tensor("out_0", (1, TOKENS, D_MODEL), mybir.dt.float32, kind="ExternalOutput").ap()
    build_program(nc, aps, out)
    result = run_bass_kernel_spmd(nc, [arrays], core_ids=[0])
    return result.results[0]["out_0"]
```

```python
import math

import numpy as np

TOKENS, TILES, P = 256, 2, 128
D_MODEL, KB = 1024, 8
HEADS_A, DIM_A = 8, 64
Q_RANK, KV_RANK, NOPE, ROPE = 768, 256, 64, 32
DIM_B = NOPE + ROPE
IN_WIDTH = 3 * HEADS_A * DIM_A + Q_RANK + KV_RANK + ROPE
NSA_WIDTH = 1024 + 6 * 256 + 48
HEADS, KV_HEADS, DIM = 16, 4, 64
N_CMP, CMP_PAD = 15, 16
EXPERTS, GROUPS, PER_GROUP = 32, 4, 8
SPAN = 384
MASKED = -1e30
EPS = 1e-6
SLOTS, SLOT, PAIRS = 8, 1024, 4
UNITS, RAW, UNIT = 32, 3, 3072

TABLE = {}
_at = 0
for _name, _width in (("ident", 128), ("dist", SPAN), ("causal", SPAN), ("cmp_bias", 512), ("cmp_valid", 32), ("spread", 128), ("own", 8),
                      ("onehot", SPAN), ("log_count", SPAN), ("inv_freq", 16), ("neg_slope", 16),
                      ("rank4", 4), ("rank8", 8)):
    TABLE[_name] = (_at, _width)
    _at += _width
TABLE_WIDTH = _at


def t5_bucket(dist):
    exact = 16
    safe = np.maximum(dist, 1).astype(np.float32)
    large = exact + (np.log(safe / exact) / math.log(2048 / exact) * 16).astype(np.int64)
    return np.where(dist < exact, dist, np.minimum(large, 31))


def constant_table():
    t = np.zeros((P, TABLE_WIDTH), np.float32)

    def put(name, value, rows=P):
        at, width = TABLE[name]
        t[:rows, at:at + width] = value.reshape(rows, width)

    q = np.arange(P)[:, None]
    dist = np.concatenate([q - np.arange(128)[None], 128 + q - np.arange(256)[None]], 1)
    put("ident", np.eye(P, dtype=np.float32))
    put("dist", np.where(dist >= 0, dist, -MASKED).astype(np.float32))
    put("causal", np.where(dist >= 0, 0, MASKED).astype(np.float32))
    slopes = (2.0 ** (-8.0 * np.arange(1, HEADS + 1) / HEADS)).astype(np.float32)
    put("neg_slope", np.broadcast_to(-slopes, (P, HEADS)))
    end = np.arange(CMP_PAD) * 16 + 31
    token = np.arange(TILES)[None, :] * P + np.arange(P)[:, None]
    cd = (token[:, :, None] - end).astype(np.float32)
    ok = (cd >= 0) & (np.arange(CMP_PAD) < N_CMP)
    bias = np.where(ok[:, None, :, None], -slopes.reshape(1, 4, 1, 4, 1) * cd[:, None, :, None], np.float32(MASKED))
    put("cmp_bias", bias.astype(np.float32))
    put("cmp_valid", ok.astype(np.float32))
    put("spread", np.tile(np.eye(CMP_PAD, dtype=np.float32), (1, 8)), CMP_PAD)
    put("own", (np.arange(P)[:, None] // CMP_PAD == np.arange(8)).astype(np.float32))
    d = 255 - np.arange(SPAN)
    real = (d >= 0)
    onehot = (t5_bucket(np.maximum(d, 0))[None] == np.arange(32)[:, None]) & real
    count = ((d <= 128).astype(int) + (d % 4 == 0) + (d % 16 == 0)) * real
    put("onehot", (onehot & (count > 0)).astype(np.float32), 32)
    logs = np.where(count > 0, np.log(np.maximum(count, 1)), MASKED).astype(np.float32)
    put("log_count", np.broadcast_to(logs, (HEADS_A, SPAN)), HEADS_A)
    inv = 1.0 / (10000.0 ** (np.arange(0, ROPE, 2) / ROPE))
    put("inv_freq", np.broadcast_to(inv.astype(np.float32), (P, 16)))
    put("rank4", np.broadcast_to(4.0 - np.arange(4), (P, 4)))
    put("rank8", np.broadcast_to(8.0 - np.arange(8), (P, 8)))
    return t


def build_program(nc, a, out):
    import concourse.bass as bass
    from concourse import mybir
    from contextlib import ExitStack

    F32, F32R = mybir.dt.float32, mybir.dt.float32r
    ALU, ACT, AX = mybir.AluOpType, mybir.ActivationFunctionType, mybir.AxisListType
    ds = bass.ds
    ctx = ExitStack()

    def sb(name, shape, dt=F32):
        return ctx.enter_context(nc.sbuf_tensor(name, shape, dt))

    def sem(name):
        return ctx.enter_context(nc.semaphore(name))

    bank = ctx.enter_context(nc.psum_tensor("bank", [P, 8, 512], F32))
    region = -(-nc.sbuf_base // 32) * 32
    ring = sb("ring", [P, SLOTS * SLOT + PAIRS * 2 * SLOT])
    mix_at = -(-nc.sbuf_base // 32) * 32
    mix = sb("mix", [P, TILES, D_MODEL])
    toep = sb("toep", [P, HEADS_A, SPAN])
    h = sb("h", [P, TILES, D_MODEL])
    rows = sb("rows", [P, TILES, D_MODEL])
    second_at = -(-nc.sbuf_base // 32) * 32
    second = sb("second", [P, 2048])
    x_high = sb("x_high", [P, KB, TOKENS], F32R)
    arena = sb("arena", [P, 8320])
    work_at = -(-nc.sbuf_base // 32) * 32
    work = sb("work", [P, 3072])
    table = sb("table", [P, TABLE_WIDTH])
    stat = sb("stat", [P, 1400])
    zeros = sb("zeros", [P, 512])
    junk = sb("junk", [P, 768])
    eps = sb("eps", [P, 1])

    raw = ring[:, 0:RAW * UNIT].rearrange("p (s n) -> p s n", s=RAW)
    weight_parts = nc.alloc_sbuf_tensor_at("weight_parts", [P, PAIRS, 2, SLOT], F32R,
                                           offset=region + SLOTS * SLOT * 4)
    parts = nc.alloc_sbuf_tensor_at("parts", [P, 2, 2, UNIT], F32R, offset=region + RAW * UNIT * 4)
    turned_x = second[:, :].rearrange("p (k n) -> p k n", k=KB)
    x_low = nc.alloc_sbuf_tensor_at("x_low", [P, KB, TOKENS], F32R, offset=work_at + 4096)
    hid_parts = nc.alloc_sbuf_tensor_at("hid_parts", [P, 2, 2, TOKENS], F32R, offset=work_at)
    embed_high = nc.alloc_sbuf_tensor_at("embed_high", [P, 2, TOKENS], F32R, offset=second_at)
    embed_low = nc.alloc_sbuf_tensor_at("embed_low", [P, 2, TOKENS], F32R, offset=second_at + 2048)
    kv_high = nc.alloc_sbuf_tensor_at("kv_high", [P, KB, TOKENS], F32R, offset=second_at)
    kv_low = nc.alloc_sbuf_tensor_at("kv_low", [P, KB, TOKENS], F32R, offset=mix_at)
    HIGH, LOW = 0, 1

    value_banks = bank[:, 6:8, :].rearrange("p t (h x d) -> p t h x d", h=4, x=2)

    def const(name, n=P):
        at, width = TABLE[name]
        return table[0:n, at:at + width]

    ident = const("ident")
    proj = arena[:, 0:2 * 2624].rearrange("p (t n) -> p t n", t=TILES)
    qb = arena[:, 5248:6784].rearrange("p (t n) -> p t n", t=TILES)
    kb = arena[:, 6784:8320].rearrange("p (t n) -> p t n", t=TILES)
    kvb = second[:, :].rearrange("p (t n) -> p t n", t=TILES)
    moba_q = arena[:, 0:2048].rearrange("p (t n) -> p t n", t=TILES)
    moba_kv = arena[:, 2048:3072].rearrange("p (t n) -> p t n", t=TILES)
    ple_y = arena[:, 0:2048].rearrange("p (t n) -> p t n", t=TILES)
    ple_gate = arena[:, 2048:4096].rearrange("p (t n) -> p t n", t=TILES)
    ple_tmp = arena[:, 4096:6144].rearrange("p (t n) -> p t n", t=TILES)
    token_weight = arena[:, 0:EXPERTS * TOKENS].rearrange("p (e n) -> p e n", e=EXPERTS)

    gains = {}
    for name in ("norm_mix_g", "norm_ffn_g", "ln_mix0", "ln_ffn0", "ln_ple0", "kv_norm", "ln_mix1", "ln_ffn1",
                 "ln_ple1"):
        gains[name] = sb(f"gain_{name}", [P, KB])
    gain_cq, gain_ckv = sb("gain_cq", [P, 6]), sb("gain_ckv", [P, 2])
    head_gain = sb("head_gain", [64, 8])
    gain_bq, gain_bk = sb("gain_bq", [P, DIM_B]), sb("gain_bk", [P, DIM_B])
    pos_rows = sb("pos_rows", [16, 2, P])
    cmp_pos = sb("cmp_pos", [P, 2, 16])
    cmp_w2 = sb("cmp_w2", [P, 2, 2, 64])
    route_w = sb("route_w", [P, 2, KB, 36])
    route_b = sb("route_b", [P, 2, 36])
    rel = sb("rel", [32, HEADS_A])
    pos_i = sb("pos_i", [P, TILES], mybir.dt.int32)
    embed = sb("embed", [P, 2, TILES, 256])

    def turned_heads(at, n, d):
        return ring[0:d, SLOTS * SLOT + at * TOKENS:SLOTS * SLOT + (at + n) * TOKENS].rearrange("p (h n) -> p h n", h=n)

    logit = work[:, 0:1536].rearrange("p (h n) -> p h n", h=4)
    prob = work[:, 1536:3072].rearrange("p (h n) -> p h n", h=4)
    probT = sb("probT", [P, 2, SPAN])
    neg_max = sb("neg_max", [P, 4, 2])
    total = sb("total", [P, 2, 8])
    share = sb("share", [P, 8])
    part = sb("part", [P, 8, 64])
    rope = sb("rope", [P, 8, TILES, 16])
    posf = sb("posf", [P, TILES])
    rope_tmp = rows[:, 1, 0:512].rearrange("p (x h d) -> p x h d", x=4, h=8)
    rope_k = sb("rope_k", [P, TILES, ROPE])
    bias_row = mix[0:HEADS_A, 0, 0:SPAN]
    spare = toep[:, :, :].rearrange("p h n -> p (h n)")
    blocks = [spare[:, at:at + 1024].rearrange("p (j g n) -> p j g n", j=16, g=KV_HEADS) for at in (0, 2048)]
    cmp_hid = spare[:, 1024:1280].rearrange("p (i c n) -> p i c n", i=2, c=2)
    cmp_kv = spare[0:CMP_PAD, 1280:1792].rearrange("p (i g d) -> p i g d", i=2, g=KV_HEADS)
    cmp_rows = spare[0:CMP_PAD, 1280:1792]
    cmp_sq = spare[0:CMP_PAD, 1792:2048].rearrange("p (g d) -> p g d", g=KV_HEADS)
    hid_rows = second[0:64, 0:512].rearrange("p (i n) -> p i n", i=2)
    kcT = sb("kcT", [64, 64 + P - CMP_PAD])
    cl = spare[:, 2560:3072].rearrange("p (t h n) -> p t h n", t=TILES, h=HEADS)
    cT = spare[:, 0:512].rearrange("p (x n) -> p x n", x=4)
    c_share = sb("c_share", [P, TILES * HEADS])
    own_values = ring[:, SLOTS * SLOT + 24 * TOKENS:SLOTS * SLOT + 28 * TOKENS].rearrange("p (o n) -> p o n", o=2)
    gates = sb("gates", [P, TILES, HEADS, 3])
    rt = sb("rt", [P, TILES, 256])
    cwT = junk[0:32, 0:TOKENS]
    cw = sb("cw", [P, TILES, EXPERTS])

    toep_dram = nc.dram_tensor("toep_dram", [HEADS_A * P * SPAN], F32).ap()
    cw_dram = nc.dram_tensor("cw_dram", [2, EXPERTS, TOKENS], F32).ap()

    x_loaded, table_loaded, small_loaded, stored = (
        sem(n) for n in ("x_loaded", "table_loaded", "small_loaded", "stored"))
    landed = [sem(f"landed{i}") for i in range(SLOTS)]
    in_landed = [sem(f"in_landed{i}") for i in range(RAW)]
    down_landed = [sem(f"down_landed{i}") for i in range(RAW)]
    weights_high, weights_split = sem("weights_high"), sem("weights_split")
    x_split, x_high_made = sem("x_split"), sem("x_high_made")
    in_high, in_split, down_high, down_split = (sem(n) for n in ("in_high", "in_split", "down_high", "down_split"))
    cleared = sem("cleared")
    squares_summed, roots_taken, rooted, rows_scaled = (
        sem(n) for n in ("squares_summed", "roots_taken", "rooted", "rows_scaled"))
    turned, act_turned, dve_turned = sem("turned"), sem("act_turned"), sem("dve_turned")
    lin_made, act_took, dve_took = sem("lin_made"), sem("act_took"), sem("dve_took")
    squared, sums_ready, scale_ready = sem("squared"), sem("sums_ready"), sem("scale_ready")
    dve_step, pool_step, mix_step = sem("dve_step"), sem("pool_step"), sem("mix_step")
    bias_row_made, bias_row_ready = sem("bias_row_made"), sem("bias_row_ready")
    gains_scaled = sem("gains_scaled")
    pos_turned, pos_ready = sem("pos_turned"), sem("pos_ready")
    toep_spread, toep_ready = sem("toep_spread"), sem("toep_ready")
    angle_ready, sines_ready = sem("angle_ready"), sem("sines_ready")
    dve_scaled, pool_scaled = sem("dve_scaled"), sem("pool_scaled")
    scores_made, biased, maxed, probs_made, probs_turned, probT_ready, values_made, mixed = (
        sem(n) for n in ("scores_made", "biased", "maxed", "probs_made", "probs_turned", "probT_ready", "values_made",
                         "mixed"))
    OPEN = 2
    c_scores, c_scored, c_shifted, c_exped, c_probs, c_turned, cT_ready, c_values, c_taken = (
        sem(n) for n in ("c_scores", "c_scored", "c_shifted", "c_exped", "c_probs", "c_turned", "cT_ready",
                         "c_values", "c_taken"))
    spread_made, own_ready = sem("spread_made"), sem("own_ready")
    doubled, cmp_turned, blocks_made, cmp_hid_made, gelu_done = (
        sem(n) for n in ("doubled", "cmp_turned", "blocks_made", "cmp_hid_made", "gelu_done"))
    cmp_out_made, cmp_rows_ready, kc_turned, kcT_ready, gates_ready = (
        sem(n) for n in ("cmp_out_made", "cmp_rows_ready", "kc_turned", "kcT_ready", "gates_ready"))
    blocks_cleared, hid_turned, hid_kept = sem("blocks_cleared"), sem("hid_turned"), sem("hid_kept")
    acc_cleared = sem("acc_cleared")
    logits_made, shifted, exped, cw_ready, cw_turned, cwT_ready, cw_stored, cw_spread = (
        sem(n) for n in ("logits_made", "shifted", "exped", "cw_ready", "cw_turned", "cwT_ready", "cw_stored",
                         "cw_spread"))
    hid_made, bent, hid_scaled, hid_high, hid_ready, down_made, units_added = (
        sem(n) for n in ("hid_made", "bent", "hid_scaled", "hid_high", "hid_ready", "down_made", "units_added"))
    weighted = sem("weighted")
    gated, ple_done = sem("gated"), sem("ple_done")

    chunks = []
    last_user = [None] * SLOTS
    uses = [0] * SLOTS
    next_place = [0]
    splits = []
    unit_at = []
    unit_waits = []

    def chunk(view_of, src, n_places, user):
        at = next_place[0]
        places = list(range(at, at + n_places))
        next_place[0] = (at + n_places) % SLOTS
        waits = []
        for q in places:
            if last_user[q] is not None and last_user[q] not in waits:
                waits.append(last_user[q])
            last_user[q] = user
        uses[at] += 1
        view = view_of(ring[:, at * SLOT:(at + n_places) * SLOT])
        chunks.append(dict(view=view, src=src, waits=waits, landed=(landed[at], 16 * uses[at])))
        return chunks[-1]

    def units():
        stage = len(unit_at)
        unit_at.append(len(chunks))
        per = UNIT // SLOT
        waits = [[u for u in last_user[per * q:per * (q + 1)] if u] for q in range(RAW)]
        waits[RAW - 1].append((lin_made, splits[-1]["made"]))
        unit_waits.append(waits)
        for q in range(SLOTS):
            last_user[q] = (down_split, OPEN + UNITS * (stage + 1))
        next_place[0] = 0

    lins = []
    made = [0]
    took = {"act": 0, "dve": 0}

    def took_sem(engine):
        return act_took if engine == "act" else dve_took

    def linear(w, k, n_cols, operand, dest, kind, norm=None, norm_part=0):
        jobs = []
        wide = [512] * (n_cols // 512)
        if n_cols % 512:
            rest = n_cols % 512 + (wide.pop() if n_cols % 512 < 256 else 0)
            wide += [rest] if rest <= 512 else [rest // 2, rest - rest // 2]
        c0 = 0
        for width in wide:
            group = []
            for t in range(TILES):
                engine = "dve" if kind == "add" or (kind == "copy" and t == 1) else "act"
                took[engine] += 1
                group.append(dict(m=len(lins), width=width, t=t, operand=operand, dest=dest[:, t, c0:c0 + width],
                                  kind=kind, engine=engine, took=took[engine],
                                  scale=norm and norm["parts"][norm_part][3]["scale"][:, t:t + 1],
                                  rooted=norm and norm["rooted"] + norm_part + 1))
                lins.append(group[-1])
            numbers = []
            for kp in range(0, k, 2):
                number = len(splits)
                c = chunk(lambda x: x[:, 0:2 * width].rearrange("p (k n) -> p k n", k=2),
                          w.rearrange("(p k) n -> p k n", k=k)[:, kp:kp + 2, c0:c0 + width], 1,
                          (weights_split, number + 1))
                splits.append(dict(chunk=c, width=width, made=made[0] + TILES, stage=len(unit_at)))
                numbers.append(number)
                for t, job in enumerate(group):
                    job["made"] = made[0] + t + 1
                made[0] += TILES
            for job in group:
                job["splits"] = numbers
            jobs += group
            c0 += width
        return run(jobs)

    def run(jobs):
        for job in jobs:
            job["end"] = jobs[-1]["splits"][-1]
        return jobs

    turns = []
    turn_took = {"act": 0, "dve": 0}

    def turn(source, k, dests):
        jobs = []
        view = source.rearrange("p t (c k) -> p t k c", k=k)
        for j in range(0, k, 2):
            engines = ("act", "dve") if len(dests[0]) == 3 else (("act", "dve")[len(turns) % 2],)
            counts = {}
            for engine in engines:
                turn_took[engine] += 1
                counts[engine] = turn_took[engine]
            jobs.append(dict(m=len(turns), j=j, view=view, dests=dests, counts=counts))
            turns.append(jobs[-1])
        return jobs

    def turn_heads(view, n, dest, gain):
        d = dest.shape[0]
        jobs = []
        for j in range(0, n, 2):
            engine = ("act", "dve")[len(turns) % 2]
            turn_took[engine] += 1
            jobs.append(dict(m=len(turns), j=j, view=view, dests=[(dest, gain)], heads=d,
                             counts={engine: turn_took[engine]}))
            turns.append(jobs[-1])
        return jobs

    roots = []
    stat_at = [0]

    def root(n, dim, n_part=P):
        w = stat_at[0]
        stat_at[0] += 6 * n
        v = [stat[0:n_part, w + i * n:w + (i + 1) * n] for i in range(6)]
        roots.append(dict(m=len(roots), sum=v[0], root=v[1], mean=v[2], tmp=v[3], first=v[4], scale=v[5], dim=dim))
        return roots[-1]

    def heads(view, n, d):
        return view.rearrange("p t (h d) -> p t h d", d=d)

    def scales(r, lo, n):
        return r["scale"].rearrange("p (t h) -> p t h", t=TILES)[:, :, lo:lo + n]

    norms = []

    def norm(sources, late=False):
        n = dict(m=len(norms), parts=[(s, d, w, root(TILES, w)) for s, d, w in sources], late=late,
                 sums=sum(len(x["parts"]) for x in norms) * TILES,
                 scaled=sum(len(x["parts"]) for x in norms if not x["late"]) * TILES,
                 rooted=sum(len(x["parts"]) for x in norms))
        norms.append(n)
        return n

    n_mix = norm([(h, rows, D_MODEL)], late=True)
    t_mix = turn(h, KB, [(x_high, gains["norm_mix_g"], x_low)])
    x_parts = (x_high, x_low)
    l_in = linear(a["w_in"], KB, IN_WIDTH, x_parts, proj, "copy", n_mix)
    n_lat = norm([(proj[:, :, 1536:2304], rows[:, :, 0:Q_RANK], Q_RANK),
                  (proj[:, :, 2304:2560], rows[:, :, Q_RANK:Q_RANK + KV_RANK], KV_RANK)], late=True)
    t_cq = turn(proj[:, :, 1536:2304], 6, [(x_high[:, 0:6, :], gain_cq, x_low[:, 0:6, :])])
    t_ckv = turn(proj[:, :, 2304:2560], 2, [(x_high[:, 6:8, :], gain_ckv, x_low[:, 6:8, :])])
    l_uq = linear(a["w_uq"], 6, Q_RANK, x_parts, qb, "copy", n_lat, 0)
    l_ukv = linear(a["w_ukv"], 2, 1024, (x_high[:, 6:8, :], x_low[:, 6:8, :]), kvb, "copy",
                   n_lat, 1)
    run(l_in + l_uq + l_ukv)
    r_a = root(32, DIM_A)
    r_bq = root(16, DIM_B)
    r_bk = root(16, DIM_B)
    qa, ka, vb_q, vb_k = (heads(x, 8, d) for x, d in ((proj[:, :, 0:512], 64), (proj[:, :, 512:1024], 64), (qb, 96),
                                                      (kb, 96)))
    qaT, kaT, qbT, kbT = turned_heads(0, 8, 64), turned_heads(8, 8, 64), turned_heads(16, 8, 96), turned_heads(24, 8, 96)
    t_a = turn_heads(qa, 8, qaT, head_gain[:, 0:1]) + turn_heads(ka, 8, kaT, head_gain[:, 1:2])
    t_b = turn_heads(vb_q, 8, qbT, None) + turn_heads(vb_k, 8, kbT, None)
    t_mix1 = turn(mix, KB, [(x_high, None, x_low)])
    l_o = linear(a["w_o"], KB, D_MODEL, x_parts, h, "add")
    n_ffn = norm([(h, rows, D_MODEL)], late=True)
    t_ffn = turn(h, KB, [(x_high, gains["norm_ffn_g"], x_low)])

    units()

    n_nsa = norm([(h, rows, D_MODEL)], late=True)
    t_nsa = turn(h, KB, [(x_high, gains["ln_mix0"], x_low)])
    l_nsa = linear(a["a_w_in_2"][0], KB, NSA_WIDTH, x_parts, proj, "copy", n_nsa)
    next_place[0] = 0
    cmp_chunks = [chunk(lambda x: x.rearrange("p (j n) -> p j n", j=16),
                        a[w][0].rearrange("(j p) n -> p j n", p=P), 4, (cmp_hid_made, i + 1))
                  for i, w in enumerate(("a_ck_w1_2", "a_cv_w1_2"))]
    r_nq, r_nk = root(32, DIM), root(16, DIM)
    r_kc = root(4, DIM, CMP_PAD)
    nq = heads(proj[:, :, 0:1024], 16, 64)
    nks, nkw = (heads(proj[:, :, at:at + 256], 4, 64) for at in (1536, 2048))
    nqT, nksT, nkwT = turned_heads(0, 16, 64), turned_heads(16, 4, 64), turned_heads(20, 4, 64)
    t_nq = turn_heads(nq, 16, nqT, head_gain[:, 2:3])
    t_nk = turn_heads(nks, 4, nksT, head_gain[:, 4:5]) + turn_heads(nkw, 4, nkwT, head_gain[:, 5:6])
    t_mix2 = turn(mix, KB, [(x_high, None, x_low)])
    l_nsa_o = linear(a["a_w_out_2"][0], KB, D_MODEL, x_parts, h, "add")

    n_moe, t_moe = [None, None], [None, None]
    n_ple, t_ple, t_embed, l_embed, l_gate = ([None, None] for _ in range(5))

    def moe_and_ple(layer):
        n_moe[layer] = norm([(h, rows, D_MODEL)])
        t_moe[layer] = turn(rows, KB, [(turned_x, gains[f"ln_ffn{layer}"])])
        units()
        t_embed[layer] = turn(embed[:, layer], 2, [(embed_high, None, embed_low)])
        l_embed[layer] = linear(a["ple_w_proj_2"][layer], 2, D_MODEL, (embed_high, embed_low), ple_y, "copy")
        n_ple[layer] = norm([(h, rows, D_MODEL)], late=True)
        t_ple[layer] = turn(h, KB, [(x_high, gains[f"ln_ple{layer}"], x_low)])
        l_gate[layer] = linear(a["ple_w_gate_2"][layer], KB, D_MODEL, x_parts, ple_gate, "gate", n_ple[layer])
        run(l_embed[layer] + l_gate[layer])

    moe_and_ple(0)
    n_moba = norm([(h, rows, D_MODEL)], late=True)
    t_kv = turn(h, KB, [(kv_high, gains["kv_norm"], kv_low)])
    t_moba = turn(h, KB, [(x_high, gains["ln_mix1"], x_low)])
    l_kv = linear(a["w_kv_shared_2"], KB, 512, (kv_high, kv_low), moba_kv, "copy", n_moba)
    l_q = linear(a["b_w_q_2"][0], KB, D_MODEL, x_parts, moba_q, "copy", n_moba)
    run(l_kv + l_q)
    r_mk, r_mq = root(8, DIM), [root(16, DIM), root(16, DIM)]
    mq = heads(moba_q, 16, 64)
    mk = heads(moba_kv[:, :, 0:256], 4, 64)
    mqT, mkT = turned_heads(0, 16, 64), turned_heads(16, 4, 64)
    t_mk = turn_heads(mk, 4, mkT, head_gain[:, 7:8])
    t_mq = [turn_heads(mq[:, :, 8 * g:8 * g + 8, :], 8, mqT[:, 8 * g:8 * g + 8], head_gain[:, 6:7]) for g in range(2)]
    t_mix3 = turn(mix, KB, [(x_high, None, x_low)])
    l_moba_o = linear(a["b_w_out_2"][0], KB, D_MODEL, x_parts, h, "add")
    moe_and_ple(1)
    assert stat_at[0] <= 1400

    n_heads, n_links = [0], [0]

    def attention(cores):
        s = dict(first=n_heads[0], cores=cores, heads=[x for c in cores for x in c["heads"]])
        n_heads[0] += len(s["heads"])
        return s

    def core(heads_here, at, gate=None, add=False):
        return dict(heads=heads_here, at=at, gate=gate, add=add)

    att_a = attention([core([dict(q=qaT[:, h_], k=kaT[:, h_], v=(proj, 1024 + 64 * h_), bias="toep", head=h_)
                             for h_ in range(c, c + 4)], c) for c in (0, 4)])
    att_b = attention([core([dict(q=qbT[:, h_], k=kbT[:, h_], v=(kvb, 64 + 128 * h_), bias="causal", head=h_)
                             for h_ in range(c, c + 4)], 8 + c) for c in (0, 4)])
    att_n = attention([core([dict(q=nqT[:, 4 * g + r], k=kT[:, g], v=(proj, v_at + 64 * g), bias="alibi",
                                  head=4 * g + r) for r in range(4)], 4 * g, gate, gate == 2)
                       for g in range(KV_HEADS) for kT, v_at, gate in ((nksT, 1792, 1), (nkwT, 2304, 2))])
    att_m = attention([core([dict(q=mqT[:, 4 * g + r], k=mkT[:, g],
                                  v=(moba_kv, 256 + 64 * g), bias="alibi", head=4 * g + r) for r in range(4)], 4 * g)
                       for g in range(KV_HEADS)])

    small = []

    def load_small(dest, src):
        small.append((dest, src))

    for name, src in (("norm_ffn_g", a["norm_ffn_g"]),
                      ("ln_mix0", a["ln_mix_2"][0]), ("ln_ffn0", a["ln_ffn_2"][0]), ("ln_ple0", a["ln_ple_2"][0]),
                      ("kv_norm", a["kv_norm_2"]), ("ln_mix1", a["ln_mix_2"][1]), ("ln_ffn1", a["ln_ffn_2"][1]),
                      ("ln_ple1", a["ln_ple_2"][1])):
        load_small(gains[name][:, :], src.rearrange("(p k) -> p k", k=KB))
    load_small(gain_cq[:, :], a["cq_norm_g"].rearrange("(p k) -> p k", k=6))
    load_small(gain_ckv[:, :], a["ckv_norm_g"].rearrange("(p k) -> p k", k=2))
    for i, src in enumerate((a["qnorm_a_g"], a["knorm_a_g"], a["a_q_norm_2"][0], a["a_k_norm_2"][0, 0],
                             a["a_k_norm_2"][0, 1], a["a_k_norm_2"][0, 2], a["b_q_norm_2"][0],
                             a["k_norm_shared_2"])):
        load_small(head_gain[:, i:i + 1], src.unsqueeze(1))
    load_small(gain_bq[:, :], a["qnorm_b_g"].partition_broadcast(P))
    load_small(gain_bk[:, :], a["knorm_b_g"].partition_broadcast(P))
    for i, (pos, w2) in enumerate((("a_ck_pos_2", "a_ck_w2_2"), ("a_cv_pos_2", "a_cv_w2_2"))):
        load_small(pos_rows[:, i, :], a[pos][0].rearrange("(j l) d -> j (l d)", l=2))
        load_small(cmp_w2[:, i], a[w2][0].rearrange("(c p) n -> p c n", p=P))
    for i in range(2):
        load_small(route_w[:, i, :, 0:4], a["moe_w_group_2"][i].rearrange("(p k) n -> p k n", k=KB))
        load_small(route_w[:, i, :, 4:36], a["moe_w_expert_2"][i].rearrange("(p k) n -> p k n", k=KB))
        load_small(route_b[:, i, 0:4], a["moe_b_group_2"][i].partition_broadcast(P))
        load_small(route_b[:, i, 4:36], a["moe_b_expert_2"][i].partition_broadcast(P))
        load_small(embed[:, i], a["p_2"][i, 0].rearrange("(t p) n -> p t n", p=P))
    load_small(rel[:, :], a["rel_bias"])
    load_small(pos_i[:, :], a["positions"][0].rearrange("(t p) -> p t", p=P))

    def wait_small(eng):
        eng.wait_ge(small_loaded, 16 * len(small))

    def wait_table(eng):
        eng.wait_ge(table_loaded, 32)

    def act_norm(act, n):
        for i, (src, dest, width, r) in enumerate(n["parts"]):
            for t in range(TILES):
                nc.scalar.activation(dest[:, t, :], src[:, t, :], ACT.Square,
                                     accum_out=r["sum"][:, t:t + 1]).then_inc(squares_summed, 1)
            act.wait_ge(squares_summed, n["sums"] + TILES * (i + 1))
            act_root(act, r)
            if not n["late"]:
                act.wait_ge(rooted, n["rooted"] + i + 1)
                nc.scalar.activation(dest[:, 1, :], src[:, 1, :], ACT.Copy,
                                     scale=r["scale"][:, 1:2]).then_inc(rows_scaled, 1)

    def act_root(act, r):
        nc.scalar.activation(r["root"], r["sum"], ACT.Sqrt, scale=1.0 / r["dim"],
                             bias=eps[0:r["sum"].shape[0], 0:1]).then_inc(roots_taken, 1)

    dve_steps = [0]

    def dve_link(dve, ins):
        dve_steps[0] += 1
        ins.then_inc(dve_step, 1)
        dve.wait_ge(dve_step, dve_steps[0])

    def dve_root(dve, r, signal=None):
        dve.wait_ge(roots_taken, r["m"] + 1)
        dve_link(dve, nc.vector.reciprocal(r["first"], r["root"]))
        dve_link(dve, nc.vector.tensor_scalar(r["mean"], r["sum"], 1.0 / r["dim"], EPS, ALU.mult, ALU.add))
        dve_link(dve, nc.vector.tensor_tensor(r["tmp"], r["first"], r["first"], ALU.mult))
        dve_link(dve, nc.vector.tensor_tensor(r["mean"], r["tmp"], r["mean"], ALU.mult))
        dve_link(dve, nc.vector.tensor_scalar(r["tmp"], r["mean"], -0.5, 1.5, ALU.mult, ALU.add))
        last = nc.vector.tensor_tensor(r["scale"], r["first"], r["tmp"], ALU.mult)
        if signal is None:
            dve_link(dve, last)
        else:
            last.then_inc(signal, 1)

    def dve_norm(dve, n):
        for i, (src, dest, _, r) in enumerate(n["parts"]):
            dve_root(dve, r, rooted)
            if not n["late"]:
                dve.wait_ge(rooted, n["rooted"] + i + 1)
                nc.vector.tensor_scalar(dest[:, 0, :], src[:, 0, :], r["scale"][:, 0:1], None,
                                        ALU.mult).then_inc(rows_scaled, 1)

    def pe_turn(pe, jobs):
        for j in jobs:
            if j["m"] >= 4:
                before = turns[j["m"] - 4]["counts"]
                last = "dve" if "dve" in before else "act"
                pe.wait_ge(dve_turned if last == "dve" else act_turned, before[last])
            b = 4 + j["m"] % 4
            for kk in range(2):
                for t in range(TILES):
                    mm = nc.tensor.transpose(bank[0:j.get("heads", P), b, kk * 256 + t * P:kk * 256 + (t + 1) * P],
                                             j["view"][:, t, j["j"] + kk, :], ident)
            mm.then_inc(turned, 1)

    def take_turn(eng, jobs, engine):
        for j in jobs:
            if engine not in j["counts"]:
                continue
            eng.wait_ge(turned, j["m"] + 1)
            b = 4 + j["m"] % 4
            split = len(j["dests"][0]) == 3
            if split and engine == "dve":
                eng.wait_ge(act_turned, j["counts"]["act"])
            if "heads" in j:
                d = j["heads"]
                (dest, gain), = j["dests"]
                src, to = bank[0:d, b, :], dest[:, j["j"]:j["j"] + 2, :].rearrange("p h n -> p (h n)")
                if engine == "act":
                    last = nc.scalar.copy(to, src) if gain is None else nc.scalar.activation(to, src, ACT.Copy,
                                                                                             scale=gain)
                else:
                    last = (nc.vector.tensor_copy(to, src) if gain is None else
                            nc.vector.tensor_scalar(to, src, gain, None, ALU.mult))
                last.then_inc(act_turned if engine == "act" else dve_turned, 1)
                continue
            for d in j["dests"]:
                dest, gain = d[0], d[1]
                if gain is None:
                    src = bank[:, b, :].rearrange("p (k n) -> p k n", k=2)
                    to = dest[:, j["j"]:j["j"] + 2, :]
                    if engine == "act":
                        last = nc.scalar.copy(to, src)
                    elif split:
                        last = nc.vector.tensor_tensor(d[2][:, j["j"]:j["j"] + 2, :], src, to, ALU.subtract)
                    else:
                        last = nc.vector.tensor_copy(to, src)
                    continue
                for kk in range(2):
                    k = j["j"] + kk
                    src = bank[:, b, kk * 256:kk * 256 + 256]
                    if engine == "act":
                        last = nc.scalar.activation(dest[:, k, :], src, ACT.Copy, scale=gain[:, k:k + 1])
                    elif split:
                        last = nc.vector.scalar_tensor_tensor(out=d[2][:, k, :], in0=src, scalar=gain[:, k:k + 1],
                                                              in1=dest[:, k, :], op0=ALU.mult, op1=ALU.subtract)
                    else:
                        last = nc.vector.tensor_scalar(dest[:, k, :], src, gain[:, k:k + 1], None, ALU.mult)
            last.then_inc(act_turned if engine == "act" else dve_turned, 1)

    def wait_turned(eng, jobs):
        for engine, s in (("act", act_turned), ("dve", dve_turned)):
            n = max((j["counts"].get(engine, 0) for j in jobs), default=0)
            if n:
                eng.wait_ge(s, n)

    def pe_linear(pe, jobs):
        for group in zip(jobs[0::2], jobs[1::2]):
            for c, number in enumerate(group[0]["splits"]):
                pe.wait_ge(weights_split, number + 1)
                for j in group:
                    if c == 0 and j["m"] >= 4:
                        before = lins[j["m"] - 4]
                        pe.wait_ge(took_sem(before["engine"]), before["took"])
                    n = j["width"]
                    at = (j["t"] * P, (j["t"] + 1) * P)
                    for kk in range(2):
                        for i, (x, w) in enumerate(((HIGH, HIGH), (HIGH, LOW), (LOW, HIGH))):
                            mm = nc.tensor.matmul(bank[:, j["m"] % 4, 0:n], j["operand"][x][:, 2 * c + kk, at[0]:at[1]],
                                                  weight_parts[:, number % PAIRS, w, kk * n:(kk + 1) * n],
                                                  start=c == kk == i == 0,
                                                  stop=c == len(j["splits"]) - 1 and kk == 1 and i == 2)
                    mm.then_inc(lin_made, 1)

    def split(eng, number, engine):
        x = splits[number]
        n = 2 * x["width"]
        raw_weights = x["chunk"]["view"].rearrange("p k n -> p (k n)")
        high, low = (weight_parts[:, number % PAIRS, w, 0:n] for w in (HIGH, LOW))
        if engine == "act":
            eng.wait_ge(*x["chunk"]["landed"])
            if number >= PAIRS:
                eng.wait_ge(lin_made, splits[number - PAIRS]["made"])
            if x["stage"] and (number < PAIRS or splits[number - PAIRS]["stage"] < x["stage"]):
                eng.wait_ge(down_made, OPEN + UNITS * x["stage"])
            nc.scalar.copy(high, raw_weights).then_inc(weights_high, 1)
        else:
            eng.wait_ge(weights_high, number + 1)
            nc.vector.tensor_tensor(low, raw_weights, high, ALU.subtract).then_inc(weights_split, 1)

    def split_first(eng, jobs, engine, lo=0, hi=PAIRS):
        first = jobs[0]["splits"][0]
        for number in range(first + lo, min(first + hi, jobs[0]["end"] + 1)):
            split(eng, number, engine)

    def take_linear(eng, jobs, engine):
        for group in zip(jobs[0::2], jobs[1::2]):
            for number in group[0]["splits"]:
                if number + PAIRS <= group[0]["end"]:
                    split(eng, number + PAIRS, engine)
            for j in group:
                if j["engine"] != engine:
                    continue
                eng.wait_ge(lin_made, j["made"])
                if j["rooted"]:
                    eng.wait_ge(rooted, j["rooted"])
                src = bank[:, j["m"] % 4, 0:j["width"]]
                if j["kind"] == "add":
                    nc.vector.tensor_tensor(j["dest"], j["dest"], src, ALU.add).then_inc(dve_took, 1)
                elif j["kind"] == "gate":
                    nc.scalar.activation(j["dest"], src, ACT.Sigmoid, scale=j["scale"]).then_inc(act_took, 1)
                elif j["rooted"] and engine == "act":
                    nc.scalar.activation(j["dest"], src, ACT.Copy, scale=j["scale"]).then_inc(act_took, 1)
                elif j["rooted"]:
                    nc.vector.tensor_scalar(j["dest"], src, j["scale"], None, ALU.mult).then_inc(dve_took, 1)
                elif engine == "act":
                    nc.scalar.copy(j["dest"], src).then_inc(act_took, 1)
                else:
                    nc.vector.tensor_copy(j["dest"], src).then_inc(dve_took, 1)

    def wait_took(eng, jobs):
        for engine in ("act", "dve"):
            n = max((j["took"] for j in jobs if j["engine"] == engine), default=0)
            if n:
                eng.wait_ge(took_sem(engine), n)

    def scale_heads(engine, view, scale, signal):
        n, d = view.shape[2], view.shape[3]
        for t in range(TILES):
            last = engine.tensor_tensor(view[:, t], view[:, t], scale[:, t].unsqueeze(2).to_broadcast([P, n, d]),
                                        ALU.mult)
        last.then_inc(signal, 1)

    def pe_attention(pe, s, compressed=False):
        def scores(n, x):
            if n >= 4:
                pe.wait_ge(biased, n - 3)
            nc.tensor.matmul(bank[:, n % 4, 0:P], x["q"][:, 0:P], x["k"][:, 0:P], start=True, stop=True)
            nc.tensor.matmul(bank[:, n % 4, P:SPAN], x["q"][:, P:2 * P], x["k"], start=True,
                             stop=True).then_inc(scores_made, 1)

        def turn_probs(n):
            pe.wait_ge(probs_made, n + 1)
            if n >= 2:
                pe.wait_ge(probT_ready, n - 1)
            for q in range(3):
                mm = nc.tensor.transpose(bank[:, 4 + n % 2, q * P:(q + 1) * P], prob[:, n % 4, q * P:(q + 1) * P],
                                         ident)
            mm.then_inc(probs_turned, 1)

        def values(n, x):
            pe.wait_ge(probT_ready, n + 1)
            if n % 4 == 0 and n:
                pe.wait_ge(mixed, n // 4)
            v, at = x["v"]
            for t, q, kt, start, stop in ((0, 0, 0, True, True), (1, 1, 0, True, False), (1, 2, 1, False, True)):
                mm = nc.tensor.matmul(bank[:, 6 + t, (n % 4) * P:(n % 4 + 1) * P], probT[:, n % 2, q * P:(q + 1) * P],
                                      v[:, kt, at - 64:at + 64], start=start, stop=stop)
            mm.then_inc(values_made, 1)

        first, here = s["first"], s["heads"]
        for j in range(len(here) + 3):
            if j < len(here):
                scores(first + j, here[j])
            if 0 <= j - 2 < len(here):
                turn_probs(first + j - 2)
            if 0 <= j - 3:
                values(first + j - 3, here[j - 3])
            if compressed and j == len(here):
                pe_turn_compressed(pe)

    flat_mix = mix[:, :, :].rearrange("p t n -> p (t n)")

    def dve_latent_sums(dve):
        dve.wait_ge(squared, 4)
        nc.vector.tensor_reduce(r_bq["sum"], flat_mix[:, 0:1536].rearrange("p (h d) -> p h d", d=96), AX.X,
                                ALU.add).then_inc(sums_ready, 1)
        nc.vector.tensor_reduce(stat[:, 1390:1392], flat_mix[:, 1536:1600].rearrange("p (h d) -> p h d", d=32), AX.X,
                                ALU.add)
        dve_link(dve, nc.vector.tensor_reduce(r_bk["sum"], rows[:, 0, :].rearrange("p (h d) -> p h d", d=64), AX.X,
                                              ALU.add))
        by_tile = r_bk["sum"].rearrange("p (t h) -> p t h", t=TILES)
        nc.vector.tensor_tensor(by_tile, by_tile, stat[:, 1390:1392].unsqueeze(2).to_broadcast([P, TILES, 8]),
                                ALU.add).then_inc(sums_ready, 1)
        dve.wait_ge(sums_ready, 3)

    def act_attention(act, s, compressed=False, latent=False):
        def exps(n):
            act.wait_ge(maxed, n + 1)
            if n >= 4:
                act.wait_ge(probs_turned, n - 3)
            for t, (lo, hi) in enumerate(((0, P), (P, SPAN))):
                at = t * 4 + n % 4
                last = nc.scalar.activation(prob[:, n % 4, lo:hi], logit[:, n % 4, lo:hi], ACT.Exp,
                                            bias=neg_max[:, n % 4, t:t + 1],
                                            accum_out=total[:, n // 4 % 2, at:at + 1])
            last.then_inc(probs_made, 1)

        def take_probs(n):
            act.wait_ge(probs_turned, n + 1)
            if n >= 2:
                act.wait_ge(values_made, n - 1)
            nc.scalar.copy(probT[:, n % 2, :], bank[:, 4 + n % 2, 0:SPAN]).then_inc(probT_ready, 1)

        first, count = s["first"], len(s["heads"])
        for j in range(count + 1):
            if j < count:
                exps(first + j)
            if j:
                take_probs(first + j - 1)
            if latent and j == 2:
                act.wait_ge(sums_ready, 3)
                act_root(act, r_bq)
                act_root(act, r_bk)
            if compressed and j == 3:
                act.wait_ge(c_shifted, 1)
                nc.scalar.activation(cl[:, :, :, :], cl[:, :, :, :], ACT.Exp).then_inc(c_exped, 1)

    def dve_attention(dve, s, compressed=False, latent=False):
        def bias(n, x):
            dve.wait_ge(scores_made, n + 1)
            if n >= 4:
                dve.wait_ge(probs_made, n - 3)
            src, to = bank[:, n % 4, 0:SPAN], logit[:, n % 4, :]
            if x["bias"] == "toep":
                ins = nc.vector.scalar_tensor_tensor(out=to, in0=src, scalar=DIM_A ** -0.5,
                                                     in1=toep[:, x["head"], :], op0=ALU.mult, op1=ALU.add)
            elif x["bias"] == "causal":
                ins = nc.vector.scalar_tensor_tensor(out=to, in0=src, scalar=DIM_B ** -0.5, in1=const("causal"),
                                                     op0=ALU.mult, op1=ALU.add)
            else:
                ins = nc.vector.scalar_tensor_tensor(out=to, in0=const("dist"),
                                                     scalar=const("neg_slope")[:, x["head"]:x["head"] + 1], in1=src,
                                                     op0=ALU.mult, op1=ALU.add)
            ins.then_inc(biased, 1)
            dve.wait_ge(biased, n + 1)
            nc.vector.tensor_reduce(neg_max[:, n % 4, 0:1], logit[:, n % 4, 0:P], AX.X, ALU.max, negate=True)
            nc.vector.tensor_reduce(neg_max[:, n % 4, 1:2], logit[:, n % 4, P:SPAN], AX.X, ALU.max,
                                    negate=True).then_inc(maxed, 1)

        def link(ins):
            n_links[0] += 1
            ins.then_inc(mix_step, 1)
            dve.wait_ge(mix_step, n_links[0])

        def mix_core(number, c):
            dve.wait_ge(probs_made, 4 * (number + 1))
            link(nc.vector.reciprocal(share[:, :], total[:, number % 2, :]))
            share4 = share[:, :].rearrange("p (t h) -> p t h", t=TILES)
            if c["gate"] is not None:
                link(nc.vector.tensor_tensor(share4, share4, gates[:, :, c["at"]:c["at"] + 4, c["gate"]], ALU.mult))
            shares = share4.unsqueeze(3).to_broadcast([P, TILES, 4, 64])
            here = mix.rearrange("p t (h d) -> p t h d", d=64)[:, :, c["at"]:c["at"] + 4, :]
            dve.wait_ge(values_made, 4 * (number + 1))
            to = part[:, :, :].rearrange("p (t h) d -> p t h d", t=TILES) if c["add"] else here
            nc.vector.tensor_tensor(to, value_banks[:, :, :, 1, :], shares, ALU.mult).then_inc(mixed, 1)
            dve.wait_ge(mixed, number + 1)
            if c["add"]:
                link(nc.vector.tensor_tensor(here, here, to, ALU.add))

        first, here = s["first"], s["heads"]
        for j in range(len(here) + 3):
            if j < len(here):
                bias(first + j, here[j])
            if j >= 6 and j % 4 == 2:
                mix_core(first // 4 + (j - 6) // 4, s["cores"][(j - 6) // 4])
            if latent and j == 1:
                dve_latent_sums(dve)
            if latent and j == 3:
                dve_root(dve, r_bq, scale_ready)
                dve_root(dve, r_bk, scale_ready)
            if compressed and j == 1:
                dve_shift_compressed(dve)
            if compressed and j == 4:
                dve_weigh_compressed(dve)

    def pe_compressed_scores(pe):
        for g in range(KV_HEADS):
            for t in range(TILES):
                for r in range(4):
                    mm = nc.tensor.matmul(bank[:, 2 * g + t, r * P:(r + 1) * P], nqT[:, 4 * g + r, t * P:(t + 1) * P],
                                          kcT[:, g * CMP_PAD:g * CMP_PAD + P], start=True, stop=True)
            mm.then_inc(c_scores, 1)

    def pe_turn_compressed(pe):
        pe.wait_ge(c_probs, 1)
        pe.wait_ge(biased, att_m["first"])
        for x in range(4):
            mm = nc.tensor.transpose(bank[:, 0, x * P:(x + 1) * P],
                                     cl[:, x % 2, 8 * (x // 2):8 * (x // 2) + 8, :].rearrange("p h n -> p (h n)"), ident)
        mm.then_inc(c_turned, 1)

    def pe_compressed_values(pe):
        pe.wait_ge(cT_ready, 1)
        for x in range(4):
            nc.tensor.matmul(bank[:, (x + 1) % 4, :], cT[:, x, :], own_values[:, x // 2, :], start=True,
                             stop=True).then_inc(c_values, 1)

    def act_compressed(act):
        act.wait_ge(c_turned, 1)
        nc.scalar.copy(cT[:, :, :].rearrange("p x n -> p (x n)"), bank[:, 0, :]).then_inc(cT_ready, 1)

    def dve_take_compressed_scores(dve):
        for g in range(KV_HEADS):
            dve.wait_ge(c_scores, g + 1)
            nc.vector.tensor_tensor(cl[:, :, 4 * g:4 * g + 4, :],
                                    bank[:, 2 * g:2 * g + 2, :].rearrange("p t (r n) -> p t r n", r=4)[:, :, :, 0:CMP_PAD],
                                    const("cmp_bias").rearrange("p (g t r n) -> p g t r n", g=4, t=2, r=4)[:, g],
                                    ALU.add).then_inc(c_scored, 1)

    def dve_shift_compressed(dve):
        dve.wait_ge(c_scored, KV_HEADS)
        rows_ = cl[:, :, :, :].rearrange("p t h n -> p (t h) n")
        dve_link(dve, nc.vector.tensor_reduce(c_share[:, :], rows_, AX.X, ALU.max))
        nc.vector.tensor_tensor(rows_, rows_, c_share[:, :].unsqueeze(2).to_broadcast([P, TILES * HEADS, CMP_PAD]),
                                ALU.subtract).then_inc(c_shifted, 1)

    def dve_weigh_compressed(dve):
        rows_ = cl[:, :, :, :].rearrange("p t h n -> p (t h) n")
        dve.wait_ge(c_exped, 1)
        for t in range(TILES):
            valid = const("cmp_valid")[:, t * CMP_PAD:(t + 1) * CMP_PAD]
            last = nc.vector.tensor_tensor(cl[:, t], cl[:, t], valid.unsqueeze(1).to_broadcast([P, HEADS, CMP_PAD]),
                                           ALU.mult)
        dve_link(dve, last)
        dve_link(dve, nc.vector.tensor_reduce(c_share[:, :], rows_, AX.X, ALU.add))
        dve_link(dve, nc.vector.tensor_scalar(c_share[:, :], c_share[:, :], 1e-30, None, ALU.max))
        dve_link(dve, nc.vector.reciprocal(c_share[:, :], c_share[:, :]))
        by_tile = c_share[:, :].rearrange("p (t h) -> p t h", t=TILES)
        dve_link(dve, nc.vector.tensor_tensor(by_tile, by_tile, gates[:, :, :, 0], ALU.mult))
        nc.vector.tensor_tensor(rows_, rows_, c_share[:, :].unsqueeze(2).to_broadcast([P, TILES * HEADS, CMP_PAD]),
                                ALU.mult).then_inc(c_probs, 1)

    def dve_mix_compressed(dve):
        for x in range(4):
            dve.wait_ge(c_values, x + 1)
            here = mix[:, x % 2, 512 * (x // 2):512 * (x // 2) + 512]
            nc.vector.tensor_tensor(here, here, bank[:, (x + 1) % 4, :], ALU.add).then_inc(c_taken, 1)

    def pe_clear(pe, n):
        for q in range(4):
            mm = nc.tensor.matmul(bank[:, q, :], zeros[0:32, 0:P], zeros[0:32, :], start=True, stop=False,
                                  skip_group_check=True)
        mm.then_inc(acc_cleared, 1)

    def in_width(s):
        return 1024 if s == 0 else 2048

    def unit_slot(u):
        return u % RAW, u // RAW + 1

    def in_landed_at(s, u):
        place_of, uses = unit_slot(u)
        per_stage = (UNITS - place_of + RAW - 1) // RAW
        return sum(per_stage * in_width(q) // 64 for q in range(s)) + uses * in_width(s) // 64

    def down_landed_at(s, u):
        place_of, uses = unit_slot(u)
        return 16 * (s * ((UNITS - place_of + RAW - 1) // RAW) + uses)

    def sp_units(sp, s):
        if s == 0:
            w_in = [a["w_ff1"].rearrange("(p k) (u n) -> p u k n", k=KB, n=P)]
            w_down = a["w_ff2"].rearrange("(u p) n -> p u n", p=P)
        else:
            w_in = [a[w][s - 1].rearrange("e (p k) f -> p e k f", k=KB) for w in ("moe_w_gate_2", "moe_w_up_2")]
            w_down = a["moe_w_down_2"][s - 1].rearrange("e p n -> p e n")

        def load_in(at, u):
            for q, w in enumerate(w_in):
                sp.dma_start(raw[:, at, q * 1024:(q + 1) * 1024].rearrange("p (k n) -> p k n", k=KB),
                             w[:, u]).then_inc(in_landed[at], 16)

        def load_down(at, u):
            sp.dma_start(raw[:, at, 2048:3072], w_down[:, u, :]).then_inc(down_landed[at], 16)

        def free_slot(at):
            for wait in unit_waits[s][at]:
                sp.wait_ge(*wait)

        for at in range(RAW):
            free_slot(at)
            load_in(at, at)
            if at < RAW - 1:
                load_down(at, at)
        with sp.Fori(0, 9) as i:
            for u in range(RAW):
                sp.wait_ge(in_split, UNITS * s + u + 1 + i * RAW)
                load_in(u, i * RAW + (u + RAW))
                sp.wait_ge(down_split, OPEN + UNITS * s + u + i * RAW)
                load_down((u + 2) % RAW, i * RAW + (u + 2))
        for u in (27, 28):
            sp.wait_ge(in_split, UNITS * s + u + 1)
            load_in(u % RAW, u + RAW)
            sp.wait_ge(down_split, OPEN + UNITS * s + u)
            load_down((u + 2) % RAW, u + 2)
        sp.wait_ge(down_split, OPEN + UNITS * s + 29)
        load_down(31 % RAW, 31)

    BODY, ROUNDS = 6, 5

    def step_in(s):
        return BODY // RAW * in_width(s) // 64, BODY // RAW * 16

    def pe_in(pe, s, u, i=0):
        b = 4 + u % 2
        pe.wait_ge(in_split, UNITS * s + u + 1 + i * BODY)
        if u >= 2:
            pe.wait_ge(hid_scaled, UNITS * s + u - 1 + i * BODY)
        for q in range(in_width(s) // 1024):
            for k in range(KB):
                for n, (w, x) in enumerate(((HIGH, x_high), (HIGH, x_low), (LOW, x_high))):
                    mm = nc.tensor.matmul(bank[:, b, q * 256:(q + 1) * 256],
                                          parts[:, u % 2, w, q * 1024 + k * P:q * 1024 + (k + 1) * P], x[:, k, :],
                                          start=k == 0 and n == 0, stop=k == KB - 1 and n == 2)
        mm.then_inc(hid_made, 1)

    def pe_down(pe, s, u, i=0):
        pe.wait_ge(down_split, OPEN + UNITS * s + u + 1 + i * BODY)
        pe.wait_ge(hid_ready, UNITS * s + u + 1 + i * BODY)
        for t in range(TILES):
            for x, w in ((HIGH, HIGH), (HIGH, LOW), (LOW, HIGH)):
                for half in range(2):
                    mm = nc.tensor.matmul(bank[:, 2 * t + half, :], hid_parts[:, u % 2, x, t * P:(t + 1) * P],
                                          parts[:, u % 2, w, 2048 + half * 512:2048 + (half + 1) * 512],
                                          start=False, stop=False, skip_group_check=True)
        mm.then_inc(down_made, 1)

    def pe_units(pe, s):
        with pe.Fori(0, ROUNDS) as i:
            for u in range(BODY):
                pe_in(pe, s, u + 1, i)
                pe_down(pe, s, u, i)
        for u in range(ROUNDS * BODY, UNITS):
            if u + 1 < UNITS:
                pe_in(pe, s, u + 1)
            pe_down(pe, s, u)

    def bent_rows(u):
        return junk[:, 256 + (u % 2) * 256:512 + (u % 2) * 256]

    def act_high_in(act, s, u, i=0):
        act.wait_ge(in_landed[u % RAW], in_landed_at(s, u) + i * step_in(s)[0])
        nc.scalar.copy(parts[:, u % 2, HIGH, 0:in_width(s)], raw[:, u % RAW, 0:in_width(s)]).then_inc(in_high, 1)

    def act_high_down(act, s, u, i=0):
        act.wait_ge(down_landed[u % RAW], down_landed_at(s, u) + i * step_in(s)[1])
        act.wait_ge(down_made, OPEN + UNITS * s + u - 1 + i * BODY)
        nc.scalar.copy(parts[:, u % 2, HIGH, 2048:3072], raw[:, u % RAW, 2048:3072]).then_inc(down_high, 1)

    def act_first_units(act, s):
        act_high_in(act, s, 0)
        act_high_down(act, s, 0)
        act_high_in(act, s, 1)

    def act_units(act, s):
        def step(u, i=0, last=UNITS):
            act.wait_ge(hid_made, UNITS * s + u + 1 + i * BODY)
            nc.scalar.activation(bent_rows(u), bank[:, 4 + u % 2, 0:256],
                                 ACT.Relu if s == 0 else ACT.Silu).then_inc(bent, 1)
            if u + 2 < last:
                act_high_in(act, s, u + 2, i)
            if u + 1 < last:
                act_high_down(act, s, u + 1, i)

        with act.Fori(0, ROUNDS) as i:
            for u in range(BODY):
                step(u, i)
        for u in range(ROUNDS * BODY, UNITS):
            step(u)

    def dve_low_in(dve, s, u, i=0):
        dve.wait_ge(in_high, UNITS * s + u + 1 + i * BODY)
        n = in_width(s)
        nc.vector.tensor_tensor(parts[:, u % 2, LOW, 0:n], raw[:, u % RAW, 0:n], parts[:, u % 2, HIGH, 0:n],
                                ALU.subtract).then_inc(in_split, 1)

    def dve_low_down(dve, s, u, i=0):
        dve.wait_ge(down_high, UNITS * s + u + 1 + i * BODY)
        nc.vector.tensor_tensor(parts[:, u % 2, LOW, 2048:3072], raw[:, u % RAW, 2048:3072],
                                parts[:, u % 2, HIGH, 2048:3072], ALU.subtract).then_inc(down_split, 1)

    def dve_units(dve, s):
        def step(u, i=0):
            dve.wait_ge(bent, UNITS * s + u + 1 + i * BODY)
            rows_here = bent_rows(u)
            if s == 0:
                nc.vector.tensor_tensor(rows_here, rows_here, rows_here, ALU.mult).then_inc(hid_scaled, 1)
                dve.wait_ge(hid_scaled, UNITS * s + u + 1 + i * BODY)
            else:
                if isinstance(i, int) or u % 2 == 0:
                    dve.wait_ge(cw_spread, 16 * (UNITS // 2 * (s - 1) + u // 2 + 1) + i * (16 * BODY // 2))
                nc.vector.tensor_tensor(rows_here, rows_here, bank[:, 4 + u % 2, 256:512],
                                        ALU.mult).then_inc(hid_scaled, 1)
                dve.wait_ge(hid_scaled, UNITS * s + u + 1 + i * BODY)
                dve_scaled = nc.vector.tensor_tensor(rows_here, rows_here, token_weight[:, i * BODY + u, :], ALU.mult)
                dve_scaled.then_inc(weighted, 1)
                dve.wait_ge(weighted, UNITS * (s - 1) + u + 1 + i * BODY)
            dve.wait_ge(down_made, OPEN + UNITS * s + u - 1 + i * BODY)
            nc.vector.tensor_copy(hid_parts[:, u % 2, HIGH, :], rows_here).then_inc(hid_high, 1)
            dve.wait_ge(hid_high, UNITS * s + u + 1 + i * BODY)
            nc.vector.tensor_tensor(hid_parts[:, u % 2, LOW, :], rows_here, hid_parts[:, u % 2, HIGH, :],
                                    ALU.subtract).then_inc(hid_ready, 1)
            if u + 2 < UNITS:
                dve_low_in(dve, s, u + 2, i)
            if u + 1 < UNITS:
                dve_low_down(dve, s, u + 1, i)

        with dve.Fori(0, ROUNDS) as i:
            for u in range(BODY):
                step(u, i)
        for u in range(ROUNDS * BODY, UNITS):
            step(u)
        scale = None
        if s == 0:
            r = n_ffn["parts"][0][3]
            dve.wait_ge(rooted, n_ffn["rooted"] + 1)
            dve_link(dve, nc.vector.tensor_tensor(r["mean"], r["scale"], r["scale"], ALU.mult))
            scale = r["mean"]
        dve.wait_ge(down_made, OPEN + UNITS * (s + 1))
        for t in range(TILES):
            for half in range(2):
                cols = h[:, t, half * 512:(half + 1) * 512]
                if scale is None:
                    ins = nc.vector.tensor_tensor(cols, cols, bank[:, 2 * t + half, :], ALU.add)
                else:
                    ins = nc.vector.scalar_tensor_tensor(out=cols, in0=bank[:, 2 * t + half, :],
                                                         scalar=scale[:, t:t + 1], in1=cols, op0=ALU.mult, op1=ALU.add)
                ins.then_inc(units_added, 1)

    def wait_units_added(eng, s):
        eng.wait_ge(units_added, 4 * (s + 1))

    def act_split_rows(act, jobs, s):
        wait_turned(act, jobs)
        nc.scalar.copy(x_high[:, :, :], turned_x[:, :, :]).then_inc(x_high_made, 1)

    def dve_split_rows(dve, s):
        dve.wait_ge(x_high_made, s)
        nc.vector.tensor_tensor(x_low[:, :, :], turned_x[:, :, :], x_high[:, :, :], ALU.subtract).then_inc(x_split, 1)

    def pool_spread(pool, layer):
        pool.wait_ge(cwT_ready, layer + 1)
        pool.dma_start(cw_dram[layer], cwT[:, :]).then_inc(cw_stored, 16)
        pool.wait_ge(cw_stored, 16 * (layer + 1))
        src = cw_dram[layer].rearrange("e n -> (e n)")
        with pool.Fori(0, EXPERTS // 2) as i:
            pool.dma_start(arena[:, ds(i * (2 * TOKENS), 2 * TOKENS)],
                           src[ds(i * (2 * TOKENS), 2 * TOKENS)].partition_broadcast(P)).then_inc(cw_spread, 16)
            pool.wait_ge(cw_spread, 16 * (EXPERTS // 2 * layer + 1) + i * 16)

    def pe_route(pe, layer):
        for t in range(TILES):
            for k in range(KB):
                mm = nc.tensor.matmul(bank[:, 6, t * 64:t * 64 + 36], turned_x[:, k, t * P:(t + 1) * P],
                                      route_w[:, layer, k, :], start=k == 0, stop=k == KB - 1)
        mm.then_inc(logits_made, 1)

    def pe_turn_weights(pe, layer):
        pe.wait_ge(cw_ready, layer + 1)
        for t in range(TILES):
            mm = nc.tensor.transpose(bank[0:32, 7, t * P:(t + 1) * P], cw[:, t, :], ident)
        mm.then_inc(cw_turned, 1)

    def act_route(act, layer):
        for q, (lo, hi) in enumerate(((40, 44), (48, 56))):
            act.wait_ge(shifted, 2 * layer + q + 1)
            nc.scalar.activation(rt[:, :, lo + 20:hi + 20], rt[:, :, lo:hi], ACT.Exp).then_inc(exped, 1)
        act.wait_ge(cw_turned, layer + 1)
        nc.scalar.copy(cwT[:, :], bank[0:32, 7, 0:256]).then_inc(cwT_ready, 1)

    def dve_route(dve, layer):
        v = nc.vector

        def link(ins):
            dve_link(dve, ins)

        def c1(at):
            return rt[:, :, at]

        def wide(x, n):
            return x.unsqueeze(2).to_broadcast([P, TILES, n])

        dve.wait_ge(logits_made, layer + 1)
        link(v.tensor_tensor(rt[:, :, 0:36], bank[:, 6, 0:128].rearrange("p (t n) -> p t n", t=TILES)[:, :, 0:36],
                             route_b[:, layer, :].unsqueeze(1).to_broadcast([P, TILES, 36]), ALU.add))
        link(v.tensor_reduce(c1(36), rt[:, :, 0:4], AX.X, ALU.max))
        v.tensor_tensor(rt[:, :, 40:44], rt[:, :, 0:4], wide(c1(36), 4), ALU.subtract).then_inc(shifted, 1)
        dve.wait_ge(exped, 2 * layer + 1)
        group_p = rt[:, :, 60:64]
        link(v.tensor_reduce(c1(37), group_p, AX.X, ALU.add))
        link(v.reciprocal(c1(38), c1(37)))

        def first_best(values, best, n, rank, out_at, tmp_at):
            tmp, hot = rt[:, :, tmp_at:tmp_at + n], rt[:, :, out_at:out_at + n]
            link(v.tensor_tensor(tmp, values, wide(best, n), ALU.is_equal))
            link(v.tensor_tensor(tmp, tmp, rank.unsqueeze(1).to_broadcast([P, TILES, n]), ALU.mult))
            link(v.tensor_reduce(c1(39), tmp, AX.X, ALU.max))
            link(v.tensor_tensor(hot, tmp, wide(c1(39), n), ALU.is_equal))
            return hot

        link(v.tensor_reduce(c1(45), group_p, AX.X, ALU.max))
        group_hot = first_best(group_p, c1(45), 4, const("rank4"), 80, 84)
        for t in range(TILES):
            link(v.tensor_tensor(rt[:, t, 96:128].rearrange("p (g j) -> p g j", g=4),
                                 rt[:, t, 4:36].rearrange("p (g j) -> p g j", g=4),
                                 group_hot[:, t].unsqueeze(2).to_broadcast([P, 4, 8]), ALU.mult))
            link(v.tensor_reduce(rt[:, t, 88:96], rt[:, t, 96:128].rearrange("p (g j) -> p j g", g=4), AX.X, ALU.add))
        link(v.tensor_reduce(c1(46), rt[:, :, 88:96], AX.X, ALU.max))
        v.tensor_tensor(rt[:, :, 48:56], rt[:, :, 88:96], wide(c1(46), 8), ALU.subtract).then_inc(shifted, 1)
        dve.wait_ge(exped, 2 * layer + 2)
        e = rt[:, :, 68:76]
        link(v.tensor_reduce(c1(47), e, AX.X, ALU.max))
        hot1 = first_best(e, c1(47), 8, const("rank8"), 128, 136)
        link(v.scalar_tensor_tensor(out=rt[:, :, 144:152], in0=hot1, scalar=-4.0, in1=e, op0=ALU.mult, op1=ALU.add))
        link(v.tensor_reduce(c1(56), rt[:, :, 144:152], AX.X, ALU.max))
        hot2 = first_best(rt[:, :, 144:152], c1(56), 8, const("rank8"), 152, 160)
        link(v.tensor_tensor(c1(57), c1(47), c1(56), ALU.add))
        link(v.reciprocal(c1(57), c1(57)))
        link(v.tensor_tensor(c1(57), c1(57), c1(38), ALU.mult))
        link(v.tensor_tensor(c1(58), c1(57), c1(56), ALU.mult))
        link(v.tensor_tensor(c1(57), c1(57), c1(47), ALU.mult))
        link(v.tensor_tensor(hot1, hot1, wide(c1(57), 8), ALU.mult))
        link(v.tensor_tensor(hot2, hot2, wide(c1(58), 8), ALU.mult))
        link(v.tensor_tensor(hot1, hot1, hot2, ALU.add))
        for t in range(TILES):
            last = v.tensor_tensor(cw[:, t, :].rearrange("p (g j) -> p g j", g=4),
                                   group_hot[:, t].unsqueeze(2).to_broadcast([P, 4, 8]),
                                   hot1[:, t].unsqueeze(1).to_broadcast([P, 4, 8]), ALU.mult)
        last.then_inc(cw_ready, 1)

    def pe_moe_and_ple(pe, layer):
        wait_took(pe, l_nsa_o if layer == 0 else l_moba_o)
        pe_clear(pe, layer + 1)
        pe.wait_ge(rows_scaled, n_moe[layer]["scaled"] + 2)
        pe_turn(pe, t_moe[layer])
        wait_turned(pe, t_moe[layer])
        pe_route(pe, layer)
        pe.wait_ge(x_split, layer + 1)
        pe_in(pe, layer + 1, 0)
        pe_turn_weights(pe, layer)
        pe_units(pe, layer + 1)
        pe_turn(pe, t_embed[layer])
        wait_units_added(pe, layer + 1)
        pe_turn(pe, t_ple[layer])
        wait_turned(pe, t_embed[layer])
        pe_linear(pe, l_embed[layer])
        wait_turned(pe, t_ple[layer])
        pe_linear(pe, l_gate[layer])

    def act_moe_and_ple(act, layer):
        act_norm(act, n_moe[layer])
        take_turn(act, t_moe[layer], "act")
        act_split_rows(act, t_moe[layer], layer + 1)
        act_first_units(act, layer + 1)
        act_route(act, layer)
        act_units(act, layer + 1)
        split_first(act, l_embed[layer], "act", 0, 2)
        take_turn(act, t_embed[layer], "act")
        split_first(act, l_embed[layer], "act", 2)
        take_turn(act, t_ple[layer], "act")
        take_linear(act, l_embed[layer], "act")
        wait_units_added(act, layer + 1)
        act_norm(act, n_ple[layer])
        take_linear(act, l_gate[layer], "act")
        act.wait_ge(ple_done, 4 * (layer + 1))

    def dve_moe_and_ple(dve, layer):
        dve_norm(dve, n_moe[layer])
        take_turn(dve, t_moe[layer], "dve")
        dve_split_rows(dve, layer + 1)
        dve_low_in(dve, layer + 1, 0)
        dve_route(dve, layer)
        dve_low_in(dve, layer + 1, 1)
        dve_low_down(dve, layer + 1, 0)
        dve_units(dve, layer + 1)
        take_turn(dve, t_embed[layer], "dve")
        split_first(dve, l_embed[layer], "dve", 0, 2)
        take_turn(dve, t_ple[layer], "dve")
        split_first(dve, l_embed[layer], "dve", 2)
        take_linear(dve, l_embed[layer], "dve")
        wait_units_added(dve, layer + 1)
        dve_norm(dve, n_ple[layer])
        wait_took(dve, l_embed[layer])
        for g in range(2):
            take_linear(dve, l_gate[layer][2 * g:2 * g + 2], "dve")
            cols = slice(g * 512, (g + 1) * 512)
            for t in range(TILES):
                wait_took(dve, l_gate[layer][2 * g + t:2 * g + t + 1])
                nc.vector.tensor_tensor(ple_tmp[:, t, cols], ple_gate[:, t, cols], ple_y[:, t, cols],
                                        ALU.mult).then_inc(gated, 1)
                dve.wait_ge(gated, 4 * layer + 2 * g + t + 1)
                nc.vector.tensor_tensor(h[:, t, cols], h[:, t, cols], ple_tmp[:, t, cols], ALU.add).then_inc(ple_done, 1)
        dve.wait_ge(ple_done, 4 * (layer + 1))

    block = ctx.enter_context(nc.Block())

    def sp_chunk(sp, n):
        c = chunks[n]
        for wait in c["waits"]:
            sp.wait_ge(*wait)
        sp.dma_start(c["view"], c["src"]).then_inc(c["landed"][0], 16)

    @block.sync
    def _(sp):
        for t in range(TILES):
            sp.dma_start(h[:, t, :], a["x"][0, t * P:(t + 1) * P, :]).then_inc(x_loaded, 16)
        for n in range(unit_at[0]):
            sp_chunk(sp, n)
        sp_units(sp, 0)
        for n in range(unit_at[0], unit_at[1]):
            sp_chunk(sp, n)
        sp_units(sp, 1)
        for n in range(unit_at[1], unit_at[2]):
            sp_chunk(sp, n)
        sp_units(sp, 2)
        for n in range(unit_at[2], len(chunks)):
            sp_chunk(sp, n)
        for t in range(TILES):
            sp.wait_ge(ple_done, 7 + t)
            sp.dma_start(out[0, t * P:(t + 1) * P, :], h[:, t, :]).then_inc(stored, 16)
        sp.wait_ge(stored, 32)

    @block.gpsimd
    def _(pool):
        steps = [0]

        def link(ins):
            steps[0] += 1
            ins.then_inc(pool_step, 1)
            pool.wait_ge(pool_step, steps[0])

        g = nc.gpsimd
        g.memset(zeros[:, :], 0.0)
        g.memset(kcT[:, 64:], 0.0)
        g.memset(eps[:, :], EPS).then_inc(cleared, 1)
        for dest, src in small:
            pool.dma_start(dest, src, allow_slow_non_contiguous=True).then_inc(small_loaded, 16)

        pool.wait_ge(bias_row_ready, 1)
        pool.dma_start(toep_dram.rearrange("(h p n) -> h p n", h=HEADS_A, p=P),
                       bias_row[:, :].unsqueeze(1).to_broadcast([HEADS_A, P, SPAN])).then_inc(toep_spread, 16)
        pool.wait_ge(toep_spread, 16)
        pool.dma_start(toep[:, :, P:SPAN], bass.AP(toep_dram.tensor, 127, [[SPAN - 1, P], [P * SPAN, HEADS_A], [1, 256]])
                       ).then_inc(toep_ready, 16)
        pool.dma_start(toep[:, :, 0:P], bass.AP(toep_dram.tensor, 255, [[SPAN - 1, P], [P * SPAN, HEADS_A], [1, P]])
                       ).then_inc(toep_ready, 16)

        wait_took(pool, l_ukv)
        pool.wait_ge(squared, 4)
        pool.wait_ge(sums_ready, 1)
        pool.wait_ge(sines_ready, 2)
        wait_small(pool)
        q4, k4, kv4 = heads(qb, 8, 96), heads(kb, 8, 96), heads(kvb, 8, 128)
        sine, cosine = rope[:, 6], rope[:, 7]
        for t in range(TILES):
            g.tensor_tensor(k4[:, t, :, 0:NOPE], kv4[:, t, :, 0:NOPE],
                            gain_bk[:, 0:NOPE].unsqueeze(1).to_broadcast([P, 8, NOPE]), ALU.mult)
            g.tensor_tensor(rope_k[:, t, :], proj[:, t, 2560:2592], gain_bk[:, NOPE:DIM_B], ALU.mult)
            link(g.tensor_tensor(q4[:, t], q4[:, t], gain_bq[:, :].unsqueeze(1).to_broadcast([P, 8, DIM_B]), ALU.mult))
            for x1, x2, n in ((q4[:, t, :, NOPE:NOPE + 16], q4[:, t, :, NOPE + 16:DIM_B], 8),
                              (rope_k[:, t, 0:16].unsqueeze(1), rope_k[:, t, 16:32].unsqueeze(1), 1)):
                cos = cosine[:, t].unsqueeze(1).to_broadcast([P, n, 16])
                sin = sine[:, t].unsqueeze(1).to_broadcast([P, n, 16])
                tmp = rope_tmp[:, :, 0:n, :]
                g.tensor_tensor(tmp[:, 0], x1, cos, ALU.mult)
                g.tensor_tensor(tmp[:, 1], x2, sin, ALU.mult)
                g.tensor_tensor(tmp[:, 2], x2, cos, ALU.mult)
                link(g.tensor_tensor(tmp[:, 3], x1, sin, ALU.mult))
                g.tensor_tensor(x1, tmp[:, 0], tmp[:, 1], ALU.subtract)
                link(g.tensor_tensor(x2, tmp[:, 2], tmp[:, 3], ALU.add))
            link(g.tensor_copy(k4[:, t, :, NOPE:DIM_B], rope_k[:, t].unsqueeze(1).to_broadcast([P, 8, ROPE])))
        pool.wait_ge(scale_ready, 3)
        scale_heads(g, heads(qb, 8, 96), scales(r_bq, 0, 8), pool_scaled)
        scale_heads(g, heads(kb, 8, 96), scales(r_bk, 0, 8), pool_scaled)

        wait_took(pool, l_nsa[:6])
        g.memset(blocks[0], 0.0)
        g.memset(blocks[1], 0.0).then_inc(blocks_cleared, 1)
        for i in range(2):
            for t in range(TILES):
                src = proj[:, t, 1024 + 256 * i:1280 + 256 * i].rearrange("p (g d) -> p g d", d=64)
                last = g.tensor_copy(rows[:, i, t * 512:(t + 1) * 512].rearrange("p (g x d) -> p g x d", g=4, x=2),
                                     src.unsqueeze(2).to_broadcast([P, 4, 2, 64]))
            last.then_inc(doubled, 1)
        pool.wait_ge(scale_ready, 5)
        scale_heads(g, nks, scales(r_nk, 0, 4), pool_scaled)
        scale_heads(g, nkw, scales(r_nk, 4, 4), pool_scaled)
        pool_spread(pool, 0)
        pool.wait_ge(scale_ready, 6)
        scale_heads(g, mk, scales(r_mk, 0, 4), pool_scaled)
        pool_spread(pool, 1)

    @block.tensor
    def _(pe):
        pe.sem_inc(down_made, OPEN)
        pe.wait_ge(cleared, 1)
        wait_table(pe)
        pe.wait_ge(x_loaded, 32)
        pe_turn(pe, t_mix)
        wait_turned(pe, t_mix)
        pe_linear(pe, l_in[:4])
        wait_small(pe)
        nc.tensor.matmul(bank[0:HEADS_A, 4, 0:SPAN], rel[:, :], const("onehot", 32), start=True,
                         stop=True).then_inc(bias_row_made, 1)
        for i in range(2):
            mm = nc.tensor.transpose(bank[:, 5, i * 16:(i + 1) * 16], pos_rows[:, i, :], ident[0:16, 0:16])
        mm.then_inc(pos_turned, 1)
        pe_linear(pe, l_in[4:])
        pe.wait_ge(bias_row_ready, 1)
        pe.wait_ge(pos_ready, 1)
        wait_took(pe, l_in)
        pe_turn(pe, t_cq)
        pe_turn(pe, t_ckv)
        wait_turned(pe, t_cq + t_ckv)
        pe_linear(pe, l_uq)
        pe_linear(pe, l_ukv)
        pe.wait_ge(dve_scaled, 2)
        pe_turn(pe, t_a)
        wait_turned(pe, t_a)
        wait_took(pe, l_ukv)
        pe_attention(pe, att_a)
        pe.wait_ge(pool_scaled, 2)
        pe.wait_ge(probT_ready, att_b["first"])
        pe.wait_ge(mixed, att_b["first"] // 4)
        pe_turn(pe, t_b)
        wait_turned(pe, t_b)
        pe_attention(pe, att_b)
        pe.wait_ge(mixed, att_n["first"] // 4)
        pe_turn(pe, t_mix1)
        wait_turned(pe, t_mix1)
        pe_linear(pe, l_o)
        wait_took(pe, l_o)
        pe_turn(pe, t_ffn)
        pe_clear(pe, 0)
        wait_turned(pe, t_ffn)
        pe_in(pe, 0, 0)
        pe_units(pe, 0)
        wait_units_added(pe, 0)
        pe_turn(pe, t_nsa)
        wait_turned(pe, t_nsa)
        pe_linear(pe, l_nsa)
        wait_took(pe, l_nsa)
        for i in range(2):
            pe.wait_ge(doubled, i + 1)
            for gr in range(4):
                for t in range(TILES):
                    mm = nc.tensor.transpose(
                        bank[:, 2 * i + gr // 2, (gr % 2) * 256 + t * P:(gr % 2) * 256 + (t + 1) * P],
                        rows[:, i, t * 512 + gr * P:t * 512 + (gr + 1) * P], ident)
            mm.then_inc(cmp_turned, 1)
        pe.wait_ge(dve_scaled, 3)
        pe_turn(pe, t_nq)
        for i in range(2):
            w1 = cmp_chunks[i]["view"]
            pe.wait_ge(*cmp_chunks[i]["landed"])
            pe.wait_ge(blocks_made, i + 1)
            for j in range(16):
                mm = nc.tensor.matmul(bank[0:64, 2 * i, 0:256], blocks[i][:, j, :, :].rearrange("p g n -> p (g n)"),
                                      w1[:, j, :], start=j == 0, stop=j == 15)
            mm.then_inc(cmp_hid_made, 1)
        pe.wait_ge(pool_scaled, 4)
        pe_turn(pe, t_nk)
        for i in range(2):
            pe.wait_ge(gelu_done, i + 1)
            for c in range(2):
                mm = nc.tensor.transpose(bank[:, 2 * i + 1, c * 64:(c + 1) * 64], hid_rows[:, i, c * P:(c + 1) * P],
                                         ident[0:64, 0:64])
            mm.then_inc(hid_turned, 1)
        for i in range(2):
            pe.wait_ge(hid_kept, i + 1)
            for gr in range(4):
                for c in range(2):
                    mm = nc.tensor.matmul(bank[0:CMP_PAD, 2 * i, gr * 64:(gr + 1) * 64],
                                          cmp_hid[:, i, c, gr * CMP_PAD:(gr + 1) * CMP_PAD], cmp_w2[:, i, c, :],
                                          start=c == 0, stop=c == 1)
            mm.then_inc(cmp_out_made, 1)
        pe.wait_ge(cmp_rows_ready, 1)
        for gr in range(4):
            mm = nc.tensor.transpose(bank[0:64, 1, gr * CMP_PAD:(gr + 1) * CMP_PAD], cmp_kv[:, 0, gr, :],
                                     ident[0:CMP_PAD, 0:CMP_PAD])
        mm.then_inc(kc_turned, 1)
        nc.tensor.matmul(bank[:, 3, 0:256], const("spread", CMP_PAD), cmp_rows[:, 256:512], start=True,
                         stop=True).then_inc(spread_made, 1)
        pe.wait_ge(kcT_ready, 1)
        pe.wait_ge(own_ready, 2)
        wait_turned(pe, t_nq + t_nk)
        pe_compressed_scores(pe)
        pe.wait_ge(c_scored, KV_HEADS)
        pe_attention(pe, att_n, compressed=True)
        pe_compressed_values(pe)
        pe.wait_ge(c_taken, 4)
        pe_turn(pe, t_mix2)
        wait_turned(pe, t_mix2)
        pe_linear(pe, l_nsa_o)
        pe_moe_and_ple(pe, 0)
        pe.wait_ge(ple_done, 4)
        pe_turn(pe, t_kv)
        pe_turn(pe, t_moba)
        wait_turned(pe, t_kv)
        pe_linear(pe, l_kv)
        wait_turned(pe, t_moba)
        pe_linear(pe, l_q)
        wait_took(pe, l_kv + l_q)
        pe.wait_ge(pool_scaled, 5)
        pe_turn(pe, t_mk)
        for g in range(2):
            pe.wait_ge(dve_scaled, 4 + g)
            pe_turn(pe, t_mq[g])
        wait_turned(pe, t_mk + t_mq[0] + t_mq[1])
        pe_attention(pe, att_m)
        pe.wait_ge(mixed, n_heads[0] // 4)
        pe_turn(pe, t_mix3)
        wait_turned(pe, t_mix3)
        pe_linear(pe, l_moba_o)
        pe_moe_and_ple(pe, 1)

    @block.scalar
    def _(act):
        def squares(dest, src, last=False):
            ins = nc.scalar.activation(dest, src, ACT.Square)
            if last:
                ins.then_inc(squared, 1)

        act.dma_start(table[:, :], a["table"]).then_inc(table_loaded, 16)
        act.dma_start(gains["norm_mix_g"][:, :], a["norm_mix_g"].rearrange("(p k) -> p k", k=KB),
                      allow_slow_non_contiguous=True).then_inc(table_loaded, 16)
        act.wait_ge(cleared, 1)
        act.wait_ge(x_loaded, 32)
        wait_table(act)
        take_turn(act, t_mix, "act")
        split_first(act, l_in, "act")
        act_norm(act, n_mix)
        take_linear(act, l_in[:8], "act")
        act.wait_ge(angle_ready, 1)
        nc.scalar.activation(rope[:, 6], rope[:, 4], ACT.Sin).then_inc(sines_ready, 1)
        nc.scalar.activation(rope[:, 7], rope[:, 5], ACT.Sin).then_inc(sines_ready, 1)
        wait_small(act)
        act.wait_ge(gains_scaled, 2)
        take_linear(act, l_in[8:], "act")
        wait_took(act, l_in)
        take_turn(act, t_cq, "act")
        take_turn(act, t_ckv, "act")
        act_norm(act, n_lat)
        for t in range(TILES):
            squares(rows[:, t], proj[:, t, 0:1024], last=t == 1)
        act.wait_ge(sums_ready, 1)
        act_root(act, r_a)
        take_linear(act, l_uq, "act")
        take_linear(act, l_ukv, "act")
        take_turn(act, t_a, "act")
        wait_took(act, l_uq + l_ukv)
        act.wait_ge(toep_spread, 16)
        squares(flat_mix[:, 0:1536], arena[:, 5248:6784], last=True)
        for t in range(TILES):
            squares(rows[:, 0, t * 512:(t + 1) * 512].rearrange("p (h d) -> p h d", d=64),
                    heads(kvb, 8, 128)[:, t, :, 0:NOPE], last=t == 1)
        squares(flat_mix[:, 1536:1600].rearrange("p (t d) -> p t d", t=TILES), proj[:, :, 2560:2592], last=True)
        act_attention(act, att_a, latent=True)
        take_turn(act, t_b, "act")
        act_attention(act, att_b)
        split_first(act, l_o, "act", 0, 1)
        take_turn(act, t_mix1, "act")
        split_first(act, l_o, "act", 1)
        take_linear(act, l_o, "act")
        wait_took(act, l_o)
        take_turn(act, t_ffn, "act")
        act_first_units(act, 0)
        act_norm(act, n_ffn)
        act_units(act, 0)
        split_first(act, l_nsa, "act", 0, 1)
        take_turn(act, t_nsa, "act")
        split_first(act, l_nsa, "act", 1)
        wait_units_added(act, 0)
        act_norm(act, n_nsa)
        take_linear(act, l_nsa[:4], "act")
        wait_took(act, l_nsa[:4])
        for t in range(TILES):
            squares(mix[:, t], proj[:, t, 0:1024], last=t == 1)
        take_linear(act, l_nsa[4:8], "act")
        act.wait_ge(sums_ready, 4)
        act_root(act, r_nq)
        take_linear(act, l_nsa[8:], "act")
        take_turn(act, t_nq, "act")
        wait_took(act, l_nsa)
        for t in range(TILES):
            for q, c0 in enumerate((1536, 2048)):
                squares(work[:, q * 512 + t * 256:q * 512 + t * 256 + 256], proj[:, t, c0:c0 + 256],
                        last=t == 1 and q == 1)
        nc.scalar.activation(gates[:, :, :, :].rearrange("p t h b -> p t (h b)"), proj[:, :, 2560:2608],
                             ACT.Sigmoid).then_inc(gates_ready, 1)
        act.wait_ge(sums_ready, 5)
        act_root(act, r_nk)
        for i in range(2):
            act.wait_ge(cmp_hid_made, i + 1)
            nc.scalar.activation(hid_rows[:, i, :], bank[0:64, 2 * i, 0:256], ACT.Gelu_apprx_tanh).then_inc(gelu_done, 1)
        take_turn(act, t_nk, "act")
        for i in range(2):
            act.wait_ge(hid_turned, i + 1)
            nc.scalar.copy(cmp_hid[:, i].rearrange("p c n -> p (c n)"), bank[:, 2 * i + 1, 0:128]).then_inc(hid_kept, 1)
        act.wait_ge(sums_ready, 6)
        act_root(act, r_kc)
        act_attention(act, att_n, compressed=True)
        act_compressed(act)
        act.wait_ge(c_values, 4)
        split_first(act, l_nsa_o, "act", 0, 1)
        take_turn(act, t_mix2, "act")
        split_first(act, l_nsa_o, "act", 1)
        take_linear(act, l_nsa_o, "act")
        wait_took(act, l_nsa_o)
        act_moe_and_ple(act, 0)
        split_first(act, l_kv, "act", 0, 2)
        take_turn(act, t_kv, "act")
        split_first(act, l_kv, "act", 2)
        take_turn(act, t_moba, "act")
        act_norm(act, n_moba)
        take_linear(act, l_kv, "act")
        wait_took(act, l_kv)
        for t in range(TILES):
            squares(work[:, t * 256:(t + 1) * 256], moba_kv[:, t, 0:256], last=t == 1)
        take_linear(act, l_q[0:2], "act")
        act.wait_ge(sums_ready, 7)
        act_root(act, r_mk)
        for g in range(2):
            if g:
                take_turn(act, t_mk, "act")
            wait_took(act, l_q[2 * g:2 * g + 2])
            for t in range(TILES):
                squares(rows[:, g, t * 512:(t + 1) * 512], moba_q[:, t, g * 512:(g + 1) * 512], last=t == 1)
            act.wait_ge(sums_ready, 8 + g)
            act_root(act, r_mq[g])
            if g == 0:
                take_linear(act, l_q[2:4], "act")
        take_turn(act, t_mq[0], "act")
        take_turn(act, t_mq[1], "act")
        act_attention(act, att_m)
        split_first(act, l_moba_o, "act", 0, 1)
        take_turn(act, t_mix3, "act")
        split_first(act, l_moba_o, "act", 1)
        take_linear(act, l_moba_o, "act")
        wait_took(act, l_moba_o)
        act_moe_and_ple(act, 1)

    @block.vector
    def _(dve):
        v = nc.vector

        def link(ins):
            dve_link(dve, ins)

        dve.sem_inc(down_split, OPEN)
        dve.wait_ge(x_loaded, 32)
        wait_table(dve)
        take_turn(dve, t_mix, "dve")
        split_first(dve, l_in, "dve")
        dve_norm(dve, n_mix)
        take_linear(dve, l_in[:4], "dve")
        wait_small(dve)
        dve.wait_ge(bias_row_made, 1)
        v.tensor_tensor(bias_row[:, :], bank[0:HEADS_A, 4, 0:SPAN], const("log_count", HEADS_A),
                        ALU.add).then_inc(bias_row_ready, 1)
        dve.wait_ge(pos_turned, 1)
        v.tensor_copy(cmp_pos[:, :, :].rearrange("p i j -> p (i j)"), bank[:, 5, 0:32]).then_inc(pos_ready, 1)
        for col in (2, 6):
            v.tensor_scalar(head_gain[:, col:col + 1], head_gain[:, col:col + 1], DIM ** -0.5, None,
                            ALU.mult).then_inc(gains_scaled, 1)
        link(v.tensor_copy(posf[:, :], pos_i[:, :]))
        for t in range(TILES):
            last = v.tensor_scalar(rope[:, 0, t], const("inv_freq"), posf[:, t:t + 1], None, ALU.mult)
        link(last)
        magic = 12582912.0
        p1 = 6.28125
        p2 = float(np.float32(2 * math.pi - p1))
        p2 = float(np.frombuffer((np.float32(p2).view(np.uint32) & np.uint32(0xFFFFF000)).tobytes(), np.float32)[0])
        p3 = float(np.float32(2 * math.pi - p1 - p2))
        link(v.tensor_scalar(rope[:, 1], rope[:, 0], 1 / (2 * math.pi), magic, ALU.mult, ALU.add))
        link(v.tensor_scalar(rope[:, 1], rope[:, 1], magic, None, ALU.subtract))
        for src, part_of, dest in ((0, p1, 2), (2, p2, 3), (3, p3, 2)):
            link(v.scalar_tensor_tensor(out=rope[:, dest], in0=rope[:, 1], scalar=-part_of, in1=rope[:, src],
                                        op0=ALU.mult, op1=ALU.add))
        link(v.tensor_scalar(rope[:, 4], rope[:, 2], 3.1415925, -3.1415925, ALU.min, ALU.max))
        link(v.scalar_tensor_tensor(out=rope[:, 3], in0=rope[:, 4], scalar=-1.0, in1=rope[:, 4], op0=ALU.mult,
                                    op1=ALU.max))
        v.tensor_scalar(rope[:, 5], rope[:, 3], -1.0, math.pi / 2, ALU.mult, ALU.add).then_inc(angle_ready, 1)
        take_linear(dve, l_in[4:], "dve")
        wait_took(dve, l_in)
        take_turn(dve, t_cq, "dve")
        take_turn(dve, t_ckv, "dve")
        dve_norm(dve, n_lat)
        dve.wait_ge(squared, 1)
        v.tensor_reduce(r_a["sum"], rows[:, :, :].rearrange("p t (h d) -> p (t h) d", d=64), AX.X,
                        ALU.add).then_inc(sums_ready, 1)
        dve_root(dve, r_a, scale_ready)
        dve.wait_ge(scale_ready, 1)
        scale_heads(v, qa, scales(r_a, 0, 8), dve_scaled)
        scale_heads(v, ka, scales(r_a, 8, 8), dve_scaled)
        take_linear(dve, l_uq, "dve")
        take_linear(dve, l_ukv, "dve")
        take_turn(dve, t_a, "dve")
        dve.wait_ge(toep_ready, 32)
        dve_attention(dve, att_a, latent=True)
        take_turn(dve, t_b, "dve")
        dve_attention(dve, att_b)
        split_first(dve, l_o, "dve", 0, 1)
        take_turn(dve, t_mix1, "dve")
        split_first(dve, l_o, "dve", 1)
        take_linear(dve, l_o, "dve")
        wait_took(dve, l_o)
        take_turn(dve, t_ffn, "dve")
        dve_low_in(dve, 0, 0)
        dve_low_down(dve, 0, 0)
        dve_low_in(dve, 0, 1)
        dve_norm(dve, n_ffn)
        dve_units(dve, 0)
        split_first(dve, l_nsa, "dve", 0, 1)
        take_turn(dve, t_nsa, "dve")
        split_first(dve, l_nsa, "dve", 1)
        wait_units_added(dve, 0)
        dve_norm(dve, n_nsa)
        take_linear(dve, l_nsa[:6], "dve")
        dve.wait_ge(squared, 5)
        v.tensor_reduce(r_nq["sum"], mix[:, :, :].rearrange("p t (h d) -> p (t h) d", d=64), AX.X,
                        ALU.add).then_inc(sums_ready, 1)
        take_linear(dve, l_nsa[6:8], "dve")
        dve_root(dve, r_nq, scale_ready)
        dve.wait_ge(scale_ready, 4)
        scale_heads(v, nq, scales(r_nq, 0, 16), dve_scaled)
        take_linear(dve, l_nsa[8:], "dve")
        dve.wait_ge(blocks_cleared, 1)
        for i in range(2):
            dve.wait_ge(cmp_turned, i + 1)
            for gr in range(4):
                for half in range(2):
                    lo = 64 * half
                    at = bank[lo:lo + 64, 2 * i + gr // 2, (gr % 2) * 256 + half:(gr % 2) * 256 + half + 1]
                    src = bass.AP(at.tensor, at.offset, [list(at.ap[0]), [2, 16], [16, N_CMP]])
                    last = v.tensor_tensor(blocks[i][lo:lo + 64, :, gr, 0:N_CMP], src,
                                           cmp_pos[lo:lo + 64, i, :].unsqueeze(2).to_broadcast([64, 16, N_CMP]),
                                           ALU.add)
            last.then_inc(blocks_made, 1)
            if i == 0:
                take_turn(dve, t_nq, "dve")
        dve.wait_ge(squared, 6)
        r3 = r_nk["sum"].rearrange("p (t h) -> p t h", t=TILES)
        for q in range(2):
            last = v.tensor_reduce(r3[:, :, 4 * q:4 * q + 4],
                                   work[:, q * 512:q * 512 + 512].rearrange("p (t h d) -> p t h d", t=TILES, d=64),
                                   AX.X, ALU.add)
        last.then_inc(sums_ready, 1)
        dve_root(dve, r_nk, scale_ready)
        take_turn(dve, t_nk, "dve")
        for i in range(2):
            dve.wait_ge(cmp_out_made, i + 1)
            link(v.tensor_copy(cmp_kv[:, i].rearrange("p g d -> p (g d)"), bank[0:CMP_PAD, 2 * i, 0:256]))
        link(v.tensor_tensor(cmp_sq[:, :, :], cmp_kv[:, 0], cmp_kv[:, 0], ALU.mult))
        v.tensor_reduce(r_kc["sum"], cmp_sq[:, :, :], AX.X, ALU.add).then_inc(sums_ready, 1)
        dve_root(dve, r_kc)
        v.tensor_tensor(cmp_kv[:, 0], cmp_kv[:, 0], r_kc["scale"].unsqueeze(2).to_broadcast([CMP_PAD, 4, 64]),
                        ALU.mult).then_inc(cmp_rows_ready, 1)
        dve.wait_ge(kc_turned, 1)
        v.tensor_scalar(kcT[:, 0:64], bank[0:64, 1, 0:64], head_gain[:, 3:4], None, ALU.mult).then_inc(kcT_ready, 1)
        dve.wait_ge(spread_made, 1)
        for o in range(2):
            values_here = bank[:, 3, o * P:(o + 1) * P].rearrange("p (g d) -> p g d", g=2)
            v.tensor_tensor(own_values[:, o, :].rearrange("p (g r d) -> p g r d", g=2, r=4),
                            values_here.unsqueeze(2).to_broadcast([P, 2, 4, 64]),
                            const("own").rearrange("p (g r) -> p g r", g=2).unsqueeze(3).to_broadcast([P, 2, 4, 64]),
                            ALU.mult).then_inc(own_ready, 1)
        dve_take_compressed_scores(dve)
        dve.wait_ge(gates_ready, 1)
        dve_attention(dve, att_n, compressed=True)
        dve_mix_compressed(dve)
        split_first(dve, l_nsa_o, "dve", 0, 1)
        take_turn(dve, t_mix2, "dve")
        split_first(dve, l_nsa_o, "dve", 1)
        take_linear(dve, l_nsa_o, "dve")
        wait_took(dve, l_nsa_o)
        dve_moe_and_ple(dve, 0)
        split_first(dve, l_kv, "dve", 0, 2)
        take_turn(dve, t_kv, "dve")
        split_first(dve, l_kv, "dve", 2)
        take_turn(dve, t_moba, "dve")
        dve_norm(dve, n_moba)
        take_linear(dve, l_kv, "dve")
        dve.wait_ge(squared, 7)
        v.tensor_reduce(r_mk["sum"], work[:, 0:512].rearrange("p (h d) -> p h d", d=64), AX.X,
                        ALU.add).then_inc(sums_ready, 1)
        take_linear(dve, l_q[0:2], "dve")
        dve_root(dve, r_mk, scale_ready)
        for g in range(2):
            if g:
                take_turn(dve, t_mk, "dve")
            dve.wait_ge(squared, 8 + g)
            v.tensor_reduce(r_mq[g]["sum"], rows[:, g, :].rearrange("p (h d) -> p h d", d=64), AX.X,
                            ALU.add).then_inc(sums_ready, 1)
            dve_root(dve, r_mq[g], scale_ready)
            dve.wait_ge(scale_ready, 7 + g)
            scale_heads(v, mq[:, :, 8 * g:8 * g + 8, :], scales(r_mq[g], 0, 8), dve_scaled)
            if g == 0:
                take_linear(dve, l_q[2:4], "dve")
        take_turn(dve, t_mq[0], "dve")
        take_turn(dve, t_mq[1], "dve")
        dve_attention(dve, att_m)
        split_first(dve, l_moba_o, "dve", 0, 1)
        take_turn(dve, t_mix3, "dve")
        split_first(dve, l_moba_o, "dve", 1)
        take_linear(dve, l_moba_o, "dve")
        wait_took(dve, l_moba_o)
        dve_moe_and_ple(dve, 1)

    ctx.close()


INPUTS = (
    "x", "positions", "norm_mix_g", "w_in", "qnorm_a_g", "knorm_a_g", "rel_bias", "cq_norm_g", "ckv_norm_g", "w_uq",
    "w_ukv", "qnorm_b_g", "knorm_b_g", "w_o", "norm_ffn_g", "w_ff1", "w_ff2", "p_2", "ln_mix_2", "ln_ffn_2",
    "ln_ple_2", "a_w_in_2", "a_q_norm_2", "a_k_norm_2", "a_ck_pos_2", "a_ck_w1_2", "a_ck_w2_2", "a_cv_pos_2",
    "a_cv_w1_2", "a_cv_w2_2", "a_w_out_2", "kv_norm_2", "w_kv_shared_2", "k_norm_shared_2", "b_w_q_2",
    "b_q_norm_2", "b_w_out_2", "moe_w_group_2", "moe_b_group_2", "moe_w_expert_2", "moe_b_expert_2",
    "moe_w_gate_2", "moe_w_up_2", "moe_w_down_2", "ple_w_proj_2", "ple_w_gate_2",
)


def kernel(**inputs):
    import concourse.bacc as bacc
    from concourse import mybir
    from concourse.bass_utils import run_bass_kernel_spmd

    nc = bacc.Bacc("TRN2", target_bir_lowering=False, num_devices=1)
    arrays, aps = {}, {}
    given = {name: np.ascontiguousarray(inputs[name]) for name in INPUTS}
    given["table"] = constant_table()
    for name, value in given.items():
        arrays[f"in_{name}"] = value
        aps[name] = nc.dram_tensor(f"in_{name}", value.shape, mybir.dt.from_np(value.dtype),
                                   kind="ExternalInput").ap()
    out = nc.dram_tensor("out_0", (1, TOKENS, D_MODEL), mybir.dt.float32, kind="ExternalOutput").ap()
    build_program(nc, aps, out)
    result = run_bass_kernel_spmd(nc, [arrays], core_ids=[0])
    return result.results[0]["out_0"]
```
